# Optimizing a Trainium2 kernel written in Bass

```python
import math
import jax, jax.numpy as jnp
from jax import lax
import numpy as np

D_MODEL = 2048
BATCH = 1
SEQ = 256
DEPTH = 1

CHUNK = 64
MIX_WIDTH = D_MODEL
ATTN_WIDTH = MIX_WIDTH // 2
HEAD_DIM = 128
N_ATTN_HEADS = ATTN_WIDTH // HEAD_DIM
SSM_WIDTH = MIX_WIDTH - ATTN_WIDTH
SSM_GROUP = 16
N_SSM_GROUPS = SSM_WIDTH // SSM_GROUP
SSM_STATE = 64
IN_WIDTH = 3 * ATTN_WIDTH + N_ATTN_HEADS + SSM_WIDTH
D_FF = 256 * ((8 * D_MODEL // 3 + 255) // 256)
CONV_WIDTH = 3
Q_BLOCK = 128
N_MOD = 6
EPS = 1e-6
DT_MIN = 1e-3
DT_MAX = 1e-1

kernel_name = "hybrid_fox_s5_convffn_adaln"

def rms_norm(x, g):
    xf = x.astype(jnp.float32)
    y = xf * lax.rsqrt(jnp.mean(xf * xf, axis=-1, keepdims=True) + EPS)
    return (y * g.astype(jnp.float32)).astype(x.dtype)

def modulate(h, shift, scale):
    return h * (1 + scale[:, None, :]) + shift[:, None, :]

def forgetting_attention(q, k, v, f_logit):
    B, S, H, Dh = q.shape
    log_f = jax.nn.log_sigmoid(f_logit.astype(jnp.float32))
    cum = jnp.transpose(jnp.cumsum(log_f, axis=1), (0, 2, 1))
    scale = Dh ** -0.5
    outs = []
    for blk in range(S // Q_BLOCK):
        q0 = blk * Q_BLOCK
        q1 = q0 + Q_BLOCK
        qb = q[:, q0:q1]
        kb = k[:, :q1]
        vb = v[:, :q1]
        s = jnp.einsum('bqhd,bkhd->bhqk', qb, kb, preferred_element_type=jnp.float32) * scale
        s = s + (cum[:, :, q0:q1, None] - cum[:, :, None, :q1])
        t_idx = q0 + jnp.arange(Q_BLOCK)
        s_idx = jnp.arange(q1)
        causal = s_idx[None, :] <= t_idx[:, None]
        s = jnp.where(causal, s, -jnp.inf)
        p = jax.nn.softmax(s, axis=-1)
        outs.append(jnp.einsum('bhqk,bkhd->bqhd', p.astype(vb.dtype), vb))
    return jnp.concatenate(outs, axis=1)

def s5_ssm(u, a_re, a_im, log_dt, b_re, b_im, c_re, c_im, d_skip):
    B, S, _ = u.shape
    uf = u.astype(jnp.float32).reshape(B, S, N_SSM_GROUPS, SSM_GROUP)
    a_re = a_re.astype(jnp.float32)
    a_im = a_im.astype(jnp.float32)
    dt = jnp.exp(log_dt.astype(jnp.float32))[:, None]
    mag = jnp.exp(dt * a_re)
    ab_re = mag * jnp.cos(dt * a_im)
    ab_im = mag * jnp.sin(dt * a_im)
    n_re = ab_re - 1
    n_im = ab_im
    den = a_re * a_re + a_im * a_im
    z_re = (n_re * a_re + n_im * a_im) / den
    z_im = (n_im * a_re - n_re * a_im) / den
    bu_re = jnp.einsum('bsgh,gph->bsgp', uf, b_re.astype(jnp.float32))
    bu_im = jnp.einsum('bsgh,gph->bsgp', uf, b_im.astype(jnp.float32))
    e_re = z_re * bu_re - z_im * bu_im
    e_im = z_re * bu_im + z_im * bu_re
    a_re_t = jnp.broadcast_to(ab_re, e_re.shape)
    a_im_t = jnp.broadcast_to(ab_im, e_im.shape)

    def combine(left, right):
        a1r, a1i, b1r, b1i = left
        a2r, a2i, b2r, b2i = right
        return (a2r * a1r - a2i * a1i,
                a2r * a1i + a2i * a1r,
                a2r * b1r - a2i * b1i + b2r,
                a2r * b1i + a2i * b1r + b2i)

    _, _, x_re, x_im = lax.associative_scan(combine, (a_re_t, a_im_t, e_re, e_im), axis=1)
    y = (jnp.einsum('bsgp,ghp->bsgh', x_re, c_re.astype(jnp.float32))
         - jnp.einsum('bsgp,ghp->bsgh', x_im, c_im.astype(jnp.float32))
         + d_skip.astype(jnp.float32) * uf)
    return y.reshape(B, S, SSM_WIDTH).astype(u.dtype)

def causal_dwconv(a, w, bias):
    S = a.shape[1]
    ap = jnp.pad(a, ((0, 0), (CONV_WIDTH - 1, 0), (0, 0)))
    out = bias
    for i in range(CONV_WIDTH):
        out = out + w[i] * ap[:, i:i + S]
    return out

def setup_inputs(seed: int = 0) -> dict:
    key = jax.random.key(seed)
    ks = jax.random.split(key, 32)
    L, D = DEPTH, D_MODEL
    G, P, Hc = N_SSM_GROUPS, SSM_STATE, SSM_GROUP
    nrm = lambda k, shape, s: jax.random.normal(k, shape, jnp.float32) * s
    gain = lambda k, shape: 1.0 + 0.02 * jax.random.normal(k, shape, jnp.float32)
    n_idx = jnp.arange(P, dtype=jnp.float32)
    return {
        "x": nrm(ks[0], (BATCH, SEQ, D), 1.0),
        "c": nrm(ks[1], (BATCH, D), 1.0),
        "w_ada": nrm(ks[2], (L, D, N_MOD * D), 0.5 * D ** -0.5),
        "b_ada": nrm(ks[3], (L, N_MOD * D), 0.02),
        "g_mix": gain(ks[4], (L, D)),
        "w_in": nrm(ks[5], (L, D, IN_WIDTH), D ** -0.5),
        "b_f": 2.0 + 0.5 * jax.random.normal(ks[6], (L, N_ATTN_HEADS), jnp.float32),
        "a_re": -0.5 + nrm(ks[7], (L, G, P), 0.01),
        "a_im": math.pi * n_idx + nrm(ks[8], (L, G, P), 0.01),
        "log_dt": jax.random.uniform(ks[9], (L, G), jnp.float32, math.log(DT_MIN), math.log(DT_MAX)),
        "ssm_b_re": nrm(ks[10], (L, G, P, Hc), (2 * Hc) ** -0.5),
        "ssm_b_im": nrm(ks[11], (L, G, P, Hc), (2 * Hc) ** -0.5),
        "ssm_c_re": nrm(ks[12], (L, G, Hc, P), (2 * P) ** -0.5 * 4.0),
        "ssm_c_im": nrm(ks[13], (L, G, Hc, P), (2 * P) ** -0.5 * 4.0),
        "ssm_d": nrm(ks[14], (L, G, Hc), 0.5),
        "w_glu": nrm(ks[15], (L, SSM_WIDTH, SSM_WIDTH), SSM_WIDTH ** -0.5),
        "b_glu": nrm(ks[16], (L, SSM_WIDTH), 0.02),
        "g_attn_out": gain(ks[17], (L, ATTN_WIDTH)),
        "g_ssm_out": gain(ks[18], (L, SSM_WIDTH)),
        "w_out": nrm(ks[19], (L, MIX_WIDTH, D), MIX_WIDTH ** -0.5),
        "g_ffn": gain(ks[20], (L, D)),
        "w_up": nrm(ks[21], (L, D, 2 * D_FF), D ** -0.5),
        "conv_w": nrm(ks[22], (L, CONV_WIDTH, D_FF), CONV_WIDTH ** -0.5),
        "conv_b": nrm(ks[23], (L, D_FF), 0.02),
        "w_down": nrm(ks[24], (L, D_FF, D), D_FF ** -0.5),
        "g_final": gain(ks[25], (D,)),
    }

def reference(x, c, w_ada, b_ada, g_mix, w_in, b_f, a_re, a_im, log_dt, ssm_b_re, ssm_b_im,
              ssm_c_re, ssm_c_im, ssm_d, w_glu, b_glu, g_attn_out, g_ssm_out, w_out, g_ffn,
              w_up, conv_w, conv_b, w_down, g_final):
    B, S, D = x.shape
    h = x
    cond = jax.nn.silu(c)
    splits = [ATTN_WIDTH, 2 * ATTN_WIDTH, 3 * ATTN_WIDTH, 3 * ATTN_WIDTH + N_ATTN_HEADS]
    for l in range(DEPTH):
        mod = cond @ w_ada[l] + b_ada[l]
        sh1, sc1, gt1, sh2, sc2, gt2 = jnp.split(mod, N_MOD, axis=-1)

        hn = modulate(rms_norm(h, g_mix[l]), sh1, sc1)
        proj = hn @ w_in[l]
        q, k, v, f_logit, u = jnp.split(proj, splits, axis=-1)
        q = q.reshape(B, S, N_ATTN_HEADS, HEAD_DIM)
        k = k.reshape(B, S, N_ATTN_HEADS, HEAD_DIM)
        v = v.reshape(B, S, N_ATTN_HEADS, HEAD_DIM)
        attn = forgetting_attention(q, k, v, f_logit + b_f[l]).reshape(B, S, ATTN_WIDTH)

        y = s5_ssm(u, a_re[l], a_im[l], log_dt[l], ssm_b_re[l], ssm_b_im[l],
                   ssm_c_re[l], ssm_c_im[l], ssm_d[l])
        y = jax.nn.gelu(y)
        y = y * jax.nn.sigmoid(y @ w_glu[l] + b_glu[l])

        mixed = jnp.concatenate([rms_norm(attn, g_attn_out[l]), rms_norm(y, g_ssm_out[l])], axis=-1)
        h = h + gt1[:, None, :] * (mixed @ w_out[l])

        hn = modulate(rms_norm(h, g_ffn[l]), sh2, sc2)
        up = hn @ w_up[l]
        a_br, b_br = jnp.split(up, 2, axis=-1)
        a_br = causal_dwconv(a_br, conv_w[l], conv_b[l])
        h = h + gt2[:, None, :] * ((jax.nn.silu(a_br) * b_br) @ w_down[l])
    return rms_norm(h, g_final)


_drawn_inputs = setup_inputs


def setup_inputs(seed=0):
    import zlib

    import numpy as np

    out = dict(_drawn_inputs(seed))
    spreads = {}
    factors = {'g_mix': 8.0,
     'a_re': 64.0,
     'b_glu': 8.0,
     'g_attn_out': 24.789,
     'g_ssm_out': 27.316,
     'g_ffn': 8.0,
     'conv_b': 24.211,
     'g_final': 2.711}
    for name, (base, spread) in spreads.items():
        noise = np.random.default_rng([zlib.crc32(name.encode()), seed]).standard_normal(out[name].shape)
        drawn = base * np.exp(spread * noise) if base else spread * noise
        out[name] = __import__('jax').numpy.asarray(drawn.astype(out[name].dtype))
    for name, factor in factors.items():
        out[name] = (out[name] * factor).astype(out[name].dtype)
    return out
```

```python
from contextlib import ExitStack

import concourse.bass as bass
import numpy as np
from concourse import mybir

F32 = mybir.dt.float32
F32R = mybir.dt.float32r
I32 = mybir.dt.int32
ALU = mybir.AluOpType
ACT = mybir.ActivationFunctionType
AX_X = mybir.AxisListType.X

P = 128
T = 256
TT = T // P
D = 2048
KD = D // P
NH = 8
HD = 128
AW = NH * HD
SW = 1024
KS = SW // P
NG, NS, GH = 64, 64, 16
NJ = NG * NS // P
JQ = 4
FF = 5632
KF = FF // P
EPS = 1e-6
SCALE = HD ** -0.5

UK = 4
UN = 256
USZ = UK * UN
RAW = 4
AN = 512
AK = USZ // AN
AU = KD // AK
SHIFT_SCALE1 = 2 * D // AN
ADA_BLOCKS = 6 * D // AN

MAGIC = 1.5 * 2.0 ** 23
TWO_PI = 2 * np.pi
C1 = 6.28125
C2 = float(np.floor((TWO_PI - C1) * 2.0 ** 21) / 2.0 ** 21)
C3 = float(TWO_PI - C1 - C2)
PI_IN = 3.1415925
MASKED = -1.0e30

V_GMIX, V_GFFN, V_GFINAL, V_GATTN, V_GSSM, V_BGLU, V_D, V_CONVB = 0, 16, 32, 48, 56, 64, 72, 80
V_BADA, V_ARE = 128, 224
V_CONV0, V_CONV1, V_AIM = 256, 300, 344
V_CONV2, V_COND, V_LOGDT = 384, 428, 448


def wait(eng, sem, value):
    if isinstance(value, int) and value <= 0:
        return
    eng.wait_ge(sem, value)


class Chain:

    def __init__(self, eng, sem):
        self.eng, self.sem, self.start, self.n = eng, sem, 0, 0

    def __call__(self, ins):
        ins.then_inc(self.sem, 1)
        self.n += 1
        self.eng.wait_ge(self.sem, self.start + self.n)

    def loop(self, i, per):
        self.base, self.per = self.start + self.n, per
        self.start, self.n = self.base + i * per, 0

    def after(self, passes):
        assert self.n == self.per, (self.n, self.per)
        self.start, self.n = self.base + passes * self.per, 0


class Gemm:

    def __init__(self, weights, pairs, units, column, before=None):
        self.w = weights.rearrange("(u f p) n -> u p f n", f=UK, p=P)
        self.pairs, self.units = pairs, units
        self.column = column
        self.n0, self.p0 = (before.n1, before.p1) if before else (0, 0)
        self.n1, self.p1 = self.n0 + pairs * units, self.p0 + pairs
        even = 2 * units % RAW == 0
        self.slots = [[(par * units * even + u) % RAW for u in range(units)] for par in range(2)]
        self.lag = RAW if even else RAW - 1
        both = self.slots[0] + self.slots[1]
        self.per = [both.count(s) for s in range(RAW)]
        self.turn = [[both[:par * units + u].count(self.slots[par][u]) for u in range(units)]
                     for par in range(2)]


def build(nc, x, c, w_ada, b_ada, g_mix, w_in, b_f, a_re, a_im, log_dt, ssm_b_re, ssm_b_im,
          ssm_c_re, ssm_c_im, ssm_d, w_glu, b_glu, g_attn_out, g_ssm_out, w_out, g_ffn, w_up,
          conv_w, conv_b, w_down, g_final, out):
    ctx = ExitStack()
    with ctx:
        def sem(name):
            return ctx.enter_context(nc.semaphore(name))

        def place(at, *tiles):
            got = []
            for name, shape, dt in tiles:
                got.append(nc.alloc_sbuf_tensor_at(name, shape, dt, offset=at))
                at += -(-int(np.prod(shape[1:])) * 4 // 32) * 32
            return at, got

        base = -(-nc.sbuf_base // 64) * 64
        small_at, (hT, vec, mod, ident, ones, sq, rb, halves, gains, tiny, ncol, wf, bf, raw, whi,
                   wlo) = place(
            base,
            ("hT", [P, KD, T], F32),
            ("vec", [P, 512], F32),
            ("mod", [P, 96], F32),
            ("ident", [P, P], F32),
            ("ones", [P, T], F32),
            ("sq", [P, 2, T], F32),
            ("rb", [P, T], F32),
            ("halves", [P, 2, 2, T], F32),
            ("gains", [P, 2, KD], F32),
            ("tiny", [P, 24], F32),
            ("ncol", [P, 2, 8], F32),
            ("wf", [P, KD, NH], F32),
            ("bf", [NH, 8], F32),
            ("raw", [P, RAW, USZ], F32),
            ("whi", [P, RAW, USZ], F32R),
            ("wlo", [P, RAW, USZ], F32R),
        )
        end1, (cond, ada_rows, iota_i, iota_f, disc) = place(
            small_at,
            ("cond", [P, KD, 32], F32),
            ("ada_rows", [P, 2, AN], F32),
            ("iota_i", [P, 16], I32), ("iota_f", [P, 16], F32),
            ("disc", [P, 14, NJ], F32),
        )
        end2, (conv_in, gate, branch, gated) = place(
            small_at,
            ("conv_in", [P, 2, T + 2], F32), ("gate", [P, 2, T], F32),
            ("branch", [P, 2, T], F32), ("gated", [P, 2, T], F32),
        )
        acts_at = max(end1, end2)
        ffn_at, (AA,) = place(acts_at, ("AA", [P, KD, 2 * T], F32R))
        _, (prob, probT, mask, csel, cum) = place(
            acts_at,
            ("prob", [P, 2, 3 * P], F32), ("probT", [P, 2, 3 * P], F32), ("mask", [P, 3 * P], F32),
            ("csel", [NH, 2, 2, T], F32), ("cum", [NH, 4, T], F32),
        )
        _, (tab_t,) = place(acts_at + KS * 2 * T * 4 + 12288, ("tab_t", [P, JQ, 16, 16], F32))
        _, (out_n, g_rows) = place(acts_at, ("out_n", [P, TT, D], F32), ("g_rows", [P, D], F32))
        end, (GG,) = place(ffn_at, ("GG", [P, KF, 2 * T], F32R))
        assert end <= nc.sbuf_usable_end
        mix_end, (uT, qT, kT, vN, btr, bti, ctr, cti, fac, tab, ssm_w) = place(
            ffn_at,
            ("uT", [P, KS, T], F32),
            ("qT", [P, NH, T], F32),
            ("kT", [P, NH, T], F32),
            ("vN", [P, TT, AW], F32),
            ("btr", [P, KS, P], F32), ("bti", [P, KS, P], F32),
            ("ctr", [P, KS, P], F32), ("cti", [P, KS, P], F32),
            ("fac", [P, 4, NJ, 16], F32),
            ("tab", [P, 2, 2, JQ, T], F32),
            ("ssm_w", [P, 4, JQ, T], F32),
        )
        assert mix_end <= end
        at_q = ffn_at + KS * T * 4
        _, (stage,) = place(ffn_at, ("stage", [P, 4, P], F32))
        _, (b_raw, b_bar, b_wide) = place(
            at_q,
            ("b_raw", [P, 2, NJ, GH], F32), ("b_bar", [P, 2, NJ, GH], F32),
            ("b_wide", [P, 2, NJ, 2, GH], F32),
        )
        _, (c_twice,) = place(at_q + 2 * KS * T * 4, ("c_twice", [P, 2, KS, 2, NS], F32))
        tab_at = mix_end - 2 * 16384
        _, (ph,) = place(tab_at, ("ph", [P, 5, NJ, 16], F32))
        _, (vT,) = place(tab_at, ("vT", [P, NH, T], F32))
        _, (xn,) = place(mix_end - 16384, ("xn", [P, TT, D], F32))

        psG = ctx.enter_context(nc.psum_tensor("psG", [P, 4, 512], F32))
        psX = ctx.enter_context(nc.psum_tensor("psX", [P, 4, 512], F32))

        wi = w_in
        g_u = Gemm(wi[:, 3 * AW + NH:3 * AW + NH + SW], 4, KD // UK, lambda par, i: (2 * i + par) * UN)
        g_q = Gemm(wi[:, 0:AW], 4, KD // UK, lambda par, i: (2 * i + par) * UN, g_u)
        g_k = Gemm(wi[:, AW:2 * AW], 4, KD // UK, lambda par, i: (2 * i + par) * UN, g_q)
        g_v = Gemm(wi[:, 2 * AW:3 * AW], 4, KD // UK, lambda par, i: (2 * i + par) * UN, g_k)
        g_glu = Gemm(w_glu, 4, KS // UK, lambda par, i: (2 * i + par) * UN, g_v)
        g_out = Gemm(w_out, 8, KD // UK, lambda par, i: (2 * i + par) * UN, g_glu)
        g_up = Gemm(w_up, KF, KD // UK, lambda par, i: par * FF + i * UN, g_out)
        g_down = Gemm(w_down, 8, KF // UK, lambda par, i: (2 * i + par) * UN, g_up)

        raw_landed = [sem(f"raw_landed{s}") for s in range(RAW)]
        x_landed, stage_landed, bc_landed, wf_landed = map(
            sem, ("x_landed", "stage_landed", "bc_landed", "wf_landed"))
        g_rows_landed, out_stored = sem("g_rows_landed"), sem("out_stored")
        consts_ready, pool_chain = sem("consts_ready"), sem("pool_chain")
        stage_ready, vecT_done, vec_ready = sem("stage_ready"), sem("vecT_done"), sem("vec_ready")
        xT_done, hT_ready = sem("xT_done"), sem("hT_ready")
        cond_act, cond_ready = sem("cond_act"), sem("cond_ready")
        act_setup, dve_setup = sem("act_setup"), sem("dve_setup")
        bc_ready, bcT_done, bcT_ready = sem("bc_ready"), sem("bcT_done"), sem("bcT_ready")
        ada_used, ada_out, ada_cols, mod_ready = map(
            sem, ("ada_used", "ada_out", "ada_cols", "mod_ready"))
        sq_done, ss_used, root_done, rms_ready = map(
            sem, ("sq_done", "ss_used", "root_done", "rms_ready"))
        nt_ready, affine_done, nhi_done, act_ready = map(
            sem, ("nt_ready", "affine_done", "nhi_done", "act_ready"))
        hi_done, lo_done, mm_used, lo_half_out, pair_out = map(
            sem, ("hi_done", "lo_done", "mm_used", "lo_half_out", "pair_out"))
        f_done, f_half, f_abs, f_ln = sem("f_done"), sem("f_half"), sem("f_abs"), sem("f_ln")
        vN_done, vN_ready = sem("vN_done"), sem("vN_ready")
        csel_ready, score_done, masked, exp_done = map(
            sem, ("csel_ready", "score_done", "masked", "exp_done"))
        max_ready, prob_ready, probT_done, probT_ready, pv_done, o_ready = map(
            sem, ("max_ready", "prob_ready", "probT_done", "probT_ready", "pv_done", "o_ready"))
        tab_ready, e_done, rotated, z_part, y_part, y_ready, gelu_done, gelu_hi = map(
            sem, ("tab_ready", "e_done", "rotated", "z_part", "y_part", "y_ready", "gelu_done",
                  "gelu_hi"))
        glu_act_ready = sem("glu_act_ready")
        z_ready, sig_done, conv_done, silu_done, gated_ready, ghi_done, g_ready = map(
            sem, ("z_ready", "sig_done", "conv_done", "silu_done", "gated_ready", "ghi_done",
                  "g_ready"))
        tail_T, tail_out, sumsq_done = sem("tail_T"), sem("tail_out"), sem("sumsq_done")
        root2_done, final_ready = sem("root2_done"), sem("final_ready")
        dve_chain, act_chain = sem("dve_chain"), sem("act_chain")

        NORM1, NORMA, NORMS, NORM2 = (0, 0), (1, KD), (2, KD + KS), (3, KD + 2 * KS)
        STAGE_DMAS, BC_DMAS = 15, 6

        block = ctx.enter_context(nc.Block())

        @block.sync
        def _(sp):
            uses = [0] * RAW

            def ada_stream(b0, b1, released):
                w = w_ada.rearrange("(u f p) n -> u p f n", f=AK, p=P)

                def unit(b, u):
                    s = u % RAW
                    sp.dma_start(raw[:, s, :].rearrange("p (f n) -> p f n", f=AK),
                                 w[u, :, :, bass.ds(b * AN, AN)]).then_inc(raw_landed[s], 16)

                for u in range(AU):
                    if u < RAW:
                        released(u)
                    else:
                        sp.wait_ge(ada_used, b0 * AU + u - RAW + 1)
                    unit(b0, u)
                with nc.sync.Fori(b0 + 1, b1) as b:
                    for u in range(AU):
                        sp.wait_ge(ada_used, b * AU + u - RAW + 1)
                        unit(b, u)

            def gemm_stream(g, released=None):
                def unit(par, i, u):
                    s = g.slots[par][u]
                    sp.dma_start(raw[:, s, :].rearrange("p (f n) -> p f n", f=UK),
                                 g.w[u, :, :, bass.ds(g.column(par, i), UN)]
                                 ).then_inc(raw_landed[s], 16)

                def pair(par, i, first):
                    for u in range(g.units):
                        if first and released and par * g.units + u < RAW:
                            released(par * g.units + u)
                        else:
                            wait(sp, lo_done, g.n0 + (2 * i + par) * g.units + u - g.lag + 1)
                        unit(par, i, u)

                pair(0, 0, True)
                pair(1, 0, True)
                with nc.sync.Fori(1, g.pairs // 2) as i:
                    pair(0, i, False)
                    pair(1, i, False)

            ada_stream(0, SHIFT_SCALE1, lambda s: None)
            gemm_stream(g_u, lambda s: sp.wait_ge(ada_used, SHIFT_SCALE1 * AU - RAW + 1 + s))
            gemm_stream(g_q)
            gemm_stream(g_k)
            gemm_stream(g_v)
            ada_stream(SHIFT_SCALE1, ADA_BLOCKS, lambda s: sp.wait_ge(lo_done, g_v.n1 - RAW + 1 + s))
            gemm_stream(g_glu, lambda s: sp.wait_ge(ada_used, ADA_BLOCKS * AU - RAW + 1 + s))
            gemm_stream(g_out)
            gemm_stream(g_up)
            gemm_stream(g_down)
            sp.wait_ge(out_stored, 16 * TT)

        @block.gpsimd
        def _(pool):
            link = Chain(pool, pool_chain)
            link(nc.gpsimd.memset(ident[:], 0.0))
            link(nc.gpsimd.affine_select(out=ident[:], in_=ident[:], compare_op=ALU.not_equal, fill=1.0,
                                         base=0, pattern=[[-1, P]], channel_multiplier=1))
            nc.gpsimd.memset(ones[:], 1.0).then_inc(consts_ready, 1)
            nc.gpsimd.iota(iota_i[:], pattern=[[1, 16]], base=0, channel_multiplier=0
                           ).then_inc(consts_ready, 1)
            for q in range(KS):
                js = slice(JQ * q, JQ * q + JQ)
                cs, ss = (fac[:, a, js, :].unsqueeze(2).to_broadcast([P, JQ, 16, 16]) for a in (0, 1))
                ck, sk = (fac[:, a, js, :].unsqueeze(3).to_broadcast([P, JQ, 16, 16]) for a in (2, 3))
                ct, st = (tab[:, q % 2, a, :, :].rearrange("p j (k s) -> p j k s", s=16)
                          for a in (0, 1))
                if q == 0:
                    pool.wait_ge(act_setup, 6)
                    pool.wait_ge(vN_done, 1)
                    pool.wait_ge(f_done, 1)
                if q >= 2:
                    pool.wait_ge(z_part, 2 * (q - 1))
                link(nc.gpsimd.tensor_tensor(ct, cs, ck, ALU.mult))
                link(nc.gpsimd.tensor_tensor(tab_t[:], ss, sk, ALU.mult))
                link(nc.gpsimd.tensor_tensor(ct, ct, tab_t[:], ALU.subtract))
                link(nc.gpsimd.tensor_tensor(st, cs, sk, ALU.mult))
                link(nc.gpsimd.tensor_tensor(tab_t[:], ss, ck, ALU.mult))
                nc.gpsimd.tensor_tensor(st, st, tab_t[:], ALU.add).then_inc(tab_ready, 1)
                pool.wait_ge(tab_ready, q + 1)

        @block.scalar
        def _(act):
            link = Chain(act, act_chain)
            uses = [0] * RAW

            def row(v):
                return v.rearrange("l (r p) -> (l r) p", p=P)

            act.wait_ge(stage_ready, 1)
            for s, at, src in (
                (3, V_COND, row(c)), (0, V_GMIX, row(g_mix)), (0, V_GFFN, row(g_ffn)),
                (0, V_GFINAL, g_final.rearrange("(r p) -> r p", p=P)), (0, V_GATTN, row(g_attn_out)),
                (0, V_GSSM, row(g_ssm_out)), (0, V_BGLU, row(b_glu)),
                (0, V_D, ssm_d.rearrange("l (r g) h -> (l r) (g h)", g=8)), (0, V_CONVB, row(conv_b)),
                (1, V_BADA, row(b_ada)), (1, V_ARE, a_re.rearrange("l (r g) p -> (l r) (g p)", g=2)),
                (2, V_AIM, a_im.rearrange("l (r g) p -> (l r) (g p)", g=2)),
                (2, V_CONV0, conv_w.rearrange("l w (r p) -> (l w r) p", p=P)[0:2 * KF]),
                (3, V_CONV2, conv_w.rearrange("l w (r p) -> (l w r) p", p=P)[2 * KF:3 * KF]),
            ):
                r = at - P * s
                act.dma_start(stage[r:r + src.shape[0], s, :], src).then_inc(stage_landed, 16)
            with nc.allow_non_contiguous_dma(reason="64 numbers"):
                act.dma_start(tiny[V_LOGDT % P:V_LOGDT % P + NJ, KD:KD + 2],
                              log_dt.rearrange("l (r g) -> (l r) g", g=2)).then_inc(stage_landed, 16)
                act.dma_start(bf[:, 0:1], b_f.rearrange("l h -> h l")).then_inc(wf_landed, 16)
            xv = x.rearrange("b (t p) d -> p (b t) d", p=P)
            for tt in range(TT):
                act.dma_start(xn[:, tt, :], xv[:, tt, :]).then_inc(x_landed, 16)
            for a, (bm, cm) in enumerate(((ssm_b_re, ssm_c_re), (ssm_b_im, ssm_c_im))):
                act.dma_start(b_raw[:, a, :, :], bm.rearrange("l (j g) p h -> (g p) (l j) h", g=2)
                              ).then_inc(bc_landed, 16)
                for twice in range(2):
                    act.dma_start(c_twice[:, a, :, twice, :],
                                  cm.rearrange("l (q g) h p -> (g h) (l q) p", g=8)
                                  ).then_inc(bc_landed, 16)
            act.dma_start(wf[:], w_in[:, 3 * AW:3 * AW + NH].rearrange("(k p) h -> p k h", p=P)
                          ).then_inc(wf_landed, 16)

            act.wait_ge(vec_ready, 1)
            nc.scalar.activation(tiny[:, 0:KD], vec[:, V_COND:V_COND + KD], ACT.Silu
                                 ).then_inc(cond_act, 1)
            for r in (1, 3):
                act.wait_ge(xT_done, r + 1)
                nc.scalar.activation(hT[:, 4 * r:4 * r + 4, :].rearrange("p (b j) t -> p b (j t)", j=2),
                                     psG[:, 2:4, :], ACT.Copy).then_inc(hT_ready, 1)
            nc.scalar.activation(disc[:, 0, :], vec[:, V_LOGDT:V_LOGDT + NJ], ACT.Exp
                                 ).then_inc(act_setup, 1)
            act.wait_ge(dve_setup, 1)
            nc.scalar.activation(disc[:, 3, :], disc[:, 1, :], ACT.Exp).then_inc(act_setup, 1)
            for half in range(2):
                act.wait_ge(dve_setup, 2 + half)
                nc.scalar.activation(fac[:, 2 * half + 1, :, :], ph[:, 1, :, :], ACT.Sin
                                     ).then_inc(act_setup, 1)
                nc.scalar.activation(fac[:, 2 * half, :, :], ph[:, 3, :, :], ACT.Sin
                                     ).then_inc(act_setup, 1)

            def ada_evacuate(b, par):
                act.wait_ge(ada_used, (b + 1) * AU)
                wait(act, ada_cols, b - 1)
                nc.scalar.activation(ada_rows[:, par, :], psX[:, par, :], ACT.Copy
                                     ).then_inc(ada_out, 1)

            def ada_phase(b0, b1):
                ada_evacuate(b0, 0)
                ada_evacuate(b0 + 1, 1)
                with nc.scalar.Fori(b0 // 2 + 1, b1 // 2) as i:
                    ada_evacuate(2 * i, 0)
                    ada_evacuate(2 * i + 1, 1)
                for s in range(RAW):
                    uses[s] += (b1 - b0) * AU // RAW

            def norm(which, width, src, n, k0, scale, shift, free):
                index, g0 = which
                for j in range(n):
                    wait(act, ss_used, g0 + j - 1)
                    nc.scalar.activation(sq[:, j % 2, :], src(j), ACT.Square).then_inc(sq_done, 1)
                act.wait_ge(ss_used, g0 + n)
                wait(act, nt_ready, g0)
                nc.scalar.activation(rb[:], psX[:, 3, 0:T], ACT.Sqrt, scale=1.0 / width,
                                     bias=ncol[:, 0, 7:8]).then_inc(root_done, 1)
                nt = halves[:, :, :, :].rearrange("p a b t -> p (a b) t")
                free()
                for j in range(n):
                    act.wait_ge(nt_ready, g0 + j + 1)
                    if shift is None:
                        nc.scalar.activation(nt[:, j % 4, :], nt[:, j % 4, :], ACT.Copy,
                                             scale=scale(j)).then_inc(affine_done, 1)
                    else:
                        nc.scalar.activation(nt[:, j % 4, :], nt[:, j % 4, :], ACT.Identity,
                                             scale=scale(j), bias=shift(j)).then_inc(affine_done, 1)
                    act.wait_ge(affine_done, g0 + j + 1)
                    nc.scalar.activation(AA[:, k0 + j, 0:T], nt[:, j % 4, :], ACT.Copy
                                         ).then_inc(nhi_done, 1)

            def gemm(g, evacuate, per=0):
                first = list(uses)

                def split(par, i):
                    n = g.n0 + (2 * i + par) * g.units
                    for u in range(g.units):
                        s = g.slots[par][u]
                        at = first[s] + i * g.per[s] + g.turn[par][u]
                        act.wait_ge(raw_landed[s], 16 * at + 16)
                        wait(act, mm_used, n + u - g.lag + 1)
                        nc.scalar.activation(whi[:, s, :], raw[:, s, :], ACT.Copy).then_inc(hi_done, 1)

                split(0, 0)
                with nc.scalar.Fori(0, g.pairs // 2 - 1) as i:
                    split(1, i)
                    evacuate(0, i)
                    split(0, i + 1)
                    evacuate(1, i)
                last = g.pairs // 2 - 1
                split(1, last)
                evacuate(0, last)
                evacuate(1, last)
                for s in range(RAW):
                    uses[s] += g.pairs // 2 * g.per[s]

            def pair_done(g, par, i):
                act.wait_ge(mm_used, g.n0 + (2 * i + par + 1) * g.units)

            def take_lo(g, scale=1.0):
                def evacuate(par, i):
                    pair_done(g, par, i)
                    nc.scalar.activation(halves[:, par, :, :], psG[:, 2 * par:2 * par + 2, T:2 * T],
                                         ACT.Copy, scale=scale).then_inc(lo_half_out, 1)
                return evacuate

            ada_phase(0, SHIFT_SCALE1)
            act.wait_ge(mod_ready, 1)
            act.wait_ge(hT_ready, 4)
            norm(NORM1, D, lambda j: hT[:, j, :], KD, 0, lambda j: gains[:, 0, j:j + 1],
                 lambda j: mod[:, j:j + 1], lambda: None)
            gemm(g_u, take_lo(g_u))
            gemm(g_q, take_lo(g_q, SCALE))
            gemm(g_k, take_lo(g_k))
            gemm(g_v, take_lo(g_v))

            act.wait_ge(f_done, 1)
            nc.scalar.activation(cum[:, 1, :], psX[0:NH, 3, T:2 * T], ACT.Copy).then_inc(f_half, 1)
            act.wait_ge(f_abs, 1)
            link(nc.scalar.activation(cum[:, 1, :], cum[:, 1, :], ACT.Exp, scale=-1.0))
            nc.scalar.activation(cum[:, 1, :], cum[:, 1, :], ACT.Ln, bias=ones[0:NH, 0:1]
                                 ).then_inc(f_ln, 1)
            act.wait_ge(vN_done, 1)
            nc.scalar.activation(vN[:, 1, :].rearrange("p (b n) -> p b n", b=2), psG[:, 2:4, :],
                                 ACT.Copy).then_inc(vN_ready, 1)

            def exps(h):
                act.wait_ge(max_ready, h + 1)
                b = h % 2
                for tt, cols in ((0, slice(0, P)), (1, slice(P, 3 * P))):
                    nc.scalar.activation(prob[:, b, cols], prob[:, b, cols], ACT.Exp,
                                         bias=ncol[:, b, 2 + tt:3 + tt],
                                         accum_out=ncol[:, b, 4 + tt:5 + tt]).then_inc(exp_done, 1)

            def take_probT(h):
                act.wait_ge(probT_done, h + 1)
                wait(act, pv_done, h - 1)
                nc.scalar.activation(probT[:, h % 2, :], psX[:, 2, 0:3 * P], ACT.Copy
                                     ).then_inc(probT_ready, 1)

            exps(0)
            for h in range(NH):
                if h + 1 < NH:
                    exps(h + 1)
                take_probT(h)

            for q in range(KS):
                act.wait_ge(y_ready, q + 1)
                nc.scalar.activation(uT[:, q, :], uT[:, q, :], ACT.Gelu_apprx_tanh
                                     ).then_inc(gelu_done, 1)
                act.wait_ge(gelu_done, q + 1)
                if KS + q >= KD - 2:
                    act.wait_ge(tab_ready, KS)
                nc.scalar.activation(AA[:, KS + q, 0:T], uT[:, q, :], ACT.Copy).then_inc(gelu_hi, 1)

            ada_phase(SHIFT_SCALE1, ADA_BLOCKS)

            act.wait_ge(o_ready, NH)
            norm(NORMA, AW, lambda j: qT[:, j, :], KS, 0, lambda j: vec[:, V_GATTN + j:V_GATTN + j + 1],
                 None, lambda: None)

            def evacuate_glu(par, i):
                take_lo(g_glu)(par, i)
                act.wait_ge(z_ready, 2 * i + par + 1)
                for m in range(2):
                    nc.scalar.activation(
                        halves[:, par, m, :], halves[:, par, m, :], ACT.Sigmoid,
                        bias=vec[:, bass.ds(V_BGLU + 4 * i + 2 * par + m, 1)]).then_inc(sig_done, 1)

            gemm(g_glu, evacuate_glu)
            act.wait_ge(pair_out, g_glu.p1)
            norm(NORMS, SW, lambda j: uT[:, j, :], KS, KS, lambda j: vec[:, V_GSSM + j:V_GSSM + j + 1],
                 None, lambda: None)

            def take_gated(g, gate_col):
                def evacuate(par, i):
                    pair_done(g, par, i)
                    for m in range(2):
                        nc.scalar.activation(
                            halves[:, par, m, :], psG[:, 2 * par + m, T:2 * T], ACT.Copy,
                            scale=mod[:, bass.ds(gate_col + 4 * i + 2 * par + m, 1)]
                        ).then_inc(lo_half_out, 1)
                return evacuate

            gemm(g_out, take_gated(g_out, 2 * KD))
            act.wait_ge(pair_out, g_out.p1)
            norm(NORM2, D, lambda j: hT[:, j, :], KD, 0, lambda j: gains[:, 1, j:j + 1],
                 lambda j: mod[:, 3 * KD + j:3 * KD + j + 1], lambda: None)

            def evacuate_up(par, i):
                take_lo(g_up)(par, i)
                if par == 0:
                    act.wait_ge(conv_done, i + 1)
                    nc.scalar.activation(gate[:], gate[:], ACT.Silu).then_inc(silu_done, 1)
                else:
                    act.wait_ge(gated_ready, i + 1)
                    nc.scalar.activation(GG[:, bass.ds(2 * i, 2), 0:T], gated[:], ACT.Copy
                                         ).then_inc(ghi_done, 1)

            gemm(g_up, evacuate_up)
            act.wait_ge(mm_used, g_up.n1)
            act.dma_start(g_rows[:], g_final.rearrange("(l d) -> l d", l=1).to_broadcast([P, D])
                          ).then_inc(g_rows_landed, 16)

            def tail_copy(pair, par):
                act.wait_ge(tail_T, pair + 1)
                nc.scalar.activation(out_n[:, :, bass.ds(pair * UN, UN)],
                                     psX[:, par, :].rearrange("p (t n) -> p t n", t=TT), ACT.Copy
                                     ).then_inc(tail_out, 1)

            def evacuate_down(par, i):
                take_gated(g_down, 5 * KD)(par, i)
                tail_copy(2 * i + par, par)

            gemm(g_down, evacuate_down)
            act.wait_ge(tail_out, g_down.pairs)
            for tt in range(TT):
                nc.scalar.activation(raw[:, 2 * tt:2 * tt + 2, :].rearrange("p s n -> p (s n)"),
                                     out_n[:, tt, :], ACT.Square, accum_out=tiny[:, tt:tt + 1]
                                     ).then_inc(act_chain, 1)
                link.n += 1
            act.wait_ge(act_chain, link.start + link.n)
            nc.scalar.activation(tiny[:, 2:4], tiny[:, 0:2], ACT.Sqrt, scale=1.0 / D,
                                 bias=ncol[:, 0, 7:8]).then_inc(root2_done, 1)
            ov = out.rearrange("b (t p) d -> p (b t) d", p=P)
            for tt in range(TT):
                act.wait_ge(final_ready, tt + 1)
                act.dma_start(ov[:, tt, :], out_n[:, tt, :]).then_inc(out_stored, 16)

        @block.vector
        def _(dve):
            link = Chain(dve, dve_chain)
            V = nc.vector
            V.memset(stage[:], 0.0).then_inc(stage_ready, 1)
            V.memset(ncol[:, 0, 7:8], EPS).then_inc(cond_ready, 1)
            V.memset(cond[:], 0.0).then_inc(cond_ready, 1)

            dve.wait_ge(stage_landed, 16 * STAGE_DMAS)
            r = V_LOGDT % P
            for g in range(2):
                V.tensor_copy(stage[r:r + NJ, 3, NS * g:NS * g + NS],
                              tiny[r:r + NJ, KD + g:KD + g + 1].to_broadcast([NJ, NS])).then_inc(stage_ready, 1)
            dve.wait_ge(vecT_done, 1)
            V.tensor_copy(vec[:], psX[:, 0, :]).then_inc(vec_ready, 1)
            dve.wait_ge(cond_act, 1)
            V.tensor_copy(cond[:, :, 0:1], tiny[:, 0:KD].unsqueeze(2)).then_inc(cond_ready, 1)
            for r in (0, 2):
                dve.wait_ge(xT_done, r + 1)
                V.tensor_copy(hT[:, 4 * r:4 * r + 4, :].rearrange("p (b j) t -> p b (j t)", j=2),
                              psG[:, 0:2, :]).then_inc(hT_ready, 1)

            d = lambda n: disc[:, n, :]
            are, aim = vec[:, V_ARE:V_ARE + NJ], vec[:, V_AIM:V_AIM + NJ]
            dve.wait_ge(act_setup, 1)
            link(V.tensor_tensor(d(1), d(0), are, ALU.mult))
            V.tensor_tensor(d(2), d(0), aim, ALU.mult).then_inc(dve_setup, 1)
            dve.wait_ge(dve_setup, 1)
            dve.wait_ge(consts_ready, 2)
            link(V.tensor_copy(iota_f[:], iota_i[:]))

            def turns(r, big, k):
                link(V.tensor_scalar(k, big, float(1 / TWO_PI), MAGIC, ALU.mult, ALU.add))
                link(V.tensor_scalar(k, k, -MAGIC, None, ALU.add))
                link(V.scalar_tensor_tensor(r, k, -C1, big, ALU.mult, ALU.add))
                link(V.scalar_tensor_tensor(r, k, -C2, r, ALU.mult, ALU.add))
                link(V.scalar_tensor_tensor(r, k, -C3, r, ALU.mult, ALU.add))

            s16 = iota_f[:].unsqueeze(1).to_broadcast([P, NJ, 16])
            p_ = lambda n: ph[:, n, :, :]
            for half in range(2):
                if half:
                    link(V.tensor_scalar(d(2), d(4), 16.0, None, ALU.mult))
                turns(d(4), d(2), d(5))
                link(V.tensor_copy(d(6).bitcast(F32R), d(4)))
                link(V.tensor_tensor(d(7), d(4), d(6), ALU.subtract))
                th, tl = (d(n).unsqueeze(2).to_broadcast([P, NJ, 16]) for n in (6, 7))
                if half:
                    dve.wait_ge(act_setup, 4)
                link(V.tensor_tensor(p_(0), s16, th, ALU.mult))
                turns(p_(1), p_(0), p_(2))
                link(V.tensor_tensor(p_(2), s16, tl, ALU.mult))
                link(V.tensor_tensor(p_(1), p_(1), p_(2), ALU.add))
                link(V.tensor_scalar(p_(3), p_(1), float(np.pi / 2), float(-TWO_PI), ALU.is_gt, ALU.mult))
                link(V.scalar_tensor_tensor(p_(3), p_(1), float(np.pi / 2), p_(3), ALU.add, ALU.add))
                link(V.tensor_scalar(p_(1), p_(1), PI_IN, -PI_IN, ALU.min, ALU.max))
                V.tensor_scalar(p_(3), p_(3), PI_IN, -PI_IN, ALU.min, ALU.max).then_inc(dve_setup, 1)
                dve.wait_ge(dve_setup, 2 + half)
            dve.wait_ge(act_setup, 6)
            c1, s1 = fac[:, 0, :, 1:2].rearrange("p j o -> p (j o)"), fac[:, 1, :, 1:2].rearrange("p j o -> p (j o)")
            link(V.tensor_tensor(d(4), d(3), c1, ALU.mult))
            link(V.tensor_scalar(d(4), d(4), -1.0, None, ALU.add))
            link(V.tensor_tensor(d(5), d(3), s1, ALU.mult))
            link(V.tensor_tensor(d(6), are, are, ALU.mult))
            link(V.tensor_tensor(d(7), aim, aim, ALU.mult))
            link(V.tensor_tensor(d(6), d(6), d(7), ALU.add))
            link(V.reciprocal(d(6), d(6)))
            link(V.tensor_tensor(d(7), d(4), are, ALU.mult))
            link(V.tensor_tensor(d(8), d(5), aim, ALU.mult))
            link(V.tensor_tensor(d(7), d(7), d(8), ALU.add))
            link(V.tensor_tensor(d(9), d(7), d(6), ALU.mult))
            link(V.tensor_tensor(d(7), d(5), are, ALU.mult))
            link(V.tensor_tensor(d(8), d(4), aim, ALU.mult))
            link(V.tensor_tensor(d(7), d(7), d(8), ALU.subtract))
            link(V.tensor_tensor(d(10), d(7), d(6), ALU.mult))
            dve.wait_ge(bc_landed, 16 * BC_DMAS)
            zr, zi = (d(n).unsqueeze(2).to_broadcast([P, NJ, GH]) for n in (9, 10))
            br, bi = b_raw[:, 0, :, :], b_raw[:, 1, :, :]
            link(V.tensor_tensor(p_(4), zi, bi, ALU.mult))
            link(V.tensor_tensor(b_bar[:, 0, :, :], zr, br, ALU.mult))
            link(V.tensor_tensor(b_bar[:, 0, :, :], b_bar[:, 0, :, :], p_(4), ALU.subtract))
            link(V.tensor_tensor(p_(4), zi, br, ALU.mult))
            link(V.tensor_tensor(b_bar[:, 1, :, :], zr, bi, ALU.mult))
            link(V.tensor_tensor(b_bar[:, 1, :, :], b_bar[:, 1, :, :], p_(4), ALU.add))
            V.memset(ctr[:], 0.0).then_inc(bc_ready, 1)
            V.memset(cti[:], 0.0).then_inc(bc_ready, 1)
            link(V.memset(b_wide[:], 0.0))
            for g in range(2):
                half = slice(NS * g, NS * g + NS)
                V.tensor_copy(b_wide[half, :, :, g, :].rearrange("p a j h -> p (a j) h"),
                              b_bar[half, :, :, :].rearrange("p a j h -> p (a j) h")
                              ).then_inc(bc_ready, 1)
            for r, dst in ((0, btr), (1, bti)):
                dve.wait_ge(bcT_done, r + 1)
                V.tensor_copy(dst[:].rearrange("p (b q) n -> p b (q n)", b=2), psG[:, 2 * r:2 * r + 2, :]
                              ).then_inc(bcT_ready, 1)
            for r, (dst, sign) in ((2, (ctr, 1.0)), (3, (cti, -1.0))):
                dve.wait_ge(bcT_done, r + 1)
                dve.wait_ge(bc_ready, 4)
                for g in range(2):
                    half = slice(NS * g, NS * g + NS)
                    V.tensor_scalar(
                        dst[half, :, :].rearrange("p q (r g h) -> p (q r) g h", g=2, h=GH)[:, :, g, :],
                        psG[half, 2 * (r - 2):2 * (r - 2) + 2, :].rearrange(
                            "p b (q g h) -> p (b q) g h", g=2, h=GH)[:, :, g, :],
                        sign, None, ALU.mult).then_inc(bcT_ready, 1)

            def modulation(count, lo, hi, done):
                dve.wait_ge(ada_cols, count)
                link(V.tensor_tensor(mod[:, lo:hi], psX[:, 2, lo:hi], vec[:, V_BADA + lo:V_BADA + hi],
                                     ALU.add))
                a, g_col, s_col = done
                V.scalar_tensor_tensor(gains[:, a, :], mod[:, s_col:s_col + KD], 1.0,
                                       vec[:, g_col:g_col + KD], ALU.add, ALU.mult
                                       ).then_inc(mod_ready, 1)

            def norm(which, src, n, k0, free):
                index, g0 = which
                dve.wait_ge(root_done, index + 1)
                V.reciprocal(rb[:], rb[:]).then_inc(rms_ready, 1)
                dve.wait_ge(rms_ready, index + 1)
                nt = halves[:, :, :, :].rearrange("p a b t -> p (a b) t")

                def low(j):
                    dve.wait_ge(nhi_done, g0 + j + 1)
                    V.tensor_tensor(AA[:, k0 + j, T:2 * T], nt[:, j % 4, :],
                                    AA[:, k0 + j, 0:T].bitcast(F32), ALU.subtract
                                    ).then_inc(act_ready, 1)

                free()
                for j in range(n):
                    if j >= 4:
                        dve.wait_ge(act_ready, g0 + j - 3)
                    V.tensor_tensor(nt[:, j % 4, :], src(j), rb[:], ALU.mult).then_inc(nt_ready, 1)
                    if j >= 2:
                        low(j - 2)
                low(n - 2)
                low(n - 1)

            def gemm(g, evacuate, links=0):
                def split(par, i):
                    n = g.n0 + (2 * i + par) * g.units
                    for u in range(g.units):
                        s = g.slots[par][u]
                        dve.wait_ge(hi_done, n + u + 1)
                        wait(dve, mm_used, n + u - g.lag + 1)
                        V.tensor_tensor(wlo[:, s, :], raw[:, s, :], whi[:, s, :].bitcast(F32),
                                        ALU.subtract).then_inc(lo_done, 1)

                split(0, 0)
                last = g.pairs // 2 - 1
                with nc.vector.Fori(0, last) as i:
                    link.loop(i, links)
                    split(1, i)
                    evacuate(0, i)
                    split(0, i + 1)
                    evacuate(1, i)
                link.after(last)
                split(1, last)
                evacuate(0, last)
                evacuate(1, last)

            half_count = [0]

            def merge(g, dst, scale=None):
                n0 = half_count[0]

                def evacuate(par, i):
                    dve.wait_ge(lo_half_out, n0 + 2 * i + par + 1)
                    hi = psG[:, 2 * par:2 * par + 2, 0:T]
                    if scale is None:
                        ins = V.tensor_tensor(dst(par, i), hi, halves[:, par, :, :], ALU.add)
                    else:
                        ins = V.scalar_tensor_tensor(dst(par, i), hi, scale, halves[:, par, :, :],
                                                     ALU.mult, ALU.add)
                    ins.then_inc(pair_out, 1)

                half_count[0] += g.pairs
                return evacuate

            def tiles(buf):
                return lambda par, i: buf[:, bass.ds(4 * i + 2 * par, 2), :]

            modulation(SHIFT_SCALE1, 0, 2 * KD, (0, V_GMIX, KD))
            norm(NORM1, lambda j: hT[:, j, :], KD, 0, lambda: None)
            gemm(g_u, merge(g_u, tiles(uT)))
            gemm(g_q, merge(g_q, tiles(qT), SCALE))
            gemm(g_k, merge(g_k, tiles(kT)))
            gemm(g_v, merge(g_v, tiles(vT)))

            dve.wait_ge(f_half, 1)
            dve.wait_ge(wf_landed, 32)
            link(V.tensor_tensor(cum[:, 0, :], psX[0:NH, 3, 0:T], cum[:, 1, :], ALU.add))
            link(V.tensor_scalar(cum[:, 0, :], cum[:, 0, :], bf[:, 0:1], None, ALU.add))
            link(V.tensor_scalar(cum[:, 2, :], cum[:, 0, :], -1.0, None, ALU.mult))
            V.tensor_tensor(cum[:, 1, :], cum[:, 0, :], cum[:, 2, :], ALU.max).then_inc(f_abs, 1)
            dve.wait_ge(f_abs, 1)
            link(V.tensor_scalar(cum[:, 2, :], cum[:, 0, :], 0.0, None, ALU.min))
            dve.wait_ge(f_ln, 1)
            link(V.tensor_tensor(cum[:, 2, :], cum[:, 2, :], cum[:, 1, :], ALU.subtract))
            link(V.tensor_tensor_scan(cum[:, 3, :], ones[0:NH, :], cum[:, 2, :], 0.0, ALU.mult, ALU.add))
            dve.wait_ge(vN_done, 1)
            V.tensor_copy(vN[:, 0, :].rearrange("p (b n) -> p b n", b=2), psG[:, 0:2, :]
                          ).then_inc(vN_ready, 1)
            link(V.tensor_tensor_scan(mask[:, 0:P], ones[:, 0:P], ident[:], 0.0, ALU.mult, ALU.add))
            link(V.tensor_tensor(mask[:, 0:P], mask[:, 0:P], ident[:], ALU.subtract))
            link(V.tensor_scalar(mask[:, 2 * P:3 * P], mask[:, 0:P], MASKED, None, ALU.mult))
            link(V.memset(mask[:, P:2 * P], 0.0))
            link(V.tensor_copy(mask[:, 0:P], mask[:, 2 * P:3 * P]))

            def select_gates(h):
                wait(dve, score_done, h - 1)
                pick = ident[0:NH, h:h + 1]
                link(V.tensor_scalar(csel[:, h % 2, 0, :], cum[:, 3, :], pick, None, ALU.mult))
                V.tensor_scalar(csel[:, h % 2, 1, :], cum[:, 3, :], pick, -1.0, ALU.mult, ALU.mult
                                ).then_inc(csel_ready, 1)

            def maxima(h):
                b = h % 2
                dve.wait_ge(score_done, h + 1)
                wait(dve, probT_done, h - 1)
                V.tensor_tensor(prob[:, b, :], psX[:, b, 0:3 * P], mask[:], ALU.add).then_inc(masked, 1)
                dve.wait_ge(masked, h + 1)
                link(V.tensor_reduce(ncol[:, b, 0:1], prob[:, b, 0:P], AX_X, ALU.max))
                link(V.tensor_reduce(ncol[:, b, 1:2], prob[:, b, P:3 * P], AX_X, ALU.max))
                V.tensor_scalar(ncol[:, b, 2:4], ncol[:, b, 0:2], -1.0, None, ALU.mult
                                ).then_inc(max_ready, 1)

            def normalise(h):
                b = h % 2
                dve.wait_ge(exp_done, 2 * h + 2)
                link(V.reciprocal(ncol[:, b, 0:2], ncol[:, b, 4:6]))
                link(V.tensor_scalar(prob[:, b, 0:P], prob[:, b, 0:P], ncol[:, b, 0:1], None, ALU.mult))
                V.tensor_scalar(prob[:, b, P:3 * P], prob[:, b, P:3 * P], ncol[:, b, 1:2], None,
                                ALU.mult).then_inc(prob_ready, 1)

            def take_o(h):
                dve.wait_ge(pv_done, h + 1)
                V.tensor_copy(qT[:, h, :], psX[:, 3, 0:T]).then_inc(o_ready, 1)

            select_gates(0)
            select_gates(1)
            maxima(0)
            for h in range(NH):
                if h + 2 < NH:
                    select_gates(h + 2)
                if h + 1 < NH:
                    maxima(h + 1)
                normalise(h)
                if h >= 1:
                    take_o(h - 1)
            take_o(NH - 1)

            zre, zim, p0, p1 = (ssm_w[:, n, :, :] for n in range(4))

            def gelu_low(q):
                dve.wait_ge(gelu_hi, q + 1)
                V.tensor_tensor(AA[:, KS + q, T:2 * T], uT[:, q, :], AA[:, KS + q, 0:T].bitcast(F32),
                                ALU.subtract).then_inc(glu_act_ready, 1)

            for q in range(KS):
                ct, st = tab[:, q % 2, 0, :, :], tab[:, q % 2, 1, :, :]
                ere, eim = psG[:, :, 0:T], psG[:, :, T:2 * T]
                dve.wait_ge(tab_ready, q + 1)
                dve.wait_ge(e_done, q + 1)
                wait(dve, y_part, 2 * q)
                link(V.tensor_tensor(zre, ct, ere, ALU.mult))
                link(V.tensor_tensor(p0, st, eim, ALU.mult))
                link(V.tensor_tensor(zre, zre, p0, ALU.add))
                link(V.tensor_tensor(zim, ct, eim, ALU.mult))
                V.tensor_tensor(p1, st, ere, ALU.mult).then_inc(rotated, 1)
                dve.wait_ge(rotated, q + 1)
                link(V.tensor_tensor(zim, zim, p1, ALU.subtract))
                for z in (zre, zim):
                    for r in range(JQ):
                        j = JQ * q + r
                        link(V.tensor_tensor_scan(z[:, r, :], d(3)[:, j:j + 1].to_broadcast([P, T]),
                                                  z[:, r, :], 0.0, ALU.mult, ALU.add))
                link(V.tensor_tensor(p0, ct, zre, ALU.mult))
                V.scalar_tensor_tensor(p1, st, -1.0, zim, ALU.mult, ALU.mult).then_inc(z_part, 1)
                dve.wait_ge(z_part, 2 * q + 1)
                link(V.tensor_tensor(zre, st, zre, ALU.mult))
                V.tensor_tensor(zim, ct, zim, ALU.mult).then_inc(z_part, 1)
                if q >= 1:
                    gelu_low(q - 1)
                dve.wait_ge(y_part, 2 * q + 2)
                V.scalar_tensor_tensor(uT[:, q, :], uT[:, q, :], vec[:, V_D + q:V_D + q + 1],
                                       psX[:, 0, 0:T], ALU.mult, ALU.add).then_inc(y_ready, 1)
            gelu_low(KS - 1)

            modulation(ADA_BLOCKS, 2 * KD, 6 * KD, (1, V_GFFN, 4 * KD))
            dve.wait_ge(pair_out, g_v.p1)
            norm(NORMA, lambda j: qT[:, j, :], KS, 0, lambda: None)

            n_glu = half_count[0]

            def evacuate_glu(par, i):
                dve.wait_ge(lo_half_out, n_glu + 2 * i + par + 1)
                V.tensor_tensor(halves[:, par, :, :], psG[:, 2 * par:2 * par + 2, 0:T],
                                halves[:, par, :, :], ALU.add).then_inc(z_ready, 1)
                dve.wait_ge(sig_done, 4 * i + 2 * par + 2)
                y = uT[:, bass.ds(4 * i + 2 * par, 2), :]
                V.tensor_tensor(y, y, halves[:, par, :, :], ALU.mult).then_inc(pair_out, 1)

            half_count[0] += g_glu.pairs
            gemm(g_glu, evacuate_glu)
            norm(NORMS, lambda j: uT[:, j, :], KS, KS, lambda: None)

            def add_gated(g, gate_col, into):
                n0 = half_count[0]

                def evacuate(par, i):
                    dve.wait_ge(lo_half_out, n0 + 4 * i + 2 * par + 2)
                    for m in range(2):
                        link(V.scalar_tensor_tensor(
                            halves[:, par, m, :], psG[:, 2 * par + m, 0:T],
                            mod[:, bass.ds(gate_col + 4 * i + 2 * par + m, 1)], halves[:, par, m, :],
                            ALU.mult, ALU.add))
                    h2 = hT[:, bass.ds(4 * i + 2 * par, 2), :]
                    V.tensor_tensor(h2 if into is None else into(par), h2, halves[:, par, :, :], ALU.add
                                    ).then_inc(pair_out, 1)

                half_count[0] += 2 * g.pairs
                return evacuate

            gemm(g_out, add_gated(g_out, 2 * KD, None), 4)
            dve.wait_ge(pair_out, g_out.p1)
            norm(NORM2, lambda j: hT[:, j, :], KD, 0, lambda: None)

            link(V.memset(conv_in[:, :, 0:2], 0.0))
            n_up = half_count[0]
            half_count[0] += g_up.pairs

            def evacuate_up(par, i):
                dve.wait_ge(lo_half_out, n_up + 2 * i + par + 1)
                hi, lo = psG[:, 2 * par:2 * par + 2, 0:T], halves[:, par, :, :]
                if par == 0:
                    V.tensor_tensor(conv_in[:, :, 2:T + 2], hi, lo, ALU.add).then_inc(pair_out, 1)
                    dve.wait_ge(pair_out, g_up.p0 + 2 * i + 1)

                    def col(at, m):
                        return vec[:, bass.ds(at + 2 * i + m, 1)]

                    for m in range(2):
                        link(V.tensor_scalar(gate[:, m, :], conv_in[:, m, 2:T + 2], col(V_CONV2, m),
                                             col(V_CONVB, m), ALU.mult, ALU.add))
                    for m in range(2):
                        link(V.scalar_tensor_tensor(gate[:, m, :], conv_in[:, m, 1:T + 1],
                                                    col(V_CONV1, m), gate[:, m, :], ALU.mult, ALU.add))
                    link(V.scalar_tensor_tensor(gate[:, 0, :], conv_in[:, 0, 0:T], col(V_CONV0, 0),
                                                gate[:, 0, :], ALU.mult, ALU.add))
                    V.scalar_tensor_tensor(gate[:, 1, :], conv_in[:, 1, 0:T], col(V_CONV0, 1),
                                           gate[:, 1, :], ALU.mult, ALU.add).then_inc(conv_done, 1)
                    dve.wait_ge(conv_done, i + 1)
                else:
                    V.tensor_tensor(branch[:], hi, lo, ALU.add).then_inc(pair_out, 1)
                    dve.wait_ge(pair_out, g_up.p0 + 2 * i + 2)
                    dve.wait_ge(silu_done, i + 1)
                    V.tensor_tensor(gated[:], gate[:], branch[:], ALU.mult).then_inc(gated_ready, 1)
                    dve.wait_ge(ghi_done, i + 1)
                    V.tensor_tensor(GG[:, bass.ds(2 * i, 2), T:2 * T], gated[:],
                                    GG[:, bass.ds(2 * i, 2), 0:T].bitcast(F32), ALU.subtract
                                    ).then_inc(g_ready, 1)

            gemm(g_up, evacuate_up, 5)

            gemm(g_down, add_gated(g_down, 5 * KD, lambda par: halves[:, par, :, :]), 4)

            dve.wait_ge(root2_done, 1)
            link(V.reciprocal(tiny[:, 2:4], tiny[:, 2:4]))
            dve.wait_ge(g_rows_landed, 16)
            for tt in range(TT):
                V.scalar_tensor_tensor(out_n[:, tt, :], out_n[:, tt, :], tiny[:, 2 + tt:3 + tt],
                                       g_rows[:], ALU.mult, ALU.mult).then_inc(final_ready, 1)

        @block.tensor
        def _(pe):
            M = nc.tensor.matmul
            uses = [0] * RAW
            pe.wait_ge(pool_chain, 2)
            pe.wait_ge(stage_ready, 3)
            for s in range(4):
                last = nc.tensor.transpose(psX[:, 0, P * s:P * s + P], stage[:, s, :], ident[:])
            last.then_inc(vecT_done, 1)
            pe.wait_ge(x_landed, 16 * TT)
            for r in range(4):
                wait(pe, hT_ready, r - 1)
                if r == 2:
                    pe.wait_ge(hT_ready, 2)
                if r == 3:
                    pe.wait_ge(hT_ready, 2)
                for j in range(4):
                    for tt in range(TT):
                        last = nc.tensor.transpose(
                            psG[:, 2 * (r % 2) + j // 2, (j % 2) * T + tt * P:(j % 2) * T + tt * P + P],
                            xn[:, tt, (4 * r + j) * P:(4 * r + j + 1) * P], ident[:])
                last.then_inc(xT_done, 1)

            def ada_block(b, par, first):
                wait(pe, ada_out, b - 1)
                for u in range(AU):
                    s = u % RAW
                    pe.wait_ge(raw_landed[s], 16 * (first[s] + (b - first["b0"]) * (AU // RAW) + u // RAW)
                               + 16)
                    for f in range(AK):
                        k = AK * u + f
                        g = k % 4
                        last = M(psX[32 * g:32 * g + 32, par, :], cond[:, k, :],
                                 raw[:, s, f * AN:(f + 1) * AN], start=(k < 4), stop=(k >= KD - 4),
                                 tile_position=(0, 32 * g))
                    last.then_inc(ada_used, 1)

            def ada_columns(b, par):
                pe.wait_ge(ada_out, b + 1)
                for m in range(AN // P):
                    last = M(psX[:, 2, bass.ds(b * (AN // P) + m, 1)], ada_rows[:, par, m * P:m * P + P],
                             ones[:, 0:1], start=True, stop=True)
                last.then_inc(ada_cols, 1)

            def ada_phase(b0, b1):
                first = dict(enumerate(uses))
                first["b0"] = b0
                ada_block(b0, 0, first)
                with nc.tensor.Fori(b0 // 2, b1 // 2 - 1) as i:
                    ada_block(2 * i + 1, 1, first)
                    ada_columns(2 * i, 0)
                    ada_block(2 * i + 2, 0, first)
                    ada_columns(2 * i + 1, 1)
                ada_block(b1 - 1, 1, first)
                ada_columns(b1 - 2, 0)
                ada_columns(b1 - 1, 1)
                for s in range(RAW):
                    uses[s] += (b1 - b0) * AU // RAW

            def norm(which, n):
                index, g0 = which
                wait(pe, root_done, index)
                for j in range(n):
                    pe.wait_ge(sq_done, g0 + j + 1)
                    M(psX[:, 3, 0:T], ones[:, 0:P], sq[:, j % 2, :], start=(j == 0), stop=(j == n - 1)
                      ).then_inc(ss_used, 1)

            def gemm(g, operand, ready):
                def pair(par, i):
                    p = g.p0 + 2 * i + par
                    wait(pe, pair_out, p - 1)
                    for u in range(g.units):
                        s = g.slots[par][u]
                        pe.wait_ge(lo_done, g.n0 + (2 * i + par) * g.units + u + 1)
                        ready(UK * u + UK - 1)
                        for f in range(UK):
                            k = UK * u + f
                            for m in range(2):
                                at = f * UN + m * P
                                bank = 2 * par + m
                                M(psG[:, bank, :], whi[:, s, at:at + P], operand(k), start=(k == 0),
                                  stop=False)
                                last = M(psG[:, bank, 0:T], wlo[:, s, at:at + P], operand(k)[:, 0:T],
                                         start=False, stop=(k == g.units * UK - 1))
                        last.then_inc(mm_used, 1)

                pair(0, 0)
                pair(1, 0)
                with nc.tensor.Fori(1, g.pairs // 2) as i:
                    pair(0, i)
                    pair(1, i)
                for s in range(RAW):
                    uses[s] += g.pairs // 2 * g.per[s]

            pe.wait_ge(cond_ready, 3)
            pe.wait_ge(consts_ready, 1)
            ada_phase(0, SHIFT_SCALE1)

            pe.wait_ge(bc_ready, 4)
            pe.wait_ge(hT_ready, 4)
            for r in range(4):
                if r >= 2:
                    pe.wait_ge(bcT_ready, r - 1)
                for q in range(KS):
                    src = (b_wide[:, r, JQ * q:JQ * q + JQ, :, :].rearrange("p j g h -> p (j g h)")
                           if r < 2 else c_twice[:, r - 2, q, :, :].rearrange("p g n -> p (g n)"))
                    last = nc.tensor.transpose(
                        psG[:, 2 * (r % 2) + q // 4, (q % 4) * P:(q % 4) * P + P], src, ident[:])
                last.then_inc(bcT_done, 1)
            pe.wait_ge(bcT_ready, 6)

            norm(NORM1, KD)
            from_aa = lambda k: AA[:, k, :]
            for g in (g_u, g_q, g_k, g_v):
                gemm(g, from_aa, lambda k: pe.wait_ge(act_ready, k + 1))

            pe.wait_ge(wf_landed, 32)
            for k in range(KD):
                last = M(psX[0:NH, 3, :], wf[:, k, :], AA[:, k, :].bitcast(F32), start=(k == 0),
                         stop=(k == KD - 1))
            last.then_inc(f_done, 1)
            pe.wait_ge(pair_out, g_v.p1)
            for tt in range(TT):
                for h in range(NH):
                    last = nc.tensor.transpose(
                        psG[:, 2 * tt + h // 4, (h % 4) * P:(h % 4) * P + P],
                        vT[:, h, tt * P:tt * P + P], ident[:])
            last.then_inc(vN_done, 1)

            def scores(h):
                b = h % 2
                pe.wait_ge(csel_ready, h + 1)
                wait(pe, masked, h - 1)
                for tt, at, n in ((0, 0, P), (1, P, 2 * P)):
                    dst = psX[:, b, at:at + n]
                    t = slice(tt * P, tt * P + P)
                    M(dst, qT[:, h, t], kT[:, h, 0:n], start=True, stop=False)
                    M(dst, csel[:, b, 0, t], ones[0:NH, 0:n], start=False, stop=False)
                    last = M(dst, ones[0:NH, 0:P], csel[:, b, 1, 0:n], start=False, stop=True)
                last.then_inc(score_done, 1)

            scores(0)
            pe.wait_ge(vN_ready, 2)
            for h in range(NH):
                b = h % 2
                if h + 1 < NH:
                    scores(h + 1)
                pe.wait_ge(prob_ready, h + 1)
                wait(pe, probT_ready, h)
                for n in range(3):
                    last = nc.tensor.transpose(psX[:, 2, n * P:n * P + P], prob[:, b, n * P:n * P + P],
                                               ident[:])
                last.then_inc(probT_done, 1)
                pe.wait_ge(probT_ready, h + 1)
                wait(pe, o_ready, h)
                v = lambda st: vN[:, st, h * HD:h * HD + HD]
                M(psX[:, 3, 0:T], v(0), probT[:, b, 0:T], start=True, stop=False)
                M(psX[:, 3, P:T], v(1), probT[:, b, T:T + P], start=False, stop=True
                  ).then_inc(pv_done, 1)

            def inputs(q):
                wait(pe, rotated, q)
                for a, mat in enumerate((btr, bti)):
                    for r in range(JQ):
                        rows = slice(32 * r, 32 * r + 32)
                        last = M(psG[:, r, a * T:a * T + T], mat[rows, q, :], uT[rows, q, :],
                                 start=True, stop=True, tile_position=(32 * r, 0))
                last.then_inc(e_done, 1)

            inputs(0)
            for q in range(KS):
                if q + 1 < KS:
                    inputs(q + 1)
                wait(pe, y_ready, q)
                for part, products in enumerate((((2, ctr), (3, ctr)), ((0, cti), (1, cti)))):
                    pe.wait_ge(z_part, 2 * q + part + 1)
                    for a, (n, mat) in enumerate(products):
                        for r in range(JQ):
                            cols = slice(32 * r, 32 * r + 32)
                            last = M(psX[cols, 0, 0:T], mat[:, q, cols], ssm_w[:, n, r, :],
                                     start=(part == 0 and a == 0), stop=(part == 1 and a == 1),
                                     tile_position=(0, 32 * r))
                    last.then_inc(y_part, 1)

            pe.wait_ge(y_ready, KS)
            ada_phase(SHIFT_SCALE1, ADA_BLOCKS)
            norm(NORMA, KS)
            gemm(g_glu, lambda k: AA[:, KS + k, :], lambda k: pe.wait_ge(glu_act_ready, k + 1))
            norm(NORMS, KS)
            gemm(g_out, from_aa, lambda k: pe.wait_ge(act_ready, NORMA[1] + k + 1))
            norm(NORM2, KD)
            gemm(g_up, from_aa, lambda k: pe.wait_ge(act_ready, NORM2[1] + k + 1))

            def down_pair(par, i):
                p = g_down.p0 + 2 * i + par
                pe.wait_ge(pair_out, p - 1)
                for u in range(g_down.units):
                    s = g_down.slots[par][u]
                    pe.wait_ge(lo_done, g_down.n0 + (2 * i + par) * g_down.units + u + 1)
                    pe.wait_ge(g_ready, (UK * (u + 1)) // 2)
                    for f in range(UK):
                        k = UK * u + f
                        for m in range(2):
                            at, bank = f * UN + m * P, 2 * par + m
                            M(psG[:, bank, :], whi[:, s, at:at + P], GG[:, k, :], start=(k == 0),
                              stop=False)
                            last = M(psG[:, bank, 0:T], wlo[:, s, at:at + P], GG[:, k, 0:T],
                                     start=False, stop=(k == KF - 1))
                    last.then_inc(mm_used, 1)

            def tail(pair, par):
                pe.wait_ge(pair_out, g_down.p0 + pair + 1)
                wait(pe, tail_out, pair - 1)
                for tt in range(TT):
                    for m in range(2):
                        last = nc.tensor.transpose(psX[:, par, tt * T + m * P:tt * T + m * P + P],
                                                   halves[:, par, m, tt * P:tt * P + P], ident[:])
                last.then_inc(tail_T, 1)

            down_pair(0, 0)

            def down_round(i):
                down_pair(1, i)
                tail(2 * i, 0)
                down_pair(0, i + 1)
                tail(2 * i + 1, 1)

            down_round(0)
            with nc.tensor.Fori(1, g_down.pairs // 2 - 1) as i:
                down_round(i)
            down_pair(1, g_down.pairs // 2 - 1)
            tail(g_down.pairs - 2, 0)
            tail(g_down.pairs - 1, 1)


_INS = ["x", "c", "w_ada", "b_ada", "g_mix", "w_in", "b_f", "a_re", "a_im", "log_dt", "ssm_b_re",
        "ssm_b_im", "ssm_c_re", "ssm_c_im", "ssm_d", "w_glu", "b_glu", "g_attn_out", "g_ssm_out",
        "w_out", "g_ffn", "w_up", "conv_w", "conv_b", "w_down", "g_final"]
_MATRICES = ("w_ada", "w_in", "w_glu", "w_out", "w_up", "w_down")


def kernel(**inputs):
    import concourse.bacc as _bacc
    from concourse.bass_utils import run_bass_kernel_spmd as _run

    nc = _bacc.Bacc("TRN2", target_bir_lowering=False, num_devices=1)
    arrays, args = {}, []
    for name in _INS:
        a = np.ascontiguousarray(inputs[name])
        if name in _MATRICES:
            a = a.reshape(a.shape[1:])
        arrays[f"in_{name}"] = a
        args.append(nc.dram_tensor(f"in_{name}", a.shape, mybir.dt.from_np(a.dtype),
                                   kind="ExternalInput").ap())
    args.append(nc.dram_tensor("out_0", (1, T, D), F32, kind="ExternalOutput").ap())
    build(nc, *args)
    r = _run(nc, [arrays], core_ids=[0])
    return r.results[0]["out_0"]
```

```python
from contextlib import ExitStack

import concourse.bass as bass
import numpy as np
from concourse import mybir

F32 = mybir.dt.float32
F32R = mybir.dt.float32r
I32 = mybir.dt.int32
ALU = mybir.AluOpType
ACT = mybir.ActivationFunctionType
AX_X = mybir.AxisListType.X

P = 128
T = 256
TT = T // P
D = 2048
KD = D // P
NH = 8
HD = 128
AW = NH * HD
SW = 1024
KS = SW // P
NG, NS, GH = 64, 64, 16
NJ = NG * NS // P
JQ = 4
FF = 5632
KF = FF // P
EPS = 1e-6
SCALE = HD ** -0.5

UK = 4
UN = 256
USZ = UK * UN
RAW = 4
SPL = 4
AN = 512
AK = USZ // AN
AU = KD // AK
SHIFT_SCALE1 = 2 * D // AN
BS = D // AN
BC = AN // P
ADA_BLOCKS = 6 * D // AN

MAGIC = 1.5 * 2.0 ** 23
TWO_PI = 2 * np.pi
C1 = 6.28125
C2 = float(np.floor((TWO_PI - C1) * 2.0 ** 21) / 2.0 ** 21)
C3 = float(TWO_PI - C1 - C2)
PI_IN = 3.1415925
MASKED = -1.0e30

V_GMIX, V_GFFN, V_GFINAL, V_GATTN, V_GSSM, V_BGLU, V_D, V_CONVB = 0, 16, 32, 48, 56, 64, 72, 80
V_BADA, V_ARE = 128, 224
V_CONV0, V_CONV1, V_AIM = 256, 300, 344
V_CONV2, V_COND, V_LOGDT = 384, 428, 448


def wait(eng, sem, value):
    if isinstance(value, int) and value <= 0:
        return
    eng.wait_ge(sem, value)


class Chain:

    def __init__(self, eng, sem):
        self.eng, self.sem, self.start, self.n = eng, sem, 0, 0

    def __call__(self, ins):
        ins.then_inc(self.sem, 1)
        self.n += 1
        self.eng.wait_ge(self.sem, self.start + self.n)

    def loop(self, i, per):
        self.base, self.per = self.start + self.n, per
        self.start, self.n = self.base + i * per, 0

    def after(self, passes):
        assert self.n == self.per, (self.n, self.per)
        self.start, self.n = self.base + passes * self.per, 0


STEPS = 64
SSM_FROM = 10
SSM_PIECES = 6
M_AT = 384


def window_pair(p):
    return ("u", p) if p < 4 else ("qkv"[(p - 4) % 3], (p - 4) // 3)


def ssm_piece(t):
    q, n = divmod(t - SSM_FROM, SSM_PIECES)
    return (q, n) if 0 <= q <= KS else None


def attention_step(t):
    found = []
    for h in range(NH):
        at = 28 + 12 * (h // 2) + 5 * (h % 2)
        if at <= t < at + 5:
            found.append((h, t - at))
    return found


class Gemm:

    def __init__(self, weights, pairs, units, column, before=None):
        self.w = weights.rearrange("(u f p) n -> u p f n", f=UK, p=P)
        self.pairs, self.units = pairs, units
        self.column = column
        self.n0, self.p0 = (before.n1, before.p1) if before else (STEPS, 0)
        self.n1, self.p1 = self.n0 + pairs * units, self.p0 + pairs
        self.skip = 0 if 2 * units % SPL == 0 else -units % SPL
        both = [par * (units + self.skip) + u for par in range(2) for u in range(units)]
        self.raw_slots = [[both[par * units + u] % RAW for u in range(units)] for par in range(2)]
        self.slots = [[both[par * units + u] % SPL for u in range(units)] for par in range(2)]
        order = self.raw_slots[0] + self.raw_slots[1]
        self.per = [order.count(s) for s in range(RAW)]
        self.turn = [[order[:par * units + u].count(self.raw_slots[par][u]) for u in range(units)]
                     for par in range(2)]
        self.raw_lag, self.lag = RAW - self.skip, SPL - self.skip


def build(nc, x, c, w_ada, b_ada, g_mix, w_in, b_f, a_re, a_im, log_dt, ssm_b_re, ssm_b_im,
          ssm_c_re, ssm_c_im, ssm_d, w_glu, b_glu, g_attn_out, g_ssm_out, w_out, g_ffn, w_up,
          conv_w, conv_b, w_down, g_final, out):
    ctx = ExitStack()
    with ctx:
        def sem(name):
            return ctx.enter_context(nc.semaphore(name))

        def place(at, *tiles):
            got = []
            for name, shape, dt in tiles:
                got.append(nc.alloc_sbuf_tensor_at(name, shape, dt, offset=at))
                at += -(-int(np.prod(shape[1:])) * 4 // 32) * 32
            return at, got

        base = -(-nc.sbuf_base // 64) * 64
        small_at, (hT, vec, mod, ident, ones, sq, rb, halves, gains, tiny, ncol, bf, sel, raw, whi,
                   wlo) = place(
            base,
            ("hT", [P, KD, T], F32),
            ("vec", [P, 512], F32),
            ("mod", [P, 96], F32),
            ("ident", [P, P], F32),
            ("ones", [P, T], F32),
            ("sq", [P, 2, T], F32),
            ("rb", [P, T], F32),
            ("halves", [P, 2, 2, T], F32),
            ("gains", [P, 2, KD], F32),
            ("tiny", [P, 24], F32),
            ("ncol", [P, 2, 8], F32),
            ("bf", [NH, 8], F32),
            ("sel", [P, 8], F32),
            ("raw", [P, RAW, USZ], F32),
            ("whi", [P, SPL, USZ], F32R),
            ("wlo", [P, SPL, USZ], F32R),
        )
        end1, (cond, ada_rows, iota_i, iota_f, disc) = place(
            small_at,
            ("cond", [P, KD, 32], F32),
            ("ada_rows", [P, 2, AN], F32),
            ("iota_i", [P, 16], I32), ("iota_f", [P, 16], F32),
            ("disc", [P, 14, NJ], F32),
        )
        end2, (conv_in, gate, branch, gated) = place(
            small_at,
            ("conv_in", [P, 2, T + 2], F32), ("gate", [P, 2, T], F32),
            ("branch", [P, 2, T], F32), ("gated", [P, 2, T], F32),
        )
        acts_at = max(end1, end2)
        attn_at, (AA,) = place(acts_at, ("AA", [P, KD, 2 * T], F32R))
        _, (out_n, g_rows) = place(acts_at, ("out_n", [P, TT, D], F32), ("g_rows", [P, D], F32))
        ffn_at, (prob, probT, mask, csel, cum, tab_t, rot_t) = place(
            attn_at,
            ("prob", [P, 2, 3 * P], F32), ("probT", [P, 2, 3 * P], F32), ("mask", [P, 3 * P], F32),
            ("csel", [NH, 2, 2, T], F32), ("cum", [NH, T], F32),
            ("tab_t", [P, JQ, 16, 16], F32), ("rot_t", [P, 2, T], F32),
        )
        _, (wf,) = place(ffn_at - 2 * T * 4, ("wf", [P, KD, 32], F32))
        csel_at = attn_at + (2 * 3 * P * 2 + 3 * P) * 4
        _, (fw,) = place(csel_at, ("fw", [NH, 4, T], F32))
        _, (b_tmp,) = place(csel_at, ("b_tmp", [P, NJ, GH], F32))
        sq_at = base + (KD * T + 512 + 96 + P + T) * 4
        _, (vT,) = place(sq_at, ("vT", [P, 2, T], F32))
        end, (GG,) = place(ffn_at, ("GG", [P, KF, 2 * T], F32R))
        assert end <= nc.sbuf_usable_end
        mix_end, (uT, qT, kT, vN, btr, bti, ctr, cti, fac, tab, ssm_w) = place(
            ffn_at,
            ("uT", [P, KS, T], F32),
            ("qT", [P, NH, T], F32),
            ("kT", [P, NH, T], F32),
            ("vN", [P, TT, AW], F32),
            ("btr", [P, KS, P], F32), ("bti", [P, KS, P], F32),
            ("ctr", [P, KS, P], F32), ("cti", [P, KS, P], F32),
            ("fac", [P, 4, NJ, 16], F32),
            ("tab", [P, 2, 2, JQ, T], F32),
            ("ssm_w", [P, 4, JQ, T], F32),
        )
        assert mix_end <= end
        at_q = ffn_at + KS * T * 4
        _, (stage,) = place(ffn_at, ("stage", [P, 4, P], F32))
        _, (b_raw, b_bar, b_wide) = place(
            at_q,
            ("b_raw", [P, 2, NJ, GH], F32), ("b_bar", [P, 2, NJ, GH], F32),
            ("b_wide", [P, 2, NJ, 2, GH], F32),
        )
        _, (c_twice,) = place(at_q + 2 * KS * T * 4, ("c_twice", [P, 2, KS, 2, NS], F32))
        tab_at = mix_end - 2 * 16384
        _, (ph,) = place(tab_at, ("ph", [P, 4, NJ, 16], F32))
        _, (xn,) = place(mix_end - 16384, ("xn", [P, TT, D], F32))
        _, (xr,) = place(mix_end - 16384, ("xr", [P, KD, T], F32))

        psG = ctx.enter_context(nc.psum_tensor("psG", [P, 4, 512], F32))
        psX = ctx.enter_context(nc.psum_tensor("psX", [P, 4, 512], F32))

        first_of = {"q": 0, "k": AW, "v": 2 * AW, "u": 3 * AW + NH}
        w_in_v = w_in.rearrange("(u f p) n -> u p f n", f=UK, p=P)
        plain = lambda par, i: (2 * i + par) * UN
        g_glu = Gemm(w_glu, 4, KS // UK, plain)
        g_out = Gemm(w_out, 8, KD // UK, plain, g_glu)
        g_up = Gemm(w_up, KF, KD // UK, lambda par, i: par * FF + i * UN, g_out)
        g_down = Gemm(w_down, 8, KF // UK, plain, g_up)

        raw_landed = [sem(f"raw_landed{s}") for s in range(RAW)]
        x_landed, stage_landed, bc_landed, wf_landed = map(
            sem, ("x_landed", "stage_landed", "bc_landed", "wf_landed"))
        g_rows_landed, out_stored = sem("g_rows_landed"), sem("out_stored")
        consts_ready, pool_chain = sem("consts_ready"), sem("pool_chain")
        stage_ready, vecT_done, vec_ready = sem("stage_ready"), sem("vecT_done"), sem("vec_ready")
        xT_done, hT_ready = sem("xT_done"), sem("hT_ready")
        cond_act, cond_ready = sem("cond_act"), sem("cond_ready")
        act_setup, dve_setup = sem("act_setup"), sem("dve_setup")
        bc_ready, bcT_done, bcT_ready = sem("bc_ready"), sem("bcT_done"), sem("bcT_ready")
        ada_used, ada_out, ada_cols, mod_ready = map(
            sem, ("ada_used", "ada_out", "ada_cols", "mod_ready"))
        sq_done, ss_used, root_done, rms_ready = map(
            sem, ("sq_done", "ss_used", "root_done", "rms_ready"))
        nt_ready, affine_done, nhi_done, act_ready = map(
            sem, ("nt_ready", "affine_done", "nhi_done", "act_ready"))
        hi_done, lo_done, mm_used, lo_half_out, pair_out = map(
            sem, ("hi_done", "lo_done", "mm_used", "lo_half_out", "pair_out"))
        tile_done, tile_half, tile_out = sem("tile_done"), sem("tile_half"), sem("tile_out")
        wf_zero, f_done, f_rows, f_sum, f_abs, f_ln, cum_ready = map(
            sem, ("wf_zero", "f_done", "f_rows", "f_sum", "f_abs", "f_ln", "cum_ready"))
        vN_done, vN_ready = sem("vN_done"), sem("vN_ready")
        csel_ready, score_done, masked, exp_done = map(
            sem, ("csel_ready", "score_done", "masked", "exp_done"))
        max_ready, prob_ready, probT_done, probT_ready, pv_done, o_ready = map(
            sem, ("max_ready", "prob_ready", "probT_done", "probT_ready", "pv_done", "o_ready"))
        tab_ready, e_done, rotated, z_part, y_part, y_ready, gelu_done = map(
            sem, ("tab_ready", "e_done", "rotated", "z_part", "y_part", "y_ready", "gelu_done"))
        glu_hi, glu_act_ready = sem("glu_hi"), sem("glu_act_ready")
        z_ready, sig_done, conv_done, silu_done, gated_ready, ghi_done, g_ready = map(
            sem, ("z_ready", "sig_done", "conv_done", "silu_done", "gated_ready", "ghi_done",
                  "g_ready"))
        tail_T, tail_out, sumsq_done = sem("tail_T"), sem("tail_out"), sem("sumsq_done")
        root2_done, final_ready = sem("root2_done"), sem("final_ready")
        dve_chain, act_chain = sem("dve_chain"), sem("act_chain")

        NORM1, NORMA, NORMS, NORM2 = (0, 0), (1, KD // 4), (2, (KD + KS) // 4), (3, (KD + 2 * KS) // 4)
        STAGE_DMAS, BC_DMAS = 15, 6
        WINDOW_ADA = SHIFT_SCALE1 * AU

        block = ctx.enter_context(nc.Block())

        @block.sync
        def _(sp):
            owner = [None] * RAW

            def load(s, f, src, done):
                if owner[s]:
                    sp.wait_ge(*owner[s])
                sp.dma_start(raw[:, s, :].rearrange("p (f n) -> p f n", f=f), src
                             ).then_inc(raw_landed[s], 16)
                owner[s] = done

            w_ada_v = w_ada.rearrange("(u f p) n -> u p f n", f=AK, p=P)

            def ada_unit(which, i, u):
                return w_ada_v[u, :, :, bass.ds((which * BS + i) * AN, AN)]

            for which in range(2):
                for u in range(AU):
                    load(u % RAW, AK, ada_unit(which, 0, u), (ada_used, which * AU + u + 1))
            with nc.sync.Fori(1, BS) as i:
                for which in range(2):
                    for u in range(AU):
                        sp.wait_ge(ada_used, (2 * i + which) * AU + u - RAW + 1)
                        sp.dma_start(raw[:, u % RAW, :].rearrange("p (f n) -> p f n", f=AK),
                                     ada_unit(which, i, u)).then_inc(raw_landed[u % RAW], 16)
            owner[:] = [(ada_used, WINDOW_ADA - RAW + s + 1) for s in range(RAW)]

            for t in range(STEPS):
                kind, j = window_pair(t // 4)
                at = first_of[kind] + j * UN
                load(3 * t % RAW, UK, w_in_v[t % 4, :, :, at:at + UN], (lo_done, t + 1))
                for n in range(2):
                    a = 2 * t + n
                    at = (SHIFT_SCALE1 + a // AU) * AN
                    load((3 * t + 1 + n) % RAW, AK, w_ada_v[a % AU, :, :, at:at + AN],
                         (ada_used, WINDOW_ADA + a + 1))

            for g in (g_glu, g_out, g_up, g_down):
                for par in range(2):
                    for u in range(g.units):
                        at = g.column(par, 0)
                        load(g.raw_slots[par][u], UK, g.w[u, :, :, at:at + UN],
                             (lo_done, g.n0 + par * g.units + u + 1))
                with nc.sync.Fori(1, g.pairs // 2) as i:
                    for par in range(2):
                        for u in range(g.units):
                            sp.wait_ge(lo_done, g.n0 + (2 * i + par) * g.units + u - g.raw_lag + 1)
                            s = g.raw_slots[par][u]
                            sp.dma_start(raw[:, s, :].rearrange("p (f n) -> p f n", f=UK),
                                         g.w[u, :, :, bass.ds(g.column(par, i), UN)]
                                         ).then_inc(raw_landed[s], 16)
                both = [(par, u) for par in range(2) for u in range(g.units)]
                for n, (par, u) in enumerate(both):
                    owner[g.raw_slots[par][u]] = (lo_done, g.n1 - 2 * g.units + n + 1)
            sp.wait_ge(out_stored, 16 * TT)

        @block.gpsimd
        def _(pool):
            link = Chain(pool, pool_chain)
            link(nc.gpsimd.memset(ident[:], 0.0))
            link(nc.gpsimd.affine_select(out=ident[:], in_=ident[:], compare_op=ALU.not_equal, fill=1.0,
                                         base=0, pattern=[[-1, P]], channel_multiplier=1))
            nc.gpsimd.memset(ones[:], 1.0).then_inc(consts_ready, 1)
            nc.gpsimd.iota(iota_i[:], pattern=[[1, 16]], base=0, channel_multiplier=0
                           ).then_inc(consts_ready, 1)
            nc.gpsimd.memset(wf[:], 0.0).then_inc(wf_zero, 1)
            for q in range(KS):
                js = slice(JQ * q, JQ * q + JQ)
                cs, ss = (fac[:, a, js, :].unsqueeze(2).to_broadcast([P, JQ, 16, 16]) for a in (0, 1))
                ck, sk = (fac[:, a, js, :].unsqueeze(3).to_broadcast([P, JQ, 16, 16]) for a in (2, 3))
                ct, st = (tab[:, q % 2, a, :, :].rearrange("p j (k s) -> p j k s", s=16)
                          for a in (0, 1))
                if q == 0:
                    pool.wait_ge(act_setup, 6)
                if q >= 2:
                    pool.wait_ge(z_part, 2 * (q - 1))
                link(nc.gpsimd.tensor_tensor(ct, cs, ck, ALU.mult))
                link(nc.gpsimd.tensor_tensor(tab_t[:], ss, sk, ALU.mult))
                link(nc.gpsimd.tensor_tensor(ct, ct, tab_t[:], ALU.subtract))
                link(nc.gpsimd.tensor_tensor(st, cs, sk, ALU.mult))
                link(nc.gpsimd.tensor_tensor(tab_t[:], ss, ck, ALU.mult))
                nc.gpsimd.tensor_tensor(st, st, tab_t[:], ALU.add).then_inc(tab_ready, 1)
                pool.wait_ge(tab_ready, q + 1)

        @block.scalar
        def _(act):
            link = Chain(act, act_chain)
            uses = [0] * RAW

            def row(v):
                return v.rearrange("l (r p) -> (l r) p", p=P)

            act.wait_ge(stage_ready, 1)
            for s, at, src in (
                (3, V_COND, row(c)), (0, V_GMIX, row(g_mix)), (0, V_GFFN, row(g_ffn)),
                (0, V_GFINAL, g_final.rearrange("(r p) -> r p", p=P)), (0, V_GATTN, row(g_attn_out)),
                (0, V_GSSM, row(g_ssm_out)), (0, V_BGLU, row(b_glu)),
                (0, V_D, ssm_d.rearrange("l (r g) h -> (l r) (g h)", g=8)), (0, V_CONVB, row(conv_b)),
                (1, V_BADA, row(b_ada)), (1, V_ARE, a_re.rearrange("l (r g) p -> (l r) (g p)", g=2)),
                (2, V_AIM, a_im.rearrange("l (r g) p -> (l r) (g p)", g=2)),
                (2, V_CONV0, conv_w.rearrange("l w (r p) -> (l w r) p", p=P)[0:2 * KF]),
                (3, V_CONV2, conv_w.rearrange("l w (r p) -> (l w r) p", p=P)[2 * KF:3 * KF]),
            ):
                r = at - P * s
                act.dma_start(stage[r:r + src.shape[0], s, :], src).then_inc(stage_landed, 16)
            with nc.allow_non_contiguous_dma(reason="64 numbers"):
                act.dma_start(tiny[V_LOGDT % P:V_LOGDT % P + NJ, KD:KD + 2],
                              log_dt.rearrange("l (r g) -> (l r) g", g=2)).then_inc(stage_landed, 16)
                act.dma_start(bf[:, 0:1], b_f.rearrange("l h -> h l")).then_inc(wf_landed, 16)
            xv = x.rearrange("b (t p) d -> p (b t) d", p=P)
            for tt in range(TT):
                act.dma_start(xn[:, tt, :], xv[:, tt, :]).then_inc(x_landed, 16)

            act.wait_ge(vec_ready, 1)
            nc.scalar.activation(tiny[:, 0:KD], vec[:, V_COND:V_COND + KD], ACT.Silu
                                 ).then_inc(cond_act, 1)
            for r in (1, 3):
                act.wait_ge(xT_done, r + 1)
                nc.scalar.activation(hT[:, 4 * r:4 * r + 4, :].rearrange("p (b j) t -> p b (j t)", j=2),
                                     psG[:, 2:4, :], ACT.Copy).then_inc(hT_ready, 1)
            nc.scalar.activation(disc[:, 0, :], vec[:, V_LOGDT:V_LOGDT + NJ], ACT.Exp
                                 ).then_inc(act_setup, 1)
            act.wait_ge(dve_setup, 1)
            nc.scalar.activation(disc[:, 3, :], disc[:, 1, :], ACT.Exp).then_inc(act_setup, 1)
            for half in range(2):
                act.wait_ge(dve_setup, 2 + half)
                nc.scalar.activation(fac[:, 2 * half + 1, :, :], ph[:, 1, :, :], ACT.Sin
                                     ).then_inc(act_setup, 1)
                nc.scalar.activation(fac[:, 2 * half, :, :], ph[:, 3, :, :], ACT.Sin
                                     ).then_inc(act_setup, 1)

            nt = xr

            def squares(src, groups, at):
                for gr in range(groups):
                    nc.scalar.activation(xr[:, 4 * gr:4 * gr + 4, :], src[:, 4 * gr:4 * gr + 4, :],
                                         ACT.Square).then_inc(sq_done, 1)

            def root(which, width, sums):
                index, g0 = which
                act.wait_ge(ss_used, sums)
                wait(act, nt_ready, g0)
                nc.scalar.activation(rb[:], psX[:, 3, 0:T], ACT.Sqrt, scale=1.0 / width,
                                     bias=ncol[:, 0, 7:8]).then_inc(root_done, 1)

            def gains_and_hi(group, gr, k0, scale, shift):
                act.wait_ge(nt_ready, group + 1)
                for j in range(4 * gr, 4 * gr + 4):
                    if shift is None:
                        nc.scalar.activation(nt[:, j, :], nt[:, j, :], ACT.Copy, scale=scale(j)
                                             ).then_inc(affine_done, 1)
                    else:
                        nc.scalar.activation(nt[:, j, :], nt[:, j, :], ACT.Identity, scale=scale(j),
                                             bias=shift(j)).then_inc(affine_done, 1)
                act.wait_ge(affine_done, 4 * group + 4)
                nc.scalar.activation(AA[:, k0 + 4 * gr:k0 + 4 * gr + 4, 0:T], nt[:, 4 * gr:4 * gr + 4, :],
                                     ACT.Copy).then_inc(nhi_done, 1)

            def hi_unit(g, par, i, u, first):
                n = g.n0 + (2 * i + par) * g.units + u
                s, r = g.slots[par][u], g.raw_slots[par][u]
                act.wait_ge(raw_landed[r], 16 * (first[r] + i * g.per[r] + g.turn[par][u]) + 16)
                act.wait_ge(mm_used, n - g.lag + 1)
                nc.scalar.activation(whi[:, s, :], raw[:, r, :], ACT.Copy).then_inc(hi_done, 1)

            def split(g, par, i):
                if isinstance(i, int) and (par, i) == (0, 0):
                    g.first = list(uses)
                    for r in range(RAW):
                        uses[r] += g.pairs // 2 * g.per[r]
                for u in range(g.units):
                    hi_unit(g, par, i, u, g.first)

            def gemm(g, evacuate, then=None):
                last = g.pairs // 2 - 1

                def turn(i):
                    split(g, 1, i)
                    evacuate(0, i)
                    split(g, 0, i + 1)
                    evacuate(1, i)

                turn(0)
                if last > 1:
                    with nc.scalar.Fori(1, last) as i:
                        turn(i)
                split(g, 1, last)
                evacuate(0, last)
                if then:
                    split(then, 0, 0)
                evacuate(1, last)

            act.wait_ge(hT_ready, 4)
            squares(hT, KD // 4, 0)
            root(NORM1, D, KD // 4)

            def ada_evacuate(b, bank, row):
                act.wait_ge(ada_used, (b + 1) * AU)
                wait(act, ada_cols, b - 1)
                nc.scalar.activation(ada_rows[:, row, :], psX[:, bank, :], ACT.Copy
                                     ).then_inc(ada_out, 1)

            for b in range(SHIFT_SCALE1):
                ada_evacuate(b, b % 2, b % 2)
                if b % 2 and b >= 3:
                    gr = b // 2 - 1
                    act.wait_ge(mod_ready, gr + 1)
                    gains_and_hi(gr, gr, 0, lambda j: gains[:, 0, j:j + 1], lambda j: mod[:, j:j + 1])
                if b == SHIFT_SCALE1 - 2:
                    for a, (bm, cm) in enumerate(((ssm_b_re, ssm_c_re), (ssm_b_im, ssm_c_im))):
                        act.dma_start(b_raw[:, a, :, :],
                                      bm.rearrange("l (j g) p h -> (g p) (l j) h", g=2)
                                      ).then_inc(bc_landed, 16)
                        for twice in range(2):
                            act.dma_start(c_twice[:, a, :, twice, :],
                                          cm.rearrange("l (q g) h p -> (g h) (l q) p", g=8)
                                          ).then_inc(bc_landed, 16)
                    act.wait_ge(wf_zero, 1)
                    act.dma_start(wf[:, :, 0:NH],
                                  w_in[:, 3 * AW:3 * AW + NH].rearrange("(k p) h -> p k h", p=P)
                                  ).then_inc(wf_landed, 16)
            for r in range(RAW):
                uses[r] += SHIFT_SCALE1 * AU // RAW

            def window_hi(t):
                r = 3 * t % RAW
                act.wait_ge(raw_landed[r], 16 * (uses[r] + 3 * t // RAW) + 16)
                wait(act, mm_used, t - SPL + 1)
                nc.scalar.activation(whi[:, t % SPL, :], raw[:, r, :], ACT.Copy).then_inc(hi_done, 1)

            window_hi(0)
            gr = BS - 1
            act.wait_ge(mod_ready, gr + 1)
            gains_and_hi(gr, gr, 0, lambda j: gains[:, 0, j:j + 1], lambda j: mod[:, j:j + 1])

            def attention_act(h, part):
                b = h % 2
                if part == 0:
                    act.wait_ge(vN_done, h + 1)
                    nc.scalar.activation(vN[:, :, h * HD:h * HD + HD],
                                         psX[:, 1, 0:T].rearrange("p (t n) -> p t n", t=TT), ACT.Copy
                                         ).then_inc(vN_ready, 1)
                elif part == 1:
                    act.wait_ge(max_ready, h + 1)
                    for tt, cols in ((0, slice(0, P)), (1, slice(P, 3 * P))):
                        nc.scalar.activation(prob[:, b, cols], prob[:, b, cols], ACT.Exp,
                                             bias=ncol[:, b, 2 + tt:3 + tt],
                                             accum_out=ncol[:, b, 4 + tt:5 + tt]).then_inc(exp_done, 1)
                elif part == 3:
                    act.wait_ge(probT_done, h + 1)
                    wait(act, pv_done, h - 1)
                    nc.scalar.activation(probT[:, b, :], psX[:, 1, 0:3 * P], ACT.Copy
                                         ).then_inc(probT_ready, 1)

            for t in range(STEPS):
                if t + 1 < STEPS:
                    window_hi(t + 1)
                if t % 4 == 3:
                    scale = SCALE if window_pair(t // 4)[0] == "q" else 1.0
                    for m in range(2):
                        if m == 0:
                            act.wait_ge(tile_done, t // 4 + 1)
                        else:
                            act.wait_ge(mm_used, t + 1)
                        nc.scalar.activation(halves[:, 0, m, :], psG[:, m, T:2 * T], ACT.Copy,
                                             scale=scale).then_inc(tile_half, 1)
                if t == 4:
                    act.wait_ge(f_done, 1)
                    nc.scalar.activation(rb[:], psX[:, 1, 0:T], ACT.Copy).then_inc(f_rows, 1)
                if t == 6:
                    act.wait_ge(f_abs, 1)
                    link(nc.scalar.activation(fw[:, 1, :], fw[:, 1, :], ACT.Exp, scale=-1.0))
                    nc.scalar.activation(fw[:, 1, :], fw[:, 1, :], ACT.Ln, bias=ones[0:NH, 0:1]
                                         ).then_inc(f_ln, 1)
                qn = ssm_piece(t)
                if qn and qn[1] == 1 and qn[0] >= 1:
                    q = qn[0] - 1
                    act.wait_ge(y_ready, q + 1)
                    nc.scalar.activation(uT[:, q, :], uT[:, q, :], ACT.Gelu_apprx_tanh
                                         ).then_inc(gelu_done, 1)
                for h, part in attention_step(t):
                    attention_act(h, part)
                if t % 4 == 3:
                    ada_evacuate(SHIFT_SCALE1 + t // 4, 0, (t // 4) % 2)
            for r in range(RAW):
                uses[r] += 3 * STEPS // RAW

            for gr in range(2):
                act.wait_ge(gelu_done, KS)
                act.wait_ge(mm_used, STEPS)
                nc.scalar.activation(AA[:, KS + 4 * gr:KS + 4 * gr + 4, 0:T],
                                     uT[:, 4 * gr:4 * gr + 4, :], ACT.Copy).then_inc(glu_hi, 1)
            def pair_done(g, par, i):
                act.wait_ge(mm_used, g.n0 + (2 * i + par + 1) * g.units)

            def take_lo(g):
                def evacuate(par, i):
                    pair_done(g, par, i)
                    nc.scalar.activation(halves[:, par, :, :], psG[:, 2 * par:2 * par + 2, T:2 * T],
                                         ACT.Copy).then_inc(lo_half_out, 1)
                return evacuate

            def evacuate_glu(par, i):
                take_lo(g_glu)(par, i)
                act.wait_ge(z_ready, 2 * i + par + 1)
                for m in range(2):
                    at = V_BGLU + 4 * i + 2 * par + m
                    nc.scalar.activation(halves[:, par, m, :], halves[:, par, m, :], ACT.Sigmoid,
                                         bias=vec[:, at:at + 1]).then_inc(sig_done, 1)

            for t in range(STEPS, STEPS + 10):
                for h, part in attention_step(t):
                    attention_act(h, part)
                if (t - STEPS) % 2 == 0:
                    p = (t - STEPS) // 2
                    if p < 4:
                        split(g_glu, p % 2, p // 2)
                    if 1 <= p:
                        evacuate_glu((p - 1) % 2, (p - 1) // 2)

            act.wait_ge(o_ready, NH)
            squares(qT, 2, 0)
            split(g_out, 0, 0)
            root(NORMA, AW, NORMA[1] + 2)
            for gr in range(2):
                gains_and_hi(NORMA[1] + gr, gr, 0, lambda j: vec[:, V_GATTN + j:V_GATTN + j + 1], None)
            act.wait_ge(pair_out, g_glu.p1)
            act.wait_ge(nhi_done, NORMA[1] + 2)
            act.wait_ge(act_ready, NORMA[1] + 2)
            squares(uT, 2, 0)
            root(NORMS, SW, NORMS[1] + 2)
            for gr in range(2):
                gains_and_hi(NORMS[1] + gr, gr, KS, lambda j: vec[:, V_GSSM + j:V_GSSM + j + 1], None)

            def take_gated(g, gate_col):
                def evacuate(par, i):
                    pair_done(g, par, i)
                    for m in range(2):
                        nc.scalar.activation(
                            halves[:, par, m, :], psG[:, 2 * par + m, T:2 * T], ACT.Copy,
                            scale=mod[:, bass.ds(gate_col + 4 * i + 2 * par + m, 1)]
                        ).then_inc(lo_half_out, 1)
                return evacuate

            def square_pair(par, i):
                p = 2 * i + par
                act.wait_ge(pair_out, g_out.p0 + p + 1)
                act.wait_ge(ss_used, NORM2[1] + p)
                nc.scalar.activation(sq[:], hT[:, bass.ds(2 * p, 2), :], ACT.Square
                                     ).then_inc(sq_done, 1)

            def evacuate_out(par, i):
                take_gated(g_out, 2 * KD)(par, i)
                if par:
                    square_pair(0, i)
                elif not (isinstance(i, int) and i == 0):
                    square_pair(1, i - 1)

            act.wait_ge(mod_ready, BS + 1)
            gemm(g_out, evacuate_out, g_up)
            square_pair(1, g_out.pairs // 2 - 1)
            root(NORM2, D, NORM2[1] + g_out.pairs)
            for gr in range(KD // 4):
                gains_and_hi(NORM2[1] + gr, gr, 0, lambda j: gains[:, 1, j:j + 1],
                             lambda j: mod[:, 3 * KD + j:3 * KD + j + 1])

            def evacuate_up(par, i):
                take_lo(g_up)(par, i)
                if par == 0:
                    act.wait_ge(conv_done, i + 1)
                    nc.scalar.activation(gate[:], gate[:], ACT.Silu).then_inc(silu_done, 1)
                else:
                    act.wait_ge(gated_ready, i + 1)
                    nc.scalar.activation(GG[:, bass.ds(2 * i, 2), 0:T], gated[:], ACT.Copy
                                         ).then_inc(ghi_done, 1)

            gemm(g_up, evacuate_up, g_down)
            act.wait_ge(mm_used, g_up.n1)
            act.dma_start(g_rows[:], g_final.rearrange("(l d) -> l d", l=1).to_broadcast([P, D])
                          ).then_inc(g_rows_landed, 16)

            def tail_copy(pair, par):
                act.wait_ge(tail_T, pair + 1)
                nc.scalar.activation(out_n[:, :, bass.ds(pair * UN, UN)],
                                     psX[:, par, :].rearrange("p (t n) -> p t n", t=TT), ACT.Copy
                                     ).then_inc(tail_out, 1)

            def evacuate_down(par, i):
                take_gated(g_down, 5 * KD)(par, i)
                if par:
                    tail_copy(2 * i, 0)
                elif not (isinstance(i, int) and i == 0):
                    tail_copy(2 * i - 1, 1)

            gemm(g_down, evacuate_down)
            tail_copy(g_down.pairs - 1, 1)
            act.wait_ge(tail_out, g_down.pairs)
            for tt in range(TT):
                nc.scalar.activation(raw[:, 2 * tt:2 * tt + 2, :].rearrange("p s n -> p (s n)"),
                                     out_n[:, tt, :], ACT.Square, accum_out=tiny[:, tt:tt + 1]
                                     ).then_inc(act_chain, 1)
                link.n += 1
            act.wait_ge(act_chain, link.start + link.n)
            nc.scalar.activation(tiny[:, 2:4], tiny[:, 0:2], ACT.Sqrt, scale=1.0 / D,
                                 bias=ncol[:, 0, 7:8]).then_inc(root2_done, 1)
            ov = out.rearrange("b (t p) d -> p (b t) d", p=P)
            for tt in range(TT):
                act.wait_ge(final_ready, tt + 1)
                act.dma_start(ov[:, tt, :], out_n[:, tt, :]).then_inc(out_stored, 16)

        @block.vector
        def _(dve):
            link = Chain(dve, dve_chain)
            V = nc.vector
            V.memset(stage[:], 0.0).then_inc(stage_ready, 1)
            V.memset(ncol[:, 0, 7:8], EPS).then_inc(cond_ready, 1)
            V.memset(cond[:], 0.0).then_inc(cond_ready, 1)
            dve.wait_ge(pool_chain, 2)
            link(V.tensor_copy(sel[:], ident[:, 0:NH]))
            for g in range(1, 4):
                link(V.tensor_tensor(sel[:], sel[:], ident[:, 32 * g:32 * g + NH], ALU.add))

            dve.wait_ge(stage_landed, 16 * STAGE_DMAS)
            r = V_LOGDT % P
            for g in range(2):
                V.tensor_copy(stage[r:r + NJ, 3, NS * g:NS * g + NS],
                              tiny[r:r + NJ, KD + g:KD + g + 1].to_broadcast([NJ, NS])).then_inc(stage_ready, 1)
            dve.wait_ge(vecT_done, 1)
            V.tensor_copy(vec[:], psX[:, 0, :]).then_inc(vec_ready, 1)
            dve.wait_ge(cond_act, 1)
            V.tensor_copy(cond[:, :, 0:1], tiny[:, 0:KD].unsqueeze(2)).then_inc(cond_ready, 1)
            for r in (0, 2):
                dve.wait_ge(xT_done, r + 1)
                V.tensor_copy(hT[:, 4 * r:4 * r + 4, :].rearrange("p (b j) t -> p b (j t)", j=2),
                              psG[:, 0:2, :]).then_inc(hT_ready, 1)

            d = lambda n: disc[:, n, :]
            are, aim = vec[:, V_ARE:V_ARE + NJ], vec[:, V_AIM:V_AIM + NJ]
            dve.wait_ge(act_setup, 1)
            link(V.tensor_tensor(d(1), d(0), are, ALU.mult))
            V.tensor_tensor(d(2), d(0), aim, ALU.mult).then_inc(dve_setup, 1)
            dve.wait_ge(dve_setup, 1)
            dve.wait_ge(consts_ready, 2)
            link(V.tensor_copy(iota_f[:], iota_i[:]))

            def turns(r, big, k):
                link(V.tensor_scalar(k, big, float(1 / TWO_PI), MAGIC, ALU.mult, ALU.add))
                link(V.tensor_scalar(k, k, -MAGIC, None, ALU.add))
                link(V.scalar_tensor_tensor(r, k, -C1, big, ALU.mult, ALU.add))
                link(V.scalar_tensor_tensor(r, k, -C2, r, ALU.mult, ALU.add))
                link(V.scalar_tensor_tensor(r, k, -C3, r, ALU.mult, ALU.add))

            s16 = iota_f[:].unsqueeze(1).to_broadcast([P, NJ, 16])
            p_ = lambda n: ph[:, n, :, :]
            for half in range(2):
                if half:
                    link(V.tensor_scalar(d(2), d(4), 16.0, None, ALU.mult))
                turns(d(4), d(2), d(5))
                link(V.tensor_copy(d(6).bitcast(F32R), d(4)))
                link(V.tensor_tensor(d(7), d(4), d(6), ALU.subtract))
                th, tl = (d(n).unsqueeze(2).to_broadcast([P, NJ, 16]) for n in (6, 7))
                if half:
                    dve.wait_ge(act_setup, 4)
                link(V.tensor_tensor(p_(0), s16, th, ALU.mult))
                turns(p_(1), p_(0), p_(2))
                link(V.tensor_tensor(p_(2), s16, tl, ALU.mult))
                link(V.tensor_tensor(p_(1), p_(1), p_(2), ALU.add))
                link(V.tensor_scalar(p_(3), p_(1), float(np.pi / 2), float(-TWO_PI), ALU.is_gt, ALU.mult))
                link(V.scalar_tensor_tensor(p_(3), p_(1), float(np.pi / 2), p_(3), ALU.add, ALU.add))
                link(V.tensor_scalar(p_(1), p_(1), PI_IN, -PI_IN, ALU.min, ALU.max))
                V.tensor_scalar(p_(3), p_(3), PI_IN, -PI_IN, ALU.min, ALU.max).then_inc(dve_setup, 1)
                dve.wait_ge(dve_setup, 2 + half)
            dve.wait_ge(act_setup, 6)
            c1, s1 = fac[:, 0, :, 1:2].rearrange("p j o -> p (j o)"), fac[:, 1, :, 1:2].rearrange("p j o -> p (j o)")
            link(V.tensor_tensor(d(4), d(3), c1, ALU.mult))
            link(V.tensor_scalar(d(4), d(4), -1.0, None, ALU.add))
            link(V.tensor_tensor(d(5), d(3), s1, ALU.mult))
            link(V.tensor_tensor(d(6), are, are, ALU.mult))
            link(V.tensor_tensor(d(7), aim, aim, ALU.mult))
            link(V.tensor_tensor(d(6), d(6), d(7), ALU.add))
            link(V.reciprocal(d(6), d(6)))
            link(V.tensor_tensor(d(7), d(4), are, ALU.mult))
            link(V.tensor_tensor(d(8), d(5), aim, ALU.mult))
            link(V.tensor_tensor(d(7), d(7), d(8), ALU.add))
            link(V.tensor_tensor(d(9), d(7), d(6), ALU.mult))
            link(V.tensor_tensor(d(7), d(5), are, ALU.mult))
            link(V.tensor_tensor(d(8), d(4), aim, ALU.mult))
            link(V.tensor_tensor(d(7), d(7), d(8), ALU.subtract))
            link(V.tensor_tensor(d(10), d(7), d(6), ALU.mult))
            def prepare_b():
              dve.wait_ge(bc_landed, 16 * BC_DMAS)
              zr, zi = (d(n).unsqueeze(2).to_broadcast([P, NJ, GH]) for n in (9, 10))
              br, bi = b_raw[:, 0, :, :], b_raw[:, 1, :, :]
              link(V.tensor_tensor(b_tmp[:], zi, bi, ALU.mult))
              link(V.tensor_tensor(b_bar[:, 0, :, :], zr, br, ALU.mult))
              link(V.tensor_tensor(b_bar[:, 0, :, :], b_bar[:, 0, :, :], b_tmp[:], ALU.subtract))
              link(V.tensor_tensor(b_tmp[:], zi, br, ALU.mult))
              link(V.tensor_tensor(b_bar[:, 1, :, :], zr, bi, ALU.mult))
              link(V.tensor_tensor(b_bar[:, 1, :, :], b_bar[:, 1, :, :], b_tmp[:], ALU.add))
              V.memset(ctr[:], 0.0).then_inc(bc_ready, 1)
              V.memset(cti[:], 0.0).then_inc(bc_ready, 1)
              link(V.memset(b_wide[:], 0.0))
              for g in range(2):
                  half = slice(NS * g, NS * g + NS)
                  V.tensor_copy(b_wide[half, :, :, g, :].rearrange("p a j h -> p (a j) h"),
                                b_bar[half, :, :, :].rearrange("p a j h -> p (a j) h")
                                ).then_inc(bc_ready, 1)

            def take_matrix(r):
                dve.wait_ge(bcT_done, r + 1)
                if r < 2:
                    V.tensor_copy((btr, bti)[r][:].rearrange("p (b q) n -> p b (q n)", b=2),
                                  psG[:, 2:4, :]).then_inc(bcT_ready, 1)
                    return
                dst, sign = ((ctr, 1.0), (cti, -1.0))[r - 2]
                for g in range(2):
                    half = slice(NS * g, NS * g + NS)
                    ins = V.tensor_scalar(
                        dst[half, :, :].rearrange("p q (r g h) -> p (q r) g h", g=2, h=GH)[:, :, g, :],
                        psG[half, 2:4, :].rearrange("p b (q g h) -> p (b q) g h", g=2, h=GH)[:, :, g, :],
                        sign, None, ALU.mult)
                    if g == 0:
                        link(ins)
                    else:
                        ins.then_inc(bcT_ready, 1)

            def recip(which):
                index, _ = which
                dve.wait_ge(root_done, index + 1)
                V.reciprocal(rb[:], rb[:]).then_inc(rms_ready, 1)
                dve.wait_ge(rms_ready, index + 1)

            def over_rms(src, gr):
                V.tensor_tensor(xr[:, 4 * gr:4 * gr + 4, :], src[:, 4 * gr:4 * gr + 4, :],
                                rb[:].unsqueeze(1).to_broadcast([P, 4, T]), ALU.mult
                                ).then_inc(nt_ready, 1)

            def low(group, gr, k0):
                dve.wait_ge(nhi_done, group + 1)
                k = slice(k0 + 4 * gr, k0 + 4 * gr + 4)
                V.tensor_tensor(AA[:, k, T:2 * T], xr[:, 4 * gr:4 * gr + 4, :],
                                AA[:, k, 0:T].bitcast(F32), ALU.subtract).then_inc(act_ready, 1)

            def lo_unit(g, par, i, u):
                n = g.n0 + (2 * i + par) * g.units + u
                s, r = g.slots[par][u], g.raw_slots[par][u]
                dve.wait_ge(hi_done, n + 1)
                dve.wait_ge(mm_used, n - g.lag + 1)
                V.tensor_tensor(wlo[:, s, :], raw[:, r, :], whi[:, s, :].bitcast(F32), ALU.subtract
                                ).then_inc(lo_done, 1)

            def split(g, par, i):
                for u in range(g.units):
                    lo_unit(g, par, i, u)

            def gemm(g, evacuate, links=0, then=None):
                last = g.pairs // 2 - 1

                def turn(i):
                    split(g, 1, i)
                    evacuate(0, i)
                    split(g, 0, i + 1)
                    evacuate(1, i)

                turn(0)
                if last > 1:
                    with nc.vector.Fori(1, last) as i:
                        link.loop(i - 1, links)
                        turn(i)
                    link.after(last - 1)
                split(g, 1, last)
                evacuate(0, last)
                if then:
                    split(then, 0, 0)
                evacuate(1, last)

            half_count = [0]

            recip(NORM1)
            for gr in range(KD // 4):
                over_rms(hT, gr)

            def window_lo(t):
                dve.wait_ge(hi_done, t + 1)
                wait(dve, mm_used, t - SPL + 1)
                V.tensor_tensor(wlo[:, t % SPL, :], raw[:, 3 * t % RAW, :],
                                whi[:, t % SPL, :].bitcast(F32), ALU.subtract).then_inc(lo_done, 1)

            two = lambda ap: ap.rearrange("p (a j) -> p a j", a=2)
            for gr in range(BS):
                dve.wait_ge(ada_cols, 2 * gr + 2)
                js = slice(BC * gr, BC * gr + BC)
                link(V.tensor_tensor(two(mod[:, 0:2 * KD])[:, :, js],
                                     two(psX[:, 2, M_AT:M_AT + 2 * KD])[:, :, js],
                                     two(vec[:, V_BADA:V_BADA + 2 * KD])[:, :, js], ALU.add))
                V.scalar_tensor_tensor(gains[:, 0, js], mod[:, KD + BC * gr:KD + BC * gr + BC], 1.0,
                                       vec[:, V_GMIX + BC * gr:V_GMIX + BC * gr + BC], ALU.add, ALU.mult
                                       ).then_inc(mod_ready, 1)
                if gr >= 1:
                    low(gr - 1, gr - 1, 0)
            window_lo(0)
            low(BS - 1, BS - 1, 0)

            def gate_logits():
                dve.wait_ge(f_sum, 1)
                dve.wait_ge(wf_landed, 32)
                link(V.tensor_scalar(fw[:, 0, :], psX[0:NH, 1, 0:T], bf[:, 0:1], None, ALU.add))
                link(V.tensor_scalar(fw[:, 2, :], fw[:, 0, :], -1.0, None, ALU.mult))
                V.tensor_tensor(fw[:, 1, :], fw[:, 0, :], fw[:, 2, :], ALU.max).then_inc(f_abs, 1)
                dve.wait_ge(f_abs, 1)

            def gate_sums():
                link(V.tensor_scalar(fw[:, 2, :], fw[:, 0, :], 0.0, None, ALU.min))
                dve.wait_ge(f_ln, 1)
                link(V.tensor_tensor(fw[:, 2, :], fw[:, 2, :], fw[:, 1, :], ALU.subtract))
                link(V.tensor_tensor_scan(cum[:], ones[0:NH, :], fw[:, 2, :], 0.0, ALU.mult, ALU.add))

            link(V.tensor_tensor_scan(mask[:, 0:P], ones[:, 0:P], ident[:], 0.0, ALU.mult, ALU.add))
            link(V.tensor_tensor(mask[:, 0:P], mask[:, 0:P], ident[:], ALU.subtract))
            link(V.tensor_scalar(mask[:, 2 * P:3 * P], mask[:, 0:P], MASKED, None, ALU.mult))
            link(V.memset(mask[:, P:2 * P], 0.0))
            link(V.tensor_copy(mask[:, 0:P], mask[:, 2 * P:3 * P]))

            def select_gates(h):
                wait(dve, score_done, h - 1)
                pick = ident[0:NH, h:h + 1]
                link(V.tensor_scalar(csel[:, h % 2, 0, :], cum[:], pick, None, ALU.mult))
                V.tensor_scalar(csel[:, h % 2, 1, :], cum[:], pick, -1.0, ALU.mult, ALU.mult
                                ).then_inc(csel_ready, 1)

            def maxima(h):
                b = h % 2
                dve.wait_ge(score_done, h + 1)
                wait(dve, probT_done, h - 1)
                V.tensor_tensor(prob[:, b, :], psX[:, 1, 0:3 * P], mask[:], ALU.add).then_inc(masked, 1)
                dve.wait_ge(masked, h + 1)
                link(V.tensor_reduce(ncol[:, b, 0:1], prob[:, b, 0:P], AX_X, ALU.max))
                link(V.tensor_reduce(ncol[:, b, 1:2], prob[:, b, P:3 * P], AX_X, ALU.max))
                V.tensor_scalar(ncol[:, b, 2:4], ncol[:, b, 0:2], -1.0, None, ALU.mult
                                ).then_inc(max_ready, 1)

            def normalise(h):
                b = h % 2
                dve.wait_ge(exp_done, 2 * h + 2)
                link(V.reciprocal(ncol[:, b, 0:2], ncol[:, b, 4:6]))
                link(V.tensor_scalar(prob[:, b, 0:P], prob[:, b, 0:P], ncol[:, b, 0:1], None, ALU.mult))
                V.tensor_scalar(prob[:, b, P:3 * P], prob[:, b, P:3 * P], ncol[:, b, 1:2], None,
                                ALU.mult).then_inc(prob_ready, 1)

            def take_o(h):
                dve.wait_ge(pv_done, h + 1)
                V.tensor_copy(qT[:, h, :], psX[:, 2, 0:T]).then_inc(o_ready, 1)

            def attention_dve(h, part):
                if part == 0:
                    select_gates(h)
                elif part == 1:
                    maxima(h)
                elif part == 2:
                    normalise(h)
                elif part == 4:
                    take_o(h)

            def ssm_dve(q, piece):
                if q < KS:
                    zre, zim, p0, p1 = (ssm_w[:, (n + 2 * (q % 2)) % 4, :, :] for n in range(4))
                    ct, st = tab[:, q % 2, 0, :, :], tab[:, q % 2, 1, :, :]
                if q < KS and piece in (0, 2):
                    half = piece // 2
                    rs = slice(2 * half, 2 * half + 2)
                    if piece == 0:
                        dve.wait_ge(tab_ready, q + 1)
                        wait(dve, y_part, 2 * q - 1)
                    ere, eim = psG[:, 2:4, 0:T], psG[:, 2:4, T:2 * T]
                    dve.wait_ge(e_done, 2 * q + half + 1)
                    link(V.tensor_tensor(zre[:, rs, :], ct[:, rs, :], ere, ALU.mult))
                    link(V.tensor_tensor(rot_t[:], st[:, rs, :], eim, ALU.mult))
                    link(V.tensor_tensor(zre[:, rs, :], zre[:, rs, :], rot_t[:], ALU.add))
                    link(V.tensor_tensor(zim[:, rs, :], ct[:, rs, :], eim, ALU.mult))
                    V.tensor_tensor(rot_t[:], st[:, rs, :], ere, ALU.mult).then_inc(rotated, 1)
                    dve.wait_ge(rotated, 2 * q + half + 1)
                    link(V.tensor_tensor(zim[:, rs, :], zim[:, rs, :], rot_t[:], ALU.subtract))
                if q < KS and piece in (1, 3):
                    for z in (zre, zim):
                        for r in (piece - 1, piece):
                            j = JQ * q + r
                            link(V.tensor_tensor_scan(z[:, r, :], d(3)[:, j:j + 1].to_broadcast([P, T]),
                                                      z[:, r, :], 0.0, ALU.mult, ALU.add))
                if q < KS and piece == 3:
                    wait(dve, y_part, 2 * q)
                    link(V.tensor_tensor(p0, ct, zre, ALU.mult))
                if q < KS and piece == 4:
                    V.scalar_tensor_tensor(p1, st, -1.0, zim, ALU.mult, ALU.mult).then_inc(z_part, 1)
                    dve.wait_ge(z_part, 2 * q + 1)
                    link(V.tensor_tensor(zre, st, zre, ALU.mult))
                if q < KS and piece == 5:
                    V.tensor_tensor(zim, ct, zim, ALU.mult).then_inc(z_part, 1)
                if q >= 1 and piece == 1:
                    q1 = q - 1
                    dve.wait_ge(y_part, 2 * q1 + 2)
                    V.scalar_tensor_tensor(uT[:, q1, :], uT[:, q1, :], vec[:, V_D + q1:V_D + q1 + 1],
                                           psX[:, 3, 0:T], ALU.mult, ALU.add).then_inc(y_ready, 1)

            for t in range(STEPS):
                if t + 1 < STEPS:
                    window_lo(t + 1)
                if t % 4 == 3:
                    p = t // 4
                    kind, j = window_pair(p)
                    dst = {"u": uT, "q": qT, "k": kT, "v": vT}[kind]
                    if kind == "v" and j >= 1:
                        dve.wait_ge(vN_done, 2 * j)
                    for m in range(2):
                        dve.wait_ge(tile_half, 2 * p + m + 1)
                        V.scalar_tensor_tensor(dst[:, m if kind == "v" else 2 * j + m, :],
                                               psG[:, m, 0:T], SCALE if kind == "q" else 1.0,
                                               halves[:, 0, m, :], ALU.mult, ALU.add
                                               ).then_inc(tile_out, 1)
                if t == 0:
                    prepare_b()
                if t in (1, 3, 5, 7):
                    take_matrix(t // 2)
                if t == 5:
                    gate_logits()
                if t == 7:
                    gate_sums()
                if ssm_piece(t):
                    ssm_dve(*ssm_piece(t))
                for h, part in attention_step(t):
                    attention_dve(h, part)

            for gr in range(2):
                dve.wait_ge(glu_hi, gr + 1)
                k = slice(KS + 4 * gr, KS + 4 * gr + 4)
                V.tensor_tensor(AA[:, k, T:2 * T], uT[:, 4 * gr:4 * gr + 4, :],
                                AA[:, k, 0:T].bitcast(F32), ALU.subtract).then_inc(glu_act_ready, 1)

            def evacuate_glu(par, i):
                dve.wait_ge(lo_half_out, 2 * i + par + 1)
                V.tensor_tensor(halves[:, par, :, :], psG[:, 2 * par:2 * par + 2, 0:T],
                                halves[:, par, :, :], ALU.add).then_inc(z_ready, 1)
                dve.wait_ge(sig_done, 4 * i + 2 * par + 2)
                y = uT[:, 4 * i + 2 * par:4 * i + 2 * par + 2, :]
                V.tensor_tensor(y, y, halves[:, par, :, :], ALU.mult).then_inc(pair_out, 1)

            for t in range(STEPS, STEPS + 10):
                for h, part in attention_step(t):
                    attention_dve(h, part)
                if (t - STEPS) % 2 == 0:
                    p = (t - STEPS) // 2
                    if p < 4:
                        split(g_glu, p % 2, p // 2)
                    if 1 <= p:
                        evacuate_glu((p - 1) % 2, (p - 1) // 2)

            dve.wait_ge(ada_cols, ADA_BLOCKS)
            link(V.tensor_tensor(mod[:, 2 * KD:6 * KD], psX[:, 2, M_AT + 2 * KD:M_AT + 6 * KD],
                                 vec[:, V_BADA + 2 * KD:V_BADA + 6 * KD], ALU.add))
            V.scalar_tensor_tensor(gains[:, 1, :], mod[:, 4 * KD:5 * KD], 1.0,
                                   vec[:, V_GFFN:V_GFFN + KD], ALU.add, ALU.mult).then_inc(mod_ready, 1)
            split(g_out, 0, 0)
            for which, src, k0 in ((NORMA, qT, 0), (NORMS, uT, KS)):
                recip(which)
                for gr in range(2):
                    over_rms(src, gr)
                for gr in range(2):
                    low(which[1] + gr, gr, k0)
            half_count[0] += g_glu.pairs

            def add_gated(g, gate_col, into):
                n0 = half_count[0]

                def evacuate(par, i):
                    dve.wait_ge(lo_half_out, n0 + 4 * i + 2 * par + 2)
                    for m in range(2):
                        link(V.scalar_tensor_tensor(
                            halves[:, par, m, :], psG[:, 2 * par + m, 0:T],
                            mod[:, bass.ds(gate_col + 4 * i + 2 * par + m, 1)], halves[:, par, m, :],
                            ALU.mult, ALU.add))
                    h2 = hT[:, bass.ds(4 * i + 2 * par, 2), :]
                    V.tensor_tensor(h2 if into is None else into(par), h2, halves[:, par, :, :], ALU.add
                                    ).then_inc(pair_out, 1)

                half_count[0] += 2 * g.pairs
                return evacuate

            gemm(g_out, add_gated(g_out, 2 * KD, None), 4, g_up)
            recip(NORM2)
            for gr in range(KD // 4):
                over_rms(hT, gr)
                if gr:
                    low(NORM2[1] + gr - 1, gr - 1, 0)
            low(NORM2[1] + KD // 4 - 1, KD // 4 - 1, 0)

            link(V.memset(conv_in[:, :, 0:2], 0.0))
            n_up = half_count[0]
            half_count[0] += g_up.pairs

            def evacuate_up(par, i):
                dve.wait_ge(lo_half_out, n_up + 2 * i + par + 1)
                hi, lo = psG[:, 2 * par:2 * par + 2, 0:T], halves[:, par, :, :]
                if par == 0:
                    V.tensor_tensor(conv_in[:, :, 2:T + 2], hi, lo, ALU.add).then_inc(pair_out, 1)
                    dve.wait_ge(pair_out, g_up.p0 + 2 * i + 1)

                    def col(at, m):
                        return vec[:, bass.ds(at + 2 * i + m, 1)]

                    for m in range(2):
                        link(V.tensor_scalar(gate[:, m, :], conv_in[:, m, 2:T + 2], col(V_CONV2, m),
                                             col(V_CONVB, m), ALU.mult, ALU.add))
                    for m in range(2):
                        link(V.scalar_tensor_tensor(gate[:, m, :], conv_in[:, m, 1:T + 1],
                                                    col(V_CONV1, m), gate[:, m, :], ALU.mult, ALU.add))
                    link(V.scalar_tensor_tensor(gate[:, 0, :], conv_in[:, 0, 0:T], col(V_CONV0, 0),
                                                gate[:, 0, :], ALU.mult, ALU.add))
                    V.scalar_tensor_tensor(gate[:, 1, :], conv_in[:, 1, 0:T], col(V_CONV0, 1),
                                           gate[:, 1, :], ALU.mult, ALU.add).then_inc(conv_done, 1)
                    dve.wait_ge(conv_done, i + 1)
                else:
                    V.tensor_tensor(branch[:], hi, lo, ALU.add).then_inc(pair_out, 1)
                    dve.wait_ge(pair_out, g_up.p0 + 2 * i + 2)
                    dve.wait_ge(silu_done, i + 1)
                    V.tensor_tensor(gated[:], gate[:], branch[:], ALU.mult).then_inc(gated_ready, 1)
                    dve.wait_ge(ghi_done, i + 1)
                    V.tensor_tensor(GG[:, bass.ds(2 * i, 2), T:2 * T], gated[:],
                                    GG[:, bass.ds(2 * i, 2), 0:T].bitcast(F32), ALU.subtract
                                    ).then_inc(g_ready, 1)

            gemm(g_up, evacuate_up, 5, g_down)

            gemm(g_down, add_gated(g_down, 5 * KD, lambda par: halves[:, par, :, :]), 4)

            dve.wait_ge(root2_done, 1)
            link(V.reciprocal(tiny[:, 2:4], tiny[:, 2:4]))
            dve.wait_ge(g_rows_landed, 16)
            for tt in range(TT):
                V.scalar_tensor_tensor(out_n[:, tt, :], out_n[:, tt, :], tiny[:, 2 + tt:3 + tt],
                                       g_rows[:], ALU.mult, ALU.mult).then_inc(final_ready, 1)

        @block.tensor
        def _(pe):
            M = nc.tensor.matmul
            pe.wait_ge(pool_chain, 2)
            pe.wait_ge(stage_ready, 3)
            for s in range(4):
                last = nc.tensor.transpose(psX[:, 0, P * s:P * s + P], stage[:, s, :], ident[:])
            last.then_inc(vecT_done, 1)
            pe.wait_ge(x_landed, 16 * TT)
            for r in range(4):
                wait(pe, hT_ready, r - 1)
                if r == 2:
                    pe.wait_ge(hT_ready, 2)
                if r == 3:
                    pe.wait_ge(hT_ready, 2)
                for j in range(4):
                    for tt in range(TT):
                        last = nc.tensor.transpose(
                            psG[:, 2 * (r % 2) + j // 2, (j % 2) * T + tt * P:(j % 2) * T + tt * P + P],
                            xn[:, tt, (4 * r + j) * P:(4 * r + j + 1) * P], ident[:])
                last.then_inc(xT_done, 1)

            def ada_unit(a, k_unit, bank, landed):
                s, value = landed
                pe.wait_ge(raw_landed[s], value)
                for f in range(AK):
                    k = AK * k_unit + f
                    g = k % 4
                    last = M(psX[32 * g:32 * g + 32, bank, :], cond[:, k, :],
                             raw[:, s, f * AN:(f + 1) * AN], start=(k < 4), stop=(k >= KD - 4),
                             tile_position=(0, 32 * g))
                last.then_inc(ada_used, 1)

            heads_out = [0]

            def ada_columns(b, column, row):
                pe.wait_ge(ada_out, b + 1)
                wait(pe, mod_ready, min(b // 2, BS))
                wait(pe, o_ready, heads_out[0])
                for m in range(BC):
                    last = M(psX[:, 2, M_AT + column + m:M_AT + column + m + 1],
                             ada_rows[:, row, m * P:m * P + P], ones[:, 0:1], start=True, stop=True)
                last.then_inc(ada_cols, 1)

            def sums(tiles, at, first=True, last=True):
                n = len(tiles)
                for j, tile in enumerate(tiles):
                    ins = M(psX[:, 3, 0:T], ones[:, 0:P], tile, start=(first and j == 0),
                            stop=(last and j == n - 1))
                ins.then_inc(ss_used, 1)

            def norm(which, groups):
                index, g0 = which
                wait(pe, root_done, index)
                for gr in range(groups):
                    pe.wait_ge(sq_done, g0 + gr + 1)
                    sums([xr[:, j, :] for j in range(4 * gr, 4 * gr + 4)], None, gr == 0,
                         gr == groups - 1)

            def pair(g, par, i, operand, ready):
                p = g.p0 + 2 * i + par
                wait(pe, pair_out, p - 1)
                for u in range(g.units):
                    s = g.slots[par][u]
                    pe.wait_ge(lo_done, g.n0 + (2 * i + par) * g.units + u + 1)
                    ready(UK * u + UK - 1)
                    for m in range(2):
                        for f in range(UK):
                            k = UK * u + f
                            at = f * UN + m * P
                            bank = 2 * par + m
                            M(psG[:, bank, :], whi[:, s, at:at + P], operand(k), start=(k == 0),
                              stop=False)
                            last = M(psG[:, bank, 0:T], wlo[:, s, at:at + P], operand(k)[:, 0:T],
                                     start=False, stop=(k == g.units * UK - 1))
                    last.then_inc(mm_used, 1)

            norm(NORM1, KD // 4)
            pe.wait_ge(cond_ready, 3)
            pe.wait_ge(consts_ready, 1)
            for b in range(SHIFT_SCALE1):
                wait(pe, ada_out, b - 1)
                for u in range(AU):
                    ada_unit(b, u, b % 2, (u % RAW, 16 * (b * (AU // RAW) + u // RAW) + 16))
                if b:
                    ada_columns(b - 1, (b - 1) % 2 * KD + (b - 1) // 2 * BC, (b - 1) % 2)
            b = SHIFT_SCALE1 - 1
            ada_columns(b, b % 2 * KD + b // 2 * BC, b % 2)

            from_aa = lambda k: AA[:, k, :]

            def window_unit(t):
                p, u, s = t // 4, t % 4, t % SPL
                pe.wait_ge(lo_done, t + 1)
                if p == 0:
                    pe.wait_ge(act_ready, u + 1)
                for m in range(2):
                    if u == 0:
                        wait(pe, tile_out, 2 * (p - 1) + m + 1)
                    for f in range(UK):
                        k, at = UK * u + f, f * UN + m * P
                        M(psG[:, m, :], whi[:, s, at:at + P], AA[:, k, :], start=(k == 0), stop=False)
                        last = M(psG[:, m, 0:T], wlo[:, s, at:at + P], AA[:, k, 0:T], start=False,
                                 stop=(k == KD - 1))
                    if u == 3 and m == 0:
                        last.then_inc(tile_done, 1)
                last.then_inc(mm_used, 1)

            def matrices(r):
                if r == 0:
                    pe.wait_ge(bc_ready, 4)
                wait(pe, bcT_ready, r)
                for q in range(KS):
                    src = (b_wide[:, r, JQ * q:JQ * q + JQ, :, :].rearrange("p j g h -> p (j g h)")
                           if r < 2 else c_twice[:, r - 2, q, :, :].rearrange("p g n -> p (g n)"))
                    last = nc.tensor.transpose(psG[:, 2 + q // 4, (q % 4) * P:(q % 4) * P + P], src,
                                               ident[:])
                last.then_inc(bcT_done, 1)

            def forget_gates():
                pe.wait_ge(wf_landed, 32)
                for k in range(KD):
                    g = k % 4
                    for a in range(2):
                        last = M(psX[32 * g:32 * g + 32, 1, 0:T], wf[:, k, :],
                                 AA[:, k, a * T:a * T + T].bitcast(F32), start=(k < 4 and a == 0),
                                 stop=(k >= KD - 4 and a == 1), tile_position=(0, 32 * g))
                last.then_inc(f_done, 1)

            def attention_pe(h, part):
                b = h % 2
                if part == 0:
                    g = h // 2
                    pe.wait_ge(tile_out, 2 * (3 * g + 7))
                    wait(pe, probT_ready, h)
                    for tt in range(TT):
                        last = nc.tensor.transpose(psX[:, 1, tt * P:tt * P + P],
                                                   vT[:, h % 2, tt * P:tt * P + P], ident[:])
                    last.then_inc(vN_done, 1)
                elif part == 1:
                    pe.wait_ge(csel_ready, h + 1)
                    pe.wait_ge(vN_ready, h + 1)
                    for tt, at, n in ((0, 0, P), (1, P, 2 * P)):
                        dst = psX[:, 1, at:at + n]
                        t = slice(tt * P, tt * P + P)
                        M(dst, qT[:, h, t], kT[:, h, 0:n], start=True, stop=False)
                        M(dst, csel[:, b, 0, t], ones[0:NH, 0:n], start=False, stop=False)
                        last = M(dst, ones[0:NH, 0:P], csel[:, b, 1, 0:n], start=False, stop=True)
                    last.then_inc(score_done, 1)
                elif part == 3:
                    pe.wait_ge(prob_ready, h + 1)
                    for n in range(3):
                        last = nc.tensor.transpose(psX[:, 1, n * P:n * P + P],
                                                   prob[:, b, n * P:n * P + P], ident[:])
                    last.then_inc(probT_done, 1)
                elif part == 4:
                    pe.wait_ge(probT_ready, h + 1)
                    wait(pe, o_ready, h)
                    v = lambda st: vN[:, st, h * HD:h * HD + HD]
                    M(psX[:, 2, 0:T], v(0), probT[:, b, 0:T], start=True, stop=False)
                    M(psX[:, 2, P:T], v(1), probT[:, b, T:T + P], start=False, stop=True
                      ).then_inc(pv_done, 1)
                    heads_out[0] = h + 1

            def inputs(q, half):
                if q == 0 and half == 0:
                    pe.wait_ge(bcT_ready, 4)
                    pe.wait_ge(tile_out, 2)
                if half == 0:
                    pe.wait_ge(tile_out, q + 1)
                wait(pe, rotated, 2 * q + half)
                for a, mat in enumerate((btr, bti)):
                    for r in (2 * half, 2 * half + 1):
                        rows = slice(32 * r, 32 * r + 32)
                        last = M(psG[:, 2 + r % 2, a * T:a * T + T], mat[rows, q, :], uT[rows, q, :],
                                 start=True, stop=True, tile_position=(32 * r, 0))
                last.then_inc(e_done, 1)

            def outputs(q):
                wait(pe, y_ready, q)
                for part, products in enumerate((((2, ctr), (3, ctr)), ((0, cti), (1, cti)))):
                    pe.wait_ge(z_part, 2 * q + part + 1)
                    for a, (n, mat) in enumerate(products):
                        for r in range(JQ):
                            cols = slice(32 * r, 32 * r + 32)
                            last = M(psX[cols, 3, 0:T], mat[:, q, cols],
                                     ssm_w[:, (n + 2 * (q % 2)) % 4, r, :],
                                     start=(part == 0 and a == 0), stop=(part == 1 and a == 1),
                                     tile_position=(0, 32 * r))
                    last.then_inc(y_part, 1)

            for t in range(STEPS):
                window_unit(t)
                for n in range(2):
                    a = 2 * t + n
                    b = SHIFT_SCALE1 + a // AU
                    if a % AU == 0:
                        pe.wait_ge(ada_out, b)
                    pos = 3 * t + 1 + n
                    ada_unit(b, a % AU, 0, (pos % RAW, 16 * (WINDOW_ADA // RAW + pos // RAW) + 16))
                if t % 4 == 0 and t:
                    b = SHIFT_SCALE1 + t // 4 - 1
                    ada_columns(b, b * BC, (t // 4 - 1) % 2)
                if t in (1, 3, 5, 7):
                    matrices(t // 2)
                if t == 4:
                    forget_gates()
                if t == 5:
                    pe.wait_ge(f_rows, 1)
                    M(psX[0:NH, 1, 0:T], sel[:], rb[:], start=True, stop=True).then_inc(f_sum, 1)
                qn = ssm_piece(t + 2)
                if qn and qn[0] < KS and qn[1] == 0:
                    inputs(qn[0], 0)
                qn = ssm_piece(t)
                if qn and qn[0] < KS and qn[1] == 1:
                    inputs(qn[0], 1)
                if qn and qn[0] >= 1 and qn[1] == 0:
                    outputs(qn[0] - 1)
                for h, part in attention_step(t):
                    attention_pe(h, part)
            b = ADA_BLOCKS - 1
            ada_columns(b, b * BC, (STEPS // 4 - 1) % 2)

            for t in range(STEPS, STEPS + 10):
                for h, part in attention_step(t):
                    attention_pe(h, part)
                p = (t - STEPS) // 2
                if (t - STEPS) % 2 == 0 and p < 4:
                    pair(g_glu, p % 2, p // 2, lambda k: AA[:, KS + k, :],
                         lambda k: pe.wait_ge(glu_act_ready, k // 4 + 1))
            norm(NORMA, 2)
            norm(NORMS, 2)

            ready_out = lambda k: pe.wait_ge(act_ready, NORMA[1] + k // 4 + 1)

            def sums_pair(p, first=False, last=False):
                pe.wait_ge(sq_done, NORM2[1] + p + 1)
                if first:
                    pe.wait_ge(root_done, NORM2[0])
                sums([sq[:, 0, :], sq[:, 1, :]], None, first, last)

            pair(g_out, 0, 0, from_aa, ready_out)
            pair(g_out, 1, 0, from_aa, ready_out)
            sums_pair(0, first=True)
            with nc.tensor.Fori(1, g_out.pairs // 2) as i:
                pair(g_out, 0, i, from_aa, ready_out)
                sums_pair(2 * i - 1)
                pair(g_out, 1, i, from_aa, ready_out)
                sums_pair(2 * i)
            sums_pair(g_out.pairs - 1, last=True)

            ready_up = lambda k: pe.wait_ge(act_ready, NORM2[1] + k // 4 + 1)
            with nc.tensor.Fori(0, g_up.pairs // 2) as i:
                for par in range(2):
                    pair(g_up, par, i, from_aa, ready_up)

            def down_pair(par, i):
                pair(g_down, par, i, lambda k: GG[:, k, :],
                     lambda k: pe.wait_ge(g_ready, (k + 1) // 2))

            def tail(p, par):
                pe.wait_ge(pair_out, g_down.p0 + p + 1)
                wait(pe, tail_out, p - 1)
                for tt in range(TT):
                    for m in range(2):
                        last = nc.tensor.transpose(psX[:, par, tt * T + m * P:tt * T + m * P + P],
                                                   halves[:, par, m, tt * P:tt * P + P], ident[:])
                last.then_inc(tail_T, 1)

            down_pair(0, 0)

            def down_round(i):
                down_pair(1, i)
                tail(2 * i, 0)
                down_pair(0, i + 1)
                tail(2 * i + 1, 1)

            down_round(0)
            with nc.tensor.Fori(1, g_down.pairs // 2 - 1) as i:
                down_round(i)
            down_pair(1, g_down.pairs // 2 - 1)
            tail(g_down.pairs - 2, 0)
            tail(g_down.pairs - 1, 1)


_INS = ["x", "c", "w_ada", "b_ada", "g_mix", "w_in", "b_f", "a_re", "a_im", "log_dt", "ssm_b_re",
        "ssm_b_im", "ssm_c_re", "ssm_c_im", "ssm_d", "w_glu", "b_glu", "g_attn_out", "g_ssm_out",
        "w_out", "g_ffn", "w_up", "conv_w", "conv_b", "w_down", "g_final"]
_MATRICES = ("w_ada", "w_in", "w_glu", "w_out", "w_up", "w_down")


def kernel(**inputs):
    import concourse.bacc as _bacc
    from concourse.bass_utils import run_bass_kernel_spmd as _run

    nc = _bacc.Bacc("TRN2", target_bir_lowering=False, num_devices=1, dynamic_dma_scratch_size=64)
    arrays, args = {}, []
    for name in _INS:
        a = np.ascontiguousarray(inputs[name])
        if name in _MATRICES:
            a = a.reshape(a.shape[1:])
        arrays[f"in_{name}"] = a
        args.append(nc.dram_tensor(f"in_{name}", a.shape, mybir.dt.from_np(a.dtype),
                                   kind="ExternalInput").ap())
    args.append(nc.dram_tensor("out_0", (1, T, D), F32, kind="ExternalOutput").ap())
    build(nc, *args)
    r = _run(nc, [arrays], core_ids=[0])
    return r.results[0]["out_0"]
```

```python
from contextlib import ExitStack

import concourse.bass as bass
import numpy as np
from concourse import mybir

F32 = mybir.dt.float32
F32R = mybir.dt.float32r
I32 = mybir.dt.int32
ALU = mybir.AluOpType
ACT = mybir.ActivationFunctionType
AX_X = mybir.AxisListType.X

P = 128
T = 256
TT = T // P
D = 2048
KD = D // P
NH = 8
HD = 128
AW = NH * HD
SW = 1024
KS = SW // P
NG, NS, GH = 64, 64, 16
NJ = NG * NS // P
JQ = 4
FF = 5632
KF = FF // P
EPS = 1e-6
SCALE = HD ** -0.5

UK = 4
UN = 256
USZ = UK * UN
RAW = 4
SPL = 4
WSPL = 3
WRAW = 3
ARING = 4
AN = 512
AK = USZ // AN
AU = KD // AK
SHIFT_SCALE1 = 2 * D // AN
BS = D // AN
BC = AN // P
ADA_BLOCKS = 6 * D // AN

MAGIC = 1.5 * 2.0 ** 23
TWO_PI = 2 * np.pi
C1 = 6.28125
C2 = float(np.floor((TWO_PI - C1) * 2.0 ** 21) / 2.0 ** 21)
C3 = float(TWO_PI - C1 - C2)
PI_IN = 3.1415925
MASKED = -1.0e30

V_GMIX, V_GFFN, V_GFINAL, V_GATTN, V_GSSM, V_BGLU, V_D, V_CONVB = 0, 16, 32, 48, 56, 64, 72, 80
V_BADA, V_ARE = 128, 224
V_CONV0, V_CONV1, V_AIM = 256, 300, 344
V_CONV2, V_COND, V_LOGDT = 384, 428, 448


def wait(eng, sem, value):
    if isinstance(value, int) and value <= 0:
        return
    eng.wait_ge(sem, value)


class Chain:

    def __init__(self, eng, sem):
        self.eng, self.sem, self.start, self.n = eng, sem, 0, 0

    def __call__(self, ins):
        ins.then_inc(self.sem, 1)
        self.n += 1
        self.eng.wait_ge(self.sem, self.start + self.n)

    def loop(self, i, per):
        self.base, self.per = self.start + self.n, per
        self.start, self.n = self.base + i * per, 0

    def after(self, passes):
        assert self.n == self.per, (self.n, self.per)
        self.start, self.n = self.base + passes * self.per, 0


STEPS = 64
EARLY = 3
SSM_FROM = 6
SSM_PIECES = 6
STAGE_AT = (0, 1, 2, 4, 5)
M_AT = 384


def window_pair(p):
    return ("u", p) if p < 4 else ("qkv"[(p - 4) % 3], (p - 4) // 3)


def ssm_piece(t):
    q, n = divmod(t - SSM_FROM, SSM_PIECES)
    return (q, n) if 0 <= q <= KS else None


def attention_step(t):
    found = []
    for h in range(NH - 2):
        at = 28 + 12 * (h // 2) + 6 * (h % 2)
        if t - at in STAGE_AT:
            found.append((h, STAGE_AT.index(t - at)))
    return found


class Gemm:

    def __init__(self, weights, pairs, units, column, before=None, first=None):
        self.w = weights.rearrange("(u f p) n -> u p f n", f=UK, p=P)
        self.pairs, self.units = pairs, units
        self.column = column
        self.n0, self.p0 = (before.n1, before.p1) if before else (STEPS, 0)
        self.n1, self.p1 = self.n0 + pairs * units, self.p0 + pairs
        self.skip = 0 if 2 * units % SPL == 0 else -units % SPL
        both = [par * (units + self.skip) + u for par in range(2) for u in range(units)]
        self.raw_slots = [[both[par * units + u] % RAW for u in range(units)] for par in range(2)]
        self.slots = [[both[par * units + u] % SPL for u in range(units)] for par in range(2)]
        order = self.raw_slots[0] + self.raw_slots[1]
        self.per = [order.count(s) for s in range(RAW)]
        self.turn = [[order[:par * units + u].count(self.raw_slots[par][u]) for u in range(units)]
                     for par in range(2)]
        self.order = first or [(par, u) for par in range(2) for u in range(units)]
        self.raw_lag, self.lag = RAW - self.skip, SPL - self.skip

    def place(self, par, i, u):
        if isinstance(i, int) and i == 0:
            n = self.order.index((par, u))
            par, u = divmod(n, self.units)
        return (self.n0 + (2 * i + par) * self.units + u, self.slots[par][u],
                self.raw_slots[par][u], self.turn[par][u])

    def done(self, par, i):
        if isinstance(i, int) and i == 0:
            return self.n0 + self.order.index((par, self.units - 1)) + 1
        return self.n0 + (2 * i + par + 1) * self.units


def build(nc, x, c, w_ada, b_ada, g_mix, w_in, b_f, a_re, a_im, log_dt, ssm_b_re, ssm_b_im,
          ssm_c_re, ssm_c_im, ssm_d, w_glu, b_glu, g_attn_out, g_ssm_out, w_out, g_ffn, w_up,
          conv_w, conv_b, w_down, g_final, out):
    ctx = ExitStack()
    with ctx:
        def sem(name):
            return ctx.enter_context(nc.semaphore(name))

        def place(at, *tiles):
            got = []
            for name, shape, dt in tiles:
                got.append(nc.alloc_sbuf_tensor_at(name, shape, dt, offset=at))
                at += -(-int(np.prod(shape[1:])) * 4 // 32) * 32
            return at, got

        base = -(-nc.sbuf_base // 64) * 64
        small_at, (hT, vec, mod, ident, ones, sq, rb, halves, gains, tiny, ncol, bf, sel, minus, w_split,
                   raw) = place(
            base,
            ("hT", [P, KD, T], F32),
            ("vec", [P, 512], F32),
            ("mod", [P, 96], F32),
            ("ident", [P, P], F32),
            ("ones", [P, T], F32),
            ("sq", [P, 2, T], F32),
            ("rb", [P, T], F32),
            ("halves", [P, 2, 2, T], F32),
            ("gains", [P, 2, KD], F32),
            ("tiny", [P, 24], F32),
            ("ncol", [P, 2, 8], F32),
            ("bf", [NH, 8], F32),
            ("sel", [P, 8], F32),
            ("minus", [NH, P], F32),
            ("w_split", [P, SPL, 2, USZ], F32R),
            ("raw", [P, RAW + 1, USZ], F32),
        )
        whi, wlo = w_split[:, :, 0, :], w_split[:, :, 1, :]
        ada_at = small_at - (RAW + 3) * USZ * 4
        _, (ada_raw,) = place(ada_at, ("ada_raw", [P, ARING, USZ], F32))
        end1, (cond, ada_rows, iota_i, iota_f, disc) = place(
            small_at,
            ("cond", [P, KD, 32], F32),
            ("ada_rows", [P, 2, AN], F32),
            ("iota_i", [P, 16], I32), ("iota_f", [P, 16], F32),
            ("disc", [P, 14, NJ], F32),
        )
        end2, (conv_in, gate, branch, gated) = place(
            small_at,
            ("conv_in", [P, 2, T + 2], F32), ("gate", [P, 2, T], F32),
            ("branch", [P, 2, T], F32), ("gated", [P, 2, T], F32),
        )
        acts_at = max(end1, end2)
        attn_at, (AA,) = place(acts_at, ("AA", [P, KD, 2 * T], F32R))
        _, (out_n, g_rows) = place(acts_at, ("out_n", [P, TT, D], F32), ("g_rows", [P, D], F32))
        ffn_at, (prob, probT, mask, csel, cum, tab_t, rot_t) = place(
            attn_at,
            ("prob", [P, 2, 3 * P], F32), ("probT", [P, 2, 3 * P], F32), ("mask", [P, 3 * P], F32),
            ("csel", [NH, 2, T], F32), ("cum", [NH, T], F32),
            ("tab_t", [P, 2, 16, 16], F32), ("rot_t", [P, 2, T], F32),
        )
        _, (wf,) = place(ffn_at - 2 * T * 4, ("wf", [P, KD, 32], F32))
        csel_at = attn_at + (2 * 3 * P * 2 + 3 * P) * 4
        _, (b_tmp,) = place(csel_at, ("b_tmp", [P, NJ, GH], F32))
        sq_at = base + (KD * T + 512 + 96 + P + T) * 4
        _, (vT,) = place(sq_at, ("vT", [P, 2, T], F32))
        end, (GG,) = place(ffn_at, ("GG", [P, KF, 2 * T], F32R))
        assert end <= nc.sbuf_usable_end
        mix_end, (uT, qT, kT, vN, btr, bti, ctr, cti, fac, tab, ssm_w) = place(
            ffn_at,
            ("uT", [P, KS, T], F32),
            ("qT", [P, NH, T], F32),
            ("kT", [P, NH, T], F32),
            ("vN", [P, TT, AW], F32),
            ("btr", [P, KS, P], F32), ("bti", [P, KS, P], F32),
            ("ctr", [P, KS, P], F32), ("cti", [P, KS, P], F32),
            ("fac", [P, 4, NJ, 16], F32),
            ("tab", [P, 2, 2, JQ, T], F32),
            ("ssm_w", [P, 4, JQ, T], F32),
        )
        assert mix_end <= end
        at_q = ffn_at + KS * T * 4
        _, (stage,) = place(ffn_at, ("stage", [P, 4, P], F32))
        _, (b_raw, b_bar, b_wide) = place(
            at_q,
            ("b_raw", [P, 2, NJ, GH], F32), ("b_bar", [P, 2, NJ, GH], F32),
            ("b_wide", [P, 2, NJ, 2, GH], F32),
        )
        _, (c_twice,) = place(at_q + 2 * KS * T * 4, ("c_twice", [P, 2, KS, 2, NS], F32))
        tab_at = mix_end - 2 * 16384
        _, (ph,) = place(tab_at, ("ph", [P, 4, NJ, 16], F32))
        _, (xn,) = place(mix_end - 16384, ("xn", [P, TT, D], F32))
        _, (xr,) = place(mix_end - 16384, ("xr", [P, KD, T], F32))
        _, (fw,) = place(attn_at, ("fw", [NH, 4, T], F32))

        psG = ctx.enter_context(nc.psum_tensor("psG", [P, 4, 512], F32))
        psX = ctx.enter_context(nc.psum_tensor("psX", [P, 4, 512], F32))

        first_of = {"q": 0, "k": AW, "v": 2 * AW, "u": 3 * AW + NH}
        w_in_v = w_in.rearrange("(u f p) n -> u p f n", f=UK, p=P)
        plain = lambda par, i: (2 * i + par) * UN
        g_glu = Gemm(w_glu, 4, KS // UK, plain)
        g_out = Gemm(w_out, 8, KD // UK, plain, g_glu,
                     [(0, 0), (0, 1), (1, 0), (1, 1), (0, 2), (0, 3), (1, 2), (1, 3)])
        g_up = Gemm(w_up, KF, KD // UK, lambda par, i: par * FF + i * UN, g_out)
        g_down = Gemm(w_down, 8, KF // UK, plain, g_up)

        raw_landed = [sem(f"raw_landed{s}") for s in range(RAW + 1)]
        ada_landed = [sem(f"ada_landed{s}") for s in range(ARING)]
        x_landed, stage_landed, bc_landed, wf_landed = map(
            sem, ("x_landed", "stage_landed", "bc_landed", "wf_landed"))
        g_rows_landed, out_stored = sem("g_rows_landed"), sem("out_stored")
        consts_ready, pool_chain = sem("consts_ready"), sem("pool_chain")
        stage_ready, vecT_done, vec_ready = sem("stage_ready"), sem("vecT_done"), sem("vec_ready")
        xT_done, hT_ready = sem("xT_done"), sem("hT_ready")
        cond_act, cond_ready = sem("cond_act"), sem("cond_ready")
        act_setup, dve_setup = sem("act_setup"), sem("dve_setup")
        bc_ready, bcT_done, bcT_ready = sem("bc_ready"), sem("bcT_done"), sem("bcT_ready")
        ada_used, ada_out, ada_cols, mod_ready = map(
            sem, ("ada_used", "ada_out", "ada_cols", "mod_ready"))
        sq_done, ss_used, root_done, rms_ready = map(
            sem, ("sq_done", "ss_used", "root_done", "rms_ready"))
        nt_ready, affine_done, nhi_done, act_ready = map(
            sem, ("nt_ready", "affine_done", "nhi_done", "act_ready"))
        hi_done, lo_done, mm_used, lo_half_out, pair_out = map(
            sem, ("hi_done", "lo_done", "mm_used", "lo_half_out", "pair_out"))
        tile_done, tile_half, tile_out = sem("tile_done"), sem("tile_half"), sem("tile_out")
        wf_zero, f_done, f_rows, f_sum, f_abs, f_ln, cum_ready = map(
            sem, ("wf_zero", "f_done", "f_rows", "f_sum", "f_abs", "f_ln", "cum_ready"))
        vN_done, vN_ready = sem("vN_done"), sem("vN_ready")
        csel_ready, score_done, masked, exp_done = map(
            sem, ("csel_ready", "score_done", "masked", "exp_done"))
        max_ready, prob_ready, probT_done, probT_ready, pv_done, o_ready = map(
            sem, ("max_ready", "prob_ready", "probT_done", "probT_ready", "pv_done", "o_ready"))
        tab_ready, e_done, rotated, scanned, z_prod_pool, z_prod, y_part, y_ready, gelu_done = map(
            sem, ("tab_ready", "e_done", "rotated", "scanned", "z_prod_pool", "z_prod", "y_part",
                  "y_ready", "gelu_done"))
        y_sq_done, y_gain_done, y_ss_used = map(sem, ("y_sq_done", "y_gain_done", "y_ss_used"))
        h_gain_done, h_hi_done = sem("h_gain_done"), sem("h_hi_done")
        glu_hi, glu_act_ready = sem("glu_hi"), sem("glu_act_ready")
        z_ready, sig_done, conv_done, silu_done, gated_ready, ghi_done, g_ready = map(
            sem, ("z_ready", "sig_done", "conv_done", "silu_done", "gated_ready", "ghi_done",
                  "g_ready"))
        tail_T, tail_sq, tail_out, sumsq_done = map(
            sem, ("tail_T", "tail_sq", "tail_out", "sumsq_done"))
        root2_done, inv_done, final_act, final_dve = map(
            sem, ("root2_done", "inv_done", "final_act", "final_dve"))
        dve_chain, act_chain = sem("dve_chain"), sem("act_chain")

        NORM1, NORMA, NORMS, NORM2 = (0, 0), (1, KD // 4), (2, (KD + KS) // 4), (3, (KD + 2 * KS) // 4)
        SUMS2 = NORMA[1] + 2
        STAGE_DMAS, BC_DMAS = 15, 4

        score_bank = lambda h: 0 if h == NH - 1 else 1
        out_bank = lambda h: 3 if h == NH - 1 else 2
        WINDOW_ADA = SHIFT_SCALE1 * AU

        block = ctx.enter_context(nc.Block())

        @block.sync
        def _(sp):
            owner = [None] * (RAW + 1)

            def load(s, f, src, done):
                if owner[s]:
                    sp.wait_ge(*owner[s])
                sp.dma_start(raw[:, s, :].rearrange("p (f n) -> p f n", f=f), src
                             ).then_inc(raw_landed[s], 16)
                owner[s] = done

            w_ada_v = w_ada.rearrange("(u f p) n -> u p f n", f=AK, p=P)

            def ada_unit(which, i, u):
                return w_ada_v[u, :, :, bass.ds((which * BS + i) * AN, AN)]

            def load_ada(n, src):
                if not isinstance(n, int) or n >= ARING:
                    sp.wait_ge(ada_used, n - ARING + 1)
                slot = n % ARING
                sp.dma_start(ada_raw[:, slot, :].rearrange("p (f n) -> p f n", f=AK), src
                             ).then_inc(ada_landed[slot], 16)

            for which in range(2):
                for u in range(AU):
                    load_ada(which * AU + u, ada_unit(which, 0, u))
            with nc.sync.Fori(1, BS - 1) as i:
                for which in range(2):
                    for u in range(AU):
                        sp.wait_ge(ada_used, (2 * i + which) * AU + u - ARING + 1)
                        slot = u % ARING
                        sp.dma_start(ada_raw[:, slot, :].rearrange("p (f n) -> p f n", f=AK),
                                     ada_unit(which, i, u)).then_inc(ada_landed[slot], 16)

            def load_w_in(t):
                kind, j = window_pair(t // 4)
                at = first_of[kind] + j * UN
                load(RAW + 1 - WRAW + t % WRAW, UK, w_in_v[t % 4, :, :, at:at + UN], (lo_done, t + 1))

            for t in range(EARLY):
                load_w_in(t)
            for which in range(2):
                for u in range(AU):
                    load_ada((2 * (BS - 1) + which) * AU + u, ada_unit(which, BS - 1, u))

            for t in range(STEPS):
                if t + EARLY < STEPS:
                    load_w_in(t + EARLY)
                for n in range(2):
                    a = 2 * t + n
                    at = (SHIFT_SCALE1 + a // AU) * AN
                    load_ada(WINDOW_ADA + a, w_ada_v[a % AU, :, :, at:at + AN])
            owner[0:2] = [(ada_used, WINDOW_ADA + 2 * STEPS)] * 2

            for g in (g_glu, g_out, g_up, g_down):
                for par, u in g.order:
                    n, _, s, _ = g.place(par, 0, u)
                    at = g.column(par, 0)
                    load(s, UK, g.w[u, :, :, at:at + UN], (lo_done, n + 1))
                with nc.sync.Fori(1, g.pairs // 2) as i:
                    for par in range(2):
                        for u in range(g.units):
                            sp.wait_ge(lo_done, g.n0 + (2 * i + par) * g.units + u - g.raw_lag + 1)
                            s = g.raw_slots[par][u]
                            sp.dma_start(raw[:, s, :].rearrange("p (f n) -> p f n", f=UK),
                                         g.w[u, :, :, bass.ds(g.column(par, i), UN)]
                                         ).then_inc(raw_landed[s], 16)
                both = [(par, u) for par in range(2) for u in range(g.units)]
                for n, (par, u) in enumerate(both):
                    owner[g.raw_slots[par][u]] = (lo_done, g.n1 - 2 * g.units + n + 1)

            ov = out.rearrange("b (t p) d -> p (b t) d", p=P)
            for half in range(2):
                cols = slice(half * D // 2, (half + 1) * D // 2)
                sp.wait_ge(final_dve, half + 1)
                sp.dma_start(ov[:, 1, cols], out_n[:, 1, cols]).then_inc(out_stored, 16)
            sp.wait_ge(out_stored, 16 * 4)

        @block.gpsimd
        def _(pool):
            link = Chain(pool, pool_chain)
            link(nc.gpsimd.memset(ident[:], 0.0))
            link(nc.gpsimd.affine_select(out=ident[:], in_=ident[:], compare_op=ALU.not_equal, fill=1.0,
                                         base=0, pattern=[[-1, P]], channel_multiplier=1))
            nc.gpsimd.memset(ones[:], 1.0).then_inc(consts_ready, 1)
            nc.gpsimd.iota(iota_i[:], pattern=[[1, 16]], base=0, channel_multiplier=0
                           ).then_inc(consts_ready, 1)
            nc.gpsimd.memset(wf[:], 0.0).then_inc(wf_zero, 1)
            def table(q):
                for half in range(2):
                    js = slice(JQ * q + 2 * half, JQ * q + 2 * half + 2)
                    cs, ss = (fac[:, a, js, :].unsqueeze(2).to_broadcast([P, 2, 16, 16])
                              for a in (0, 1))
                    ck, sk = (fac[:, a, js, :].unsqueeze(3).to_broadcast([P, 2, 16, 16])
                              for a in (2, 3))
                    ct, st = (tab[:, q % 2, a, 2 * half:2 * half + 2, :]
                              .rearrange("p j (k s) -> p j k s", s=16) for a in (0, 1))
                    link(nc.gpsimd.tensor_tensor(ct, cs, ck, ALU.mult))
                    link(nc.gpsimd.tensor_tensor(tab_t[:], ss, sk, ALU.mult))
                    link(nc.gpsimd.tensor_tensor(ct, ct, tab_t[:], ALU.subtract))
                    link(nc.gpsimd.tensor_tensor(st, cs, sk, ALU.mult))
                    link(nc.gpsimd.tensor_tensor(tab_t[:], ss, ck, ALU.mult))
                    ins = nc.gpsimd.tensor_tensor(st, st, tab_t[:], ALU.add)
                    if half == 0:
                        link(ins)
                ins.then_inc(tab_ready, 1)
                pool.wait_ge(tab_ready, q + 1)

            pool.wait_ge(act_setup, 6)
            table(0)
            table(1)
            for q in range(KS):
                zre, zim, p0, p1 = (ssm_w[:, (n + 2 * (q % 2)) % 4, :, :] for n in range(4))
                ct = tab[:, q % 2, 0, :, :]
                pool.wait_ge(scanned, 2 * q + 2)
                wait(pool, y_part, 2 * q)
                nc.gpsimd.tensor_tensor(p0, ct, zre, ALU.mult).then_inc(z_prod_pool, 1)
                pool.wait_ge(z_prod, 2 * q + 1)
                nc.gpsimd.tensor_tensor(zim, ct, zim, ALU.mult).then_inc(z_prod_pool, 1)
                if q + 2 < KS:
                    pool.wait_ge(z_prod_pool, 2 * q + 2)
                    pool.wait_ge(z_prod, 2 * q + 2)
                    table(q + 2)

        @block.scalar
        def _(act):
            link = Chain(act, act_chain)
            uses = [0] * (RAW + 1)

            def row(v):
                return v.rearrange("l (r p) -> (l r) p", p=P)

            act.wait_ge(stage_ready, 1)
            for s, at, src in (
                (3, V_COND, row(c)), (0, V_GMIX, row(g_mix)), (0, V_GFFN, row(g_ffn)),
                (0, V_GFINAL, g_final.rearrange("(r p) -> r p", p=P)), (0, V_GATTN, row(g_attn_out)),
                (0, V_GSSM, row(g_ssm_out)), (0, V_BGLU, row(b_glu)),
                (0, V_D, ssm_d.rearrange("l (r g) h -> (l r) (g h)", g=8)), (0, V_CONVB, row(conv_b)),
                (1, V_BADA, row(b_ada)), (1, V_ARE, a_re.rearrange("l (r g) p -> (l r) (g p)", g=2)),
                (2, V_AIM, a_im.rearrange("l (r g) p -> (l r) (g p)", g=2)),
                (2, V_CONV0, conv_w.rearrange("l w (r p) -> (l w r) p", p=P)[0:2 * KF]),
                (3, V_CONV2, conv_w.rearrange("l w (r p) -> (l w r) p", p=P)[2 * KF:3 * KF]),
            ):
                r = at - P * s
                act.dma_start(stage[r:r + src.shape[0], s, :], src).then_inc(stage_landed, 16)
            with nc.allow_non_contiguous_dma(reason="64 numbers"):
                act.dma_start(tiny[V_LOGDT % P:V_LOGDT % P + NJ, KD:KD + 2],
                              log_dt.rearrange("l (r g) -> (l r) g", g=2)).then_inc(stage_landed, 16)
                act.dma_start(bf[:, 0:1], b_f.rearrange("l h -> h l")).then_inc(wf_landed, 16)
            xv = x.rearrange("b (t p) d -> p (b t) d", p=P)
            for tt in range(TT):
                act.dma_start(xn[:, tt, :], xv[:, tt, :]).then_inc(x_landed, 16)

            for a, (bm, cm) in enumerate(((ssm_b_re, ssm_c_re), (ssm_b_im, ssm_c_im))):
                act.dma_start(b_raw[:, a, :, :], bm.rearrange("l (j g) p h -> (g p) (l j) h", g=2)
                              ).then_inc(bc_landed, 16)
                act.dma_start(c_twice[:, a, :, 0, :], cm.rearrange("l (q g) h p -> (g h) (l q) p", g=8)
                              ).then_inc(bc_landed, 16)
            act.wait_ge(wf_zero, 1)
            act.dma_start(wf[:, :, 0:NH],
                          w_in[:, 3 * AW:3 * AW + NH].rearrange("(k p) h -> p k h", p=P)
                          ).then_inc(wf_landed, 16)

            act.wait_ge(vec_ready, 1)
            nc.scalar.activation(tiny[:, 0:KD], vec[:, V_COND:V_COND + KD], ACT.Silu
                                 ).then_inc(cond_act, 1)
            for r in (1, 3):
                act.wait_ge(xT_done, r + 1)
                nc.scalar.activation(hT[:, 4 * r:4 * r + 4, :].rearrange("p (b j) t -> p b (j t)", j=2),
                                     psG[:, 2:4, :], ACT.Copy).then_inc(hT_ready, 1)
            nt = xr

            def squares(src, groups):
                for gr in range(groups):
                    nc.scalar.activation(xr[:, 4 * gr:4 * gr + 4, :], src[:, 4 * gr:4 * gr + 4, :],
                                         ACT.Square).then_inc(sq_done, 1)

            def ada_evacuate(b, bank, row):
                act.wait_ge(ada_used, (b + 1) * AU)
                wait(act, ada_cols, b - 1)
                nc.scalar.activation(ada_rows[:, row, :], psX[:, bank, :], ACT.Copy
                                     ).then_inc(ada_out, 1)

            nc.scalar.activation(disc[:, 0, :], vec[:, V_LOGDT:V_LOGDT + NJ], ACT.Exp
                                 ).then_inc(act_setup, 1)
            act.wait_ge(hT_ready, 4)
            squares(hT, KD // 4)
            act.wait_ge(dve_setup, 1)
            nc.scalar.activation(disc[:, 3, :], disc[:, 1, :], ACT.Exp).then_inc(act_setup, 1)
            ada_evacuate(0, 0, 0)
            for half in range(2):
                act.wait_ge(dve_setup, 2 + half)
                nc.scalar.activation(fac[:, 2 * half + 1, :, :], ph[:, 1, :, :], ACT.Sin
                                     ).then_inc(act_setup, 1)
                nc.scalar.activation(fac[:, 2 * half, :, :], ph[:, 3, :, :], ACT.Sin
                                     ).then_inc(act_setup, 1)

            def root(which, width, bank=3):
                index, g0 = which
                wait(act, nt_ready, g0)
                nc.scalar.activation(rb[:], psX[:, bank, 0:T], ACT.Sqrt, scale=1.0 / width,
                                     bias=ncol[:, 0, 7:8]).then_inc(root_done, 1)

            def gains_and_hi(group, gr, k0, scale, shift):
                act.wait_ge(nt_ready, group + 1)
                for j in range(4 * gr, 4 * gr + 4):
                    t = nt[:, k0 + j, :]
                    if shift is None:
                        nc.scalar.activation(t, t, ACT.Copy, scale=scale(j)).then_inc(affine_done, 1)
                    else:
                        nc.scalar.activation(t, t, ACT.Identity, scale=scale(j), bias=shift(j)
                                             ).then_inc(affine_done, 1)
                act.wait_ge(affine_done, 4 * group + 4)
                k = slice(k0 + 4 * gr, k0 + 4 * gr + 4)
                nc.scalar.activation(AA[:, k, 0:T], nt[:, k, :], ACT.Copy).then_inc(nhi_done, 1)

            def hi_unit(g, par, i, u, first):
                n, s, r, turn = g.place(par, i, u)
                act.wait_ge(raw_landed[r], 16 * (first[r] + i * g.per[r] + turn) + 16)
                act.wait_ge(mm_used, n - g.lag + 1)
                nc.scalar.activation(whi[:, s, :], raw[:, r, :], ACT.Copy).then_inc(hi_done, 1)

            def split(g, par, i, units=None):
                if isinstance(i, int) and (par, i) == (0, 0) and not (units and units[0]):
                    g.first = list(uses)
                    for r in range(RAW):
                        uses[r] += g.pairs // 2 * g.per[r]
                for u in units or range(g.units):
                    hi_unit(g, par, i, u, g.first)

            def gemm(g, evacuate, then=None, before=lambda par, i: None):
                last = g.pairs // 2 - 1

                def turn(i, units=None):
                    before(1, i)
                    split(g, 1, i, units)
                    evacuate(0, i)
                    before(0, i)
                    split(g, 0, i + 1)
                    evacuate(1, i)

                turn(0, [u for par, u in g.order[g.units:] if par])
                if last > 1:
                    with nc.scalar.Fori(1, last) as i:
                        turn(i)
                before(1, last)
                split(g, 1, last)
                evacuate(0, last)
                before(0, last)
                if then:
                    split(then, 0, 0, range(3))
                evacuate(1, last)
                if then:
                    split(then, 0, 0, range(3, then.units))


            def window_hi(t):
                r = RAW + 1 - WRAW + t % WRAW
                act.wait_ge(raw_landed[r], 16 * (t // WRAW) + 16)
                wait(act, mm_used, t - WSPL + 1)
                nc.scalar.activation(whi[:, t % WSPL, :], raw[:, r, :], ACT.Copy).then_inc(hi_done, 1)

            gains1 = lambda gr: gains_and_hi(gr, gr, 0, lambda j: gains[:, 0, j:j + 1],
                                             lambda j: mod[:, j:j + 1])
            for b in range(SHIFT_SCALE1):
                if b == SHIFT_SCALE1 - 2:
                    window_hi(0)
                    window_hi(1)
                if b:
                    ada_evacuate(b, b % 2, b % 2)
                if b == 1:
                    act.wait_ge(ss_used, KD // 4)
                    root(NORM1, D)
                if b % 2 == 0 and b:
                    act.wait_ge(mod_ready, b // 2)
                    gains1(b // 2 - 1)
                if b == SHIFT_SCALE1 - 2:
                    window_hi(2)
            act.wait_ge(mod_ready, BS)
            gains1(BS - 1)

            def attention_act(h, part):
                b = h % 2
                if part == 0:
                    act.wait_ge(vN_done, h + 1)
                    nc.scalar.activation(vN[:, :, h * HD:h * HD + HD],
                                         psX[:, score_bank(h), 0:T].rearrange("p (t n) -> p t n", t=TT), ACT.Copy
                                         ).then_inc(vN_ready, 1)
                    act.wait_ge(cum_ready, 1)
                    wait(act, score_done, h - 1)
                    nc.scalar.activation(csel[:, b, :], cum[:], ACT.Copy, scale=ident[0:NH, h:h + 1]
                                         ).then_inc(csel_ready, 1)
                elif part == 1:
                    act.wait_ge(max_ready, h + 1)
                    for tt, cols in ((0, slice(0, P)), (1, slice(P, 3 * P))):
                        nc.scalar.activation(prob[:, b, cols], prob[:, b, cols], ACT.Exp,
                                             bias=ncol[:, b, 2 + tt:3 + tt],
                                             accum_out=ncol[:, b, 4 + tt:5 + tt]).then_inc(exp_done, 1)
                elif part == 3:
                    act.wait_ge(probT_done, h + 1)
                    wait(act, pv_done, h - 1)
                    nc.scalar.activation(probT[:, b, :], psX[:, score_bank(h), 0:3 * P], ACT.Copy
                                         ).then_inc(probT_ready, 1)
                elif part == 4:
                    act.wait_ge(pv_done, h + 1)
                    nc.scalar.activation(qT[:, h, :], psX[:, out_bank(h), 0:T], ACT.Copy
                                         ).then_inc(o_ready, 1)

            act.wait_ge(pool_chain, 2)
            for t in range(STEPS):
                if t % 4 == 3:
                    scale = SCALE if window_pair(t // 4)[0] == "q" else 1.0
                    for m in range(2):
                        if m == 0:
                            act.wait_ge(tile_done, t // 4 + 1)
                        else:
                            act.wait_ge(mm_used, t + 1)
                        nc.scalar.activation(halves[:, 0, m, :], psG[:, m, T:2 * T], ACT.Copy,
                                             scale=scale).then_inc(tile_half, 1)
                if t + 3 < STEPS:
                    window_hi(t + 3)
                if t % 4 == 3:
                    ada_evacuate(SHIFT_SCALE1 + t // 4, 0, (t // 4) % 2)
                if t == 4:
                    act.wait_ge(f_done, 1)
                    nc.scalar.activation(rb[:], psX[:, 1, 0:T], ACT.Copy).then_inc(f_rows, 1)
                if t == 6:
                    act.wait_ge(f_abs, 1)
                    link(nc.scalar.activation(fw[:, 1, :], fw[:, 1, :], ACT.Exp, scale=-1.0))
                    nc.scalar.activation(fw[:, 1, :], fw[:, 1, :], ACT.Ln, bias=ones[0:NH, 0:1]
                                         ).then_inc(f_ln, 1)
                qn = ssm_piece(t)
                if qn and qn[1] == 2 and qn[0] >= 1:
                    q = qn[0] - 1
                    act.wait_ge(y_ready, q + 1)
                    nc.scalar.activation(uT[:, q, :], uT[:, q, :], ACT.Gelu_apprx_tanh
                                         ).then_inc(gelu_done, 1)
                for h, part in attention_step(t - 1):
                    attention_act(h, part)
            for h, part in attention_step(STEPS - 1):
                attention_act(h, part)
            for n in range(WRAW):
                uses[RAW + 1 - WRAW + n] += len(range(n, STEPS, WRAW))

            def pair_done(g, par, i):
                act.wait_ge(mm_used, g.done(par, i))

            def take_lo(g):
                def evacuate(par, i):
                    pair_done(g, par, i)
                    nc.scalar.activation(halves[:, par, :, :], psG[:, 2 * par:2 * par + 2, T:2 * T],
                                         ACT.Copy).then_inc(lo_half_out, 1)
                return evacuate

            def evacuate_glu(p):
                take_lo(g_glu)(p % 2, p // 2)
                act.wait_ge(z_ready, p + 1)
                for m in range(2):
                    at = V_BGLU + 2 * p + m
                    nc.scalar.activation(halves[:, p % 2, m, :], halves[:, p % 2, m, :], ACT.Sigmoid,
                                         bias=vec[:, at:at + 1]).then_inc(sig_done, 1)

            def square_y(p):
                act.wait_ge(pair_out, p + 1)
                nc.scalar.activation(xr[:, KS + 2 * p:KS + 2 * p + 2, :], uT[:, 2 * p:2 * p + 2, :],
                                     ACT.Square).then_inc(y_sq_done, 1)
                for j in (2 * p, 2 * p + 1):
                    nc.scalar.activation(kT[:, j, :], uT[:, j, :], ACT.Copy,
                                         scale=vec[:, V_GSSM + j:V_GSSM + j + 1]).then_inc(y_gain_done, 1)

            def last_heads(part):
                for h in (NH - 2, NH - 1):
                    attention_act(h, part)

            last_heads(0)
            act.wait_ge(gelu_done, KS)
            act.wait_ge(mm_used, STEPS)
            for gr in range(2):
                nc.scalar.activation(AA[:, KS + 4 * gr:KS + 4 * gr + 4, 0:T],
                                     uT[:, 4 * gr:4 * gr + 4, :], ACT.Copy).then_inc(glu_hi, 1)
            split(g_glu, 0, 0)
            last_heads(1)
            split(g_glu, 1, 0)
            last_heads(2)
            evacuate_glu(0)
            last_heads(3)
            split(g_glu, 0, 1)
            square_y(0)
            evacuate_glu(1)
            last_heads(4)
            act.wait_ge(o_ready, NH)
            squares(qT, 2)
            split(g_glu, 1, 1)
            square_y(1)
            evacuate_glu(2)
            act.wait_ge(ss_used, NORMA[1] + 2)
            root(NORMA, AW)
            square_y(2)
            for gr in range(2):
                split(g_out, 0, 0, range(gr, gr + 1))
                gains_and_hi(NORMA[1] + gr, gr, 0, lambda j: vec[:, V_GATTN + j:V_GATTN + j + 1], None)
            split(g_out, 1, 0, range(1))
            evacuate_glu(3)
            square_y(3)
            split(g_out, 1, 0, range(1, 2))
            act.wait_ge(y_ss_used, 4)
            root(NORMS, SW, 0)
            for gr in range(2):
                act.wait_ge(nt_ready, NORMS[1] + gr + 1)
                k = slice(KS + 4 * gr, KS + 4 * gr + 4)
                nc.scalar.activation(AA[:, k, 0:T], xr[:, k, :], ACT.Copy).then_inc(nhi_done, 1)
                split(g_out, 0, 0, range(2 + gr, 3 + gr))

            def take_gated(g, gate_col):
                def evacuate(par, i):
                    pair_done(g, par, i)
                    for m in range(2):
                        nc.scalar.activation(
                            halves[:, par, m, :], psG[:, 2 * par + m, T:2 * T], ACT.Copy,
                            scale=mod[:, bass.ds(gate_col + 4 * i + 2 * par + m, 1)]
                        ).then_inc(lo_half_out, 1)
                return evacuate

            def square_pair(par, i):
                p = 2 * i + par
                act.wait_ge(pair_out, g_out.p0 + p + 1)
                act.wait_ge(ss_used, SUMS2 + p)
                nc.scalar.activation(sq[:], hT[:, bass.ds(2 * p, 2), :], ACT.Square
                                     ).then_inc(sq_done, 1)
                for m in range(2):
                    nc.scalar.activation(xr[:, bass.ds(2 * p + m, 1), :].rearrange("p o t -> p (o t)"),
                                         hT[:, bass.ds(2 * p + m, 1), :].rearrange("p o t -> p (o t)"),
                                         ACT.Copy, scale=gains[:, 1, bass.ds(2 * p + m, 1)]
                                         ).then_inc(h_gain_done, 1)

            def square_before(par, i):
                if par == 0:
                    square_pair(0, i)
                elif not (isinstance(i, int) and i == 0):
                    square_pair(1, i - 1)

            act.wait_ge(mod_ready, BS + 1)
            gemm(g_out, take_gated(g_out, 2 * KD), g_up, square_before)
            square_pair(1, g_out.pairs // 2 - 1)
            act.wait_ge(ss_used, SUMS2 + g_out.pairs)
            root(NORM2, D)
            for j in range(KD):
                if j % 4 == 0:
                    act.wait_ge(nt_ready, NORM2[1] + j // 4 + 1)
                nc.scalar.activation(AA[:, j, 0:T], xr[:, j, :], ACT.Identity,
                                     bias=mod[:, 3 * KD + j:3 * KD + j + 1]).then_inc(h_hi_done, 1)

            def evacuate_up(par, i):
                take_lo(g_up)(par, i)
                if par == 0:
                    act.wait_ge(conv_done, i + 1)
                    nc.scalar.activation(gate[:], gate[:], ACT.Silu).then_inc(silu_done, 1)
                else:
                    act.wait_ge(gated_ready, i + 1)
                    nc.scalar.activation(GG[:, bass.ds(2 * i, 2), 0:T], gated[:], ACT.Copy
                                         ).then_inc(ghi_done, 1)

            gemm(g_up, evacuate_up, g_down)
            act.wait_ge(mm_used, g_up.n1)
            act.dma_start(g_rows[:], g_final.rearrange("(l d) -> l d", l=1).to_broadcast([P, D])
                          ).then_inc(g_rows_landed, 16)

            def tail_squares(pair, par):
                act.wait_ge(tail_T, pair + 1)
                for tt in range(TT):
                    nc.scalar.activation(sq[:, tt, :], psX[:, par, tt * T:tt * T + T], ACT.Square,
                                         accum_out=tiny[:, bass.ds(tt * g_down.pairs + pair, 1)]
                                         ).then_inc(tail_sq, 1)

            def evacuate_down(par, i):
                take_gated(g_down, 5 * KD)(par, i)
                if not (isinstance(i, int) and i == 0 and par == 0):
                    act.wait_ge(tail_sq, 2 * (2 * i + par - 1))
                if par:
                    tail_squares(2 * i, 0)
                elif not (isinstance(i, int) and i == 0):
                    tail_squares(2 * i - 1, 1)

            gemm(g_down, evacuate_down)
            act.wait_ge(tail_sq, 2 * (g_down.pairs - 1))
            tail_squares(g_down.pairs - 1, 1)
            act.wait_ge(sumsq_done, 1)
            nc.scalar.activation(tiny[:, 18:20], tiny[:, 16:18], ACT.Sqrt, scale=1.0 / D,
                                 bias=ncol[:, 0, 7:8]).then_inc(root2_done, 1)
            ov = out.rearrange("b (t p) d -> p (b t) d", p=P)
            act.wait_ge(inv_done, 1)
            act.wait_ge(tail_out, g_down.pairs)
            for half in range(2):
                cols = slice(half * D // 2, (half + 1) * D // 2)
                nc.scalar.activation(out_n[:, 0, cols], out_n[:, 0, cols], ACT.Copy,
                                     scale=tiny[:, 18:19]).then_inc(final_act, 1)
            for half in range(2):
                cols = slice(half * D // 2, (half + 1) * D // 2)
                act.wait_ge(final_act, half + 1)
                act.dma_start(ov[:, 0, cols], out_n[:, 0, cols]).then_inc(out_stored, 16)

        @block.vector
        def _(dve):
            link = Chain(dve, dve_chain)
            V = nc.vector
            V.memset(stage[:], 0.0).then_inc(stage_ready, 1)
            V.memset(ncol[:, 0, 7:8], EPS).then_inc(cond_ready, 1)
            V.memset(cond[:], 0.0).then_inc(cond_ready, 1)
            V.memset(minus[:], -1.0).then_inc(cond_ready, 1)
            dve.wait_ge(pool_chain, 2)
            link(V.tensor_copy(sel[:], ident[:, 0:NH]))
            for g in range(1, 4):
                link(V.tensor_tensor(sel[:], sel[:], ident[:, 32 * g:32 * g + NH], ALU.add))

            dve.wait_ge(stage_landed, 16 * STAGE_DMAS)
            r = V_LOGDT % P
            for g in range(2):
                V.tensor_copy(stage[r:r + NJ, 3, NS * g:NS * g + NS],
                              tiny[r:r + NJ, KD + g:KD + g + 1].to_broadcast([NJ, NS])).then_inc(stage_ready, 1)
            dve.wait_ge(vecT_done, 1)
            V.tensor_copy(vec[:], psX[:, 0, :]).then_inc(vec_ready, 1)
            dve.wait_ge(cond_act, 1)
            V.tensor_copy(cond[:, :, 0:1], tiny[:, 0:KD].unsqueeze(2)).then_inc(cond_ready, 1)
            for r in (0, 2):
                dve.wait_ge(xT_done, r + 1)
                V.tensor_copy(hT[:, 4 * r:4 * r + 4, :].rearrange("p (b j) t -> p b (j t)", j=2),
                              psG[:, 0:2, :]).then_inc(hT_ready, 1)

            d = lambda n: disc[:, n, :]
            are, aim = vec[:, V_ARE:V_ARE + NJ], vec[:, V_AIM:V_AIM + NJ]
            dve.wait_ge(act_setup, 1)
            link(V.tensor_tensor(d(1), d(0), are, ALU.mult))
            V.tensor_tensor(d(2), d(0), aim, ALU.mult).then_inc(dve_setup, 1)
            dve.wait_ge(dve_setup, 1)
            dve.wait_ge(consts_ready, 2)
            link(V.tensor_copy(iota_f[:], iota_i[:]))

            def turns(r, big, k):
                link(V.tensor_scalar(k, big, float(1 / TWO_PI), MAGIC, ALU.mult, ALU.add))
                link(V.tensor_scalar(k, k, -MAGIC, None, ALU.add))
                link(V.scalar_tensor_tensor(r, k, -C1, big, ALU.mult, ALU.add))
                link(V.scalar_tensor_tensor(r, k, -C2, r, ALU.mult, ALU.add))
                link(V.scalar_tensor_tensor(r, k, -C3, r, ALU.mult, ALU.add))

            s16 = iota_f[:].unsqueeze(1).to_broadcast([P, NJ, 16])
            p_ = lambda n: ph[:, n, :, :]
            for half in range(2):
                if half:
                    link(V.tensor_scalar(d(2), d(4), 16.0, None, ALU.mult))
                turns(d(4), d(2), d(5))
                link(V.tensor_copy(d(6).bitcast(F32R), d(4)))
                link(V.tensor_tensor(d(7), d(4), d(6), ALU.subtract))
                th, tl = (d(n).unsqueeze(2).to_broadcast([P, NJ, 16]) for n in (6, 7))
                if half:
                    dve.wait_ge(act_setup, 4)
                link(V.tensor_tensor(p_(0), s16, th, ALU.mult))
                turns(p_(1), p_(0), p_(2))
                link(V.tensor_tensor(p_(2), s16, tl, ALU.mult))
                link(V.tensor_tensor(p_(1), p_(1), p_(2), ALU.add))
                link(V.tensor_scalar(p_(3), p_(1), float(np.pi / 2), float(-TWO_PI), ALU.is_gt, ALU.mult))
                link(V.scalar_tensor_tensor(p_(3), p_(1), float(np.pi / 2), p_(3), ALU.add, ALU.add))
                link(V.tensor_scalar(p_(1), p_(1), PI_IN, -PI_IN, ALU.min, ALU.max))
                V.tensor_scalar(p_(3), p_(3), PI_IN, -PI_IN, ALU.min, ALU.max).then_inc(dve_setup, 1)
                dve.wait_ge(dve_setup, 2 + half)
            dve.wait_ge(act_setup, 6)
            c1, s1 = fac[:, 0, :, 1:2].rearrange("p j o -> p (j o)"), fac[:, 1, :, 1:2].rearrange("p j o -> p (j o)")
            link(V.tensor_tensor(d(4), d(3), c1, ALU.mult))
            link(V.tensor_scalar(d(4), d(4), -1.0, None, ALU.add))
            link(V.tensor_tensor(d(5), d(3), s1, ALU.mult))
            link(V.tensor_tensor(d(6), are, are, ALU.mult))
            link(V.tensor_tensor(d(7), aim, aim, ALU.mult))
            link(V.tensor_tensor(d(6), d(6), d(7), ALU.add))
            link(V.reciprocal(d(6), d(6)))
            link(V.tensor_tensor(d(7), d(4), are, ALU.mult))
            link(V.tensor_tensor(d(8), d(5), aim, ALU.mult))
            link(V.tensor_tensor(d(7), d(7), d(8), ALU.add))
            link(V.tensor_tensor(d(9), d(7), d(6), ALU.mult))
            link(V.tensor_tensor(d(7), d(5), are, ALU.mult))
            link(V.tensor_tensor(d(8), d(4), aim, ALU.mult))
            link(V.tensor_tensor(d(7), d(7), d(8), ALU.subtract))
            link(V.tensor_tensor(d(10), d(7), d(6), ALU.mult))
            def prepare_b():
              dve.wait_ge(bc_landed, 16 * BC_DMAS)
              zr, zi = (d(n).unsqueeze(2).to_broadcast([P, NJ, GH]) for n in (9, 10))
              br, bi = b_raw[:, 0, :, :], b_raw[:, 1, :, :]
              link(V.tensor_tensor(b_tmp[:], zi, bi, ALU.mult))
              link(V.tensor_tensor(b_bar[:, 0, :, :], zr, br, ALU.mult))
              link(V.tensor_tensor(b_bar[:, 0, :, :], b_bar[:, 0, :, :], b_tmp[:], ALU.subtract))
              link(V.tensor_tensor(b_tmp[:], zi, br, ALU.mult))
              link(V.tensor_tensor(b_bar[:, 1, :, :], zr, bi, ALU.mult))
              link(V.tensor_tensor(b_bar[:, 1, :, :], b_bar[:, 1, :, :], b_tmp[:], ALU.add))
              V.tensor_copy(c_twice[:, :, :, 1, :].rearrange("p a q n -> p (a q) n"),
                            c_twice[:, :, :, 0, :].rearrange("p a q n -> p (a q) n")
                            ).then_inc(bc_ready, 1)
              V.memset(ctr[:], 0.0).then_inc(bc_ready, 1)
              V.memset(cti[:], 0.0).then_inc(bc_ready, 1)
              link(V.memset(b_wide[:], 0.0))
              for g in range(2):
                  half = slice(NS * g, NS * g + NS)
                  V.tensor_copy(b_wide[half, :, :, g, :].rearrange("p a j h -> p (a j) h"),
                                b_bar[half, :, :, :].rearrange("p a j h -> p (a j) h")
                                ).then_inc(bc_ready, 1)

            def take_matrix(r):
                dve.wait_ge(bcT_done, r + 1)
                if r < 2:
                    V.tensor_copy((btr, bti)[r][:].rearrange("p (b q) n -> p b (q n)", b=2),
                                  psG[:, 2:4, :]).then_inc(bcT_ready, 1)
                    return
                dst, sign = ((ctr, 1.0), (cti, -1.0))[r - 2]
                for g in range(2):
                    half = slice(NS * g, NS * g + NS)
                    ins = V.tensor_scalar(
                        dst[half, :, :].rearrange("p q (r g h) -> p (q r) g h", g=2, h=GH)[:, :, g, :],
                        psG[half, 2:4, :].rearrange("p b (q g h) -> p (b q) g h", g=2, h=GH)[:, :, g, :],
                        sign, None, ALU.mult)
                    if g == 0:
                        link(ins)
                    else:
                        ins.then_inc(bcT_ready, 1)

            def recip(which):
                index, _ = which
                dve.wait_ge(root_done, index + 1)
                V.reciprocal(rb[:], rb[:]).then_inc(rms_ready, 1)
                dve.wait_ge(rms_ready, index + 1)

            def over_rms(src, gr, k0=0):
                V.tensor_tensor(xr[:, k0 + 4 * gr:k0 + 4 * gr + 4, :], src[:, 4 * gr:4 * gr + 4, :],
                                rb[:].unsqueeze(1).to_broadcast([P, 4, T]), ALU.mult
                                ).then_inc(nt_ready, 1)

            def low(group, gr, k0):
                dve.wait_ge(nhi_done, group + 1)
                k = slice(k0 + 4 * gr, k0 + 4 * gr + 4)
                V.tensor_tensor(AA[:, k, T:2 * T], xr[:, k, :],
                                AA[:, k, 0:T].bitcast(F32), ALU.subtract).then_inc(act_ready, 1)

            def lo_unit(g, par, i, u):
                n, s, r, _ = g.place(par, i, u)
                dve.wait_ge(hi_done, n + 1)
                dve.wait_ge(mm_used, n - g.lag + 1)
                V.tensor_tensor(wlo[:, s, :], raw[:, r, :], whi[:, s, :].bitcast(F32), ALU.subtract
                                ).then_inc(lo_done, 1)

            def split(g, par, i, units=None):
                for u in units or range(g.units):
                    lo_unit(g, par, i, u)

            def gemm(g, evacuate, links=0, then=None):
                last = g.pairs // 2 - 1

                def turn(i, units=None):
                    split(g, 1, i, units)
                    evacuate(0, i)
                    split(g, 0, i + 1)
                    evacuate(1, i)

                turn(0, [u for par, u in g.order[g.units:] if par])
                if last > 1:
                    with nc.vector.Fori(1, last) as i:
                        link.loop(i - 1, links)
                        turn(i)
                    link.after(last - 1)
                split(g, 1, last)
                evacuate(0, last)
                if then:
                    split(then, 0, 0, range(3))
                evacuate(1, last)
                if then:
                    split(then, 0, 0, range(3, then.units))

            half_count = [0]

            prepare_b()
            recip(NORM1)
            for gr in range(KD // 4):
                over_rms(hT, gr)

            def window_lo(t):
                dve.wait_ge(hi_done, t + 1)
                wait(dve, mm_used, t - WSPL + 1)
                V.tensor_tensor(wlo[:, t % WSPL, :], raw[:, RAW + 1 - WRAW + t % WRAW, :],
                                whi[:, t % WSPL, :].bitcast(F32), ALU.subtract).then_inc(lo_done, 1)

            two = lambda ap: ap.rearrange("p (a j) -> p a j", a=2)
            for gr in range(BS):
                if gr in (1, 2):
                    take_matrix(2 * gr - 2)
                if gr == 2:
                    window_lo(0)
                    window_lo(1)
                if gr in (1, 2):
                    take_matrix(2 * gr - 1)
                if gr == 3:
                    window_lo(2)
                dve.wait_ge(ada_cols, 2 * gr + 2)
                js = slice(BC * gr, BC * gr + BC)
                link(V.tensor_tensor(two(mod[:, 0:2 * KD])[:, :, js],
                                     two(psX[:, 2, M_AT:M_AT + 2 * KD])[:, :, js],
                                     two(vec[:, V_BADA:V_BADA + 2 * KD])[:, :, js], ALU.add))
                V.scalar_tensor_tensor(gains[:, 0, js], mod[:, KD + BC * gr:KD + BC * gr + BC], 1.0,
                                       vec[:, V_GMIX + BC * gr:V_GMIX + BC * gr + BC], ALU.add, ALU.mult
                                       ).then_inc(mod_ready, 1)
                low(gr, gr, 0)

            def gate_logits():
                dve.wait_ge(f_sum, 1)
                dve.wait_ge(wf_landed, 32)
                link(V.tensor_scalar(fw[:, 0, :], psX[0:NH, 1, 0:T], bf[:, 0:1], None, ALU.add))
                link(V.tensor_scalar(fw[:, 2, :], fw[:, 0, :], -1.0, None, ALU.mult))
                V.tensor_tensor(fw[:, 1, :], fw[:, 0, :], fw[:, 2, :], ALU.max).then_inc(f_abs, 1)
                dve.wait_ge(f_abs, 1)

            def gate_sums():
                link(V.tensor_scalar(fw[:, 2, :], fw[:, 0, :], 0.0, None, ALU.min))
                dve.wait_ge(f_ln, 1)
                link(V.tensor_tensor(fw[:, 2, :], fw[:, 2, :], fw[:, 1, :], ALU.subtract))
                V.tensor_tensor_scan(cum[:], ones[0:NH, :], fw[:, 2, :], 0.0, ALU.mult, ALU.add
                                     ).then_inc(cum_ready, 1)

            link(V.tensor_tensor_scan(mask[:, 0:P], ones[:, 0:P], ident[:], 0.0, ALU.mult, ALU.add))
            link(V.tensor_tensor(mask[:, 0:P], mask[:, 0:P], ident[:], ALU.subtract))
            link(V.tensor_scalar(mask[:, 2 * P:3 * P], mask[:, 0:P], MASKED, None, ALU.mult))
            link(V.memset(mask[:, P:2 * P], 0.0))
            link(V.tensor_copy(mask[:, 0:P], mask[:, 2 * P:3 * P]))

            def maxima(h):
                b = h % 2
                dve.wait_ge(score_done, h + 1)
                wait(dve, probT_done, h - 1)
                V.tensor_tensor(prob[:, b, :], psX[:, score_bank(h), 0:3 * P], mask[:], ALU.add).then_inc(masked, 1)
                dve.wait_ge(masked, h + 1)
                link(V.tensor_reduce(ncol[:, b, 0:1], prob[:, b, 0:P], AX_X, ALU.max))
                link(V.tensor_reduce(ncol[:, b, 1:2], prob[:, b, P:3 * P], AX_X, ALU.max))
                V.tensor_scalar(ncol[:, b, 2:4], ncol[:, b, 0:2], -1.0, None, ALU.mult
                                ).then_inc(max_ready, 1)

            def normalise(h):
                b = h % 2
                dve.wait_ge(exp_done, 2 * h + 2)
                link(V.reciprocal(ncol[:, b, 0:2], ncol[:, b, 4:6]))
                link(V.tensor_scalar(prob[:, b, 0:P], prob[:, b, 0:P], ncol[:, b, 0:1], None, ALU.mult))
                V.tensor_scalar(prob[:, b, P:3 * P], prob[:, b, P:3 * P], ncol[:, b, 1:2], None,
                                ALU.mult).then_inc(prob_ready, 1)

            def attention_dve(h, part):
                if part == 1:
                    maxima(h)
                elif part == 2:
                    normalise(h)

            def ssm_dve(q, piece):
                if q < KS:
                    zre, zim, p0, p1 = (ssm_w[:, (n + 2 * (q % 2)) % 4, :, :] for n in range(4))
                    ct, st = tab[:, q % 2, 0, :, :], tab[:, q % 2, 1, :, :]
                if q < KS and piece in (0, 2):
                    half = piece // 2
                    rs = slice(2 * half, 2 * half + 2)
                    if piece == 0:
                        dve.wait_ge(tab_ready, q + 1)
                        wait(dve, y_part, 2 * q - 1)
                    ere, eim = psG[:, 2:4, 0:T], psG[:, 2:4, T:2 * T]
                    dve.wait_ge(e_done, 2 * q + half + 1)
                    link(V.tensor_tensor(zre[:, rs, :], ct[:, rs, :], ere, ALU.mult))
                    link(V.tensor_tensor(rot_t[:], st[:, rs, :], eim, ALU.mult))
                    link(V.tensor_tensor(zre[:, rs, :], zre[:, rs, :], rot_t[:], ALU.add))
                    link(V.tensor_tensor(zim[:, rs, :], ct[:, rs, :], eim, ALU.mult))
                    V.tensor_tensor(rot_t[:], st[:, rs, :], ere, ALU.mult).then_inc(rotated, 1)
                    dve.wait_ge(rotated, 2 * q + half + 1)
                    link(V.tensor_tensor(zim[:, rs, :], zim[:, rs, :], rot_t[:], ALU.subtract))
                if q < KS and piece in (1, 3):
                    for z in (zre, zim):
                        for r in (piece - 1, piece):
                            j = JQ * q + r
                            ins = V.tensor_tensor_scan(z[:, r, :], d(3)[:, j:j + 1].to_broadcast([P, T]),
                                                       z[:, r, :], 0.0, ALU.mult, ALU.add)
                    ins.then_inc(scanned, 1)
                if q < KS and piece == 4:
                    dve.wait_ge(scanned, 2 * q + 2)
                    wait(dve, y_part, 2 * q)
                    V.scalar_tensor_tensor(p1, st, -1.0, zim, ALU.mult, ALU.mult).then_inc(z_prod, 1)
                if q < KS and piece == 5:
                    dve.wait_ge(z_prod_pool, 2 * q + 1)
                    V.tensor_tensor(zre, st, zre, ALU.mult).then_inc(z_prod, 1)
                if q >= 1 and piece == 1:
                    q1 = q - 1
                    dve.wait_ge(y_part, 2 * q1 + 2)
                    V.scalar_tensor_tensor(uT[:, q1, :], uT[:, q1, :], vec[:, V_D + q1:V_D + q1 + 1],
                                           psX[:, 3, 0:T], ALU.mult, ALU.add).then_inc(y_ready, 1)

            for t in range(STEPS):
                if t % 4 == 3:
                    p = t // 4
                    kind, j = window_pair(p)
                    dst = {"u": uT, "q": qT, "k": kT, "v": vT}[kind]
                    if kind == "v" and j >= 1:
                        dve.wait_ge(vN_done, 2 * j)
                    for m in range(2):
                        dve.wait_ge(tile_half, 2 * p + m + 1)
                        V.scalar_tensor_tensor(dst[:, m if kind == "v" else 2 * j + m, :],
                                               psG[:, m, 0:T], SCALE if kind == "q" else 1.0,
                                               halves[:, 0, m, :], ALU.mult, ALU.add
                                               ).then_inc(tile_out, 1)
                if t + 3 < STEPS:
                    window_lo(t + 3)
                if t == 5:
                    gate_logits()
                if t == 7:
                    gate_sums()
                if ssm_piece(t):
                    ssm_dve(*ssm_piece(t))
                for h, part in attention_step(t):
                    attention_dve(h, part)

            def evacuate_glu(p):
                b = p % 2
                dve.wait_ge(lo_half_out, p + 1)
                V.tensor_tensor(halves[:, b, :, :], psG[:, 2 * b:2 * b + 2, 0:T],
                                halves[:, b, :, :], ALU.add).then_inc(z_ready, 1)
                dve.wait_ge(sig_done, 2 * p + 2)
                y = uT[:, 2 * p:2 * p + 2, :]
                V.tensor_tensor(y, y, halves[:, b, :, :], ALU.mult).then_inc(pair_out, 1)

            def last_heads(part):
                for h in (NH - 2, NH - 1):
                    attention_dve(h, part)

            for gr in range(2):
                dve.wait_ge(glu_hi, gr + 1)
                k = slice(KS + 4 * gr, KS + 4 * gr + 4)
                V.tensor_tensor(AA[:, k, T:2 * T], uT[:, 4 * gr:4 * gr + 4, :],
                                AA[:, k, 0:T].bitcast(F32), ALU.subtract).then_inc(glu_act_ready, 1)
            split(g_glu, 0, 0)
            last_heads(1)
            split(g_glu, 1, 0)
            last_heads(2)
            evacuate_glu(0)
            split(g_glu, 0, 1)
            evacuate_glu(1)
            dve.wait_ge(ada_cols, ADA_BLOCKS)
            dve.wait_ge(o_ready, NH)
            link(V.tensor_tensor(mod[:, 2 * KD:6 * KD], psX[:, 2, M_AT + 2 * KD:M_AT + 6 * KD],
                                 vec[:, V_BADA + 2 * KD:V_BADA + 6 * KD], ALU.add))
            V.scalar_tensor_tensor(gains[:, 1, :], mod[:, 4 * KD:5 * KD], 1.0,
                                   vec[:, V_GFFN:V_GFFN + KD], ALU.add, ALU.mult).then_inc(mod_ready, 1)
            split(g_glu, 1, 1)
            evacuate_glu(2)
            recip(NORMA)
            for gr in range(2):
                over_rms(qT, gr)
            for gr in range(2):
                split(g_out, 0, 0, range(gr, gr + 1))
                low(NORMA[1] + gr, gr, 0)
            split(g_out, 1, 0, range(1))
            evacuate_glu(3)
            split(g_out, 1, 0, range(1, 2))
            recip(NORMS)
            dve.wait_ge(y_gain_done, KS)
            for gr in range(2):
                over_rms(kT, gr, KS)
            for gr in range(2):
                low(NORMS[1] + gr, gr, KS)
                split(g_out, 0, 0, range(2 + gr, 3 + gr))
            half_count[0] += g_glu.pairs

            def add_gated(g, gate_col, into):
                n0 = half_count[0]

                def evacuate(par, i):
                    dve.wait_ge(lo_half_out, n0 + 4 * i + 2 * par + 2)
                    for m in range(2):
                        link(V.scalar_tensor_tensor(
                            halves[:, par, m, :], psG[:, 2 * par + m, 0:T],
                            mod[:, bass.ds(gate_col + 4 * i + 2 * par + m, 1)], halves[:, par, m, :],
                            ALU.mult, ALU.add))
                    h2 = hT[:, bass.ds(4 * i + 2 * par, 2), :]
                    V.tensor_tensor(h2 if into is None else into(par), h2, halves[:, par, :, :], ALU.add
                                    ).then_inc(pair_out, 1)

                half_count[0] += 2 * g.pairs
                return evacuate

            gemm(g_out, add_gated(g_out, 2 * KD, None), 4, g_up)
            recip(NORM2)
            dve.wait_ge(h_gain_done, KD)

            def low2(gr):
                for j in range(4 * gr, 4 * gr + 4):
                    dve.wait_ge(h_hi_done, j + 1)
                    ins = V.scalar_tensor_tensor(AA[:, j, T:2 * T], xr[:, j, :],
                                                 mod[:, 3 * KD + j:3 * KD + j + 1],
                                                 AA[:, j, 0:T].bitcast(F32), ALU.add, ALU.subtract)
                ins.then_inc(act_ready, 1)

            dve.wait_ge(nt_ready, NORM2[1])
            for gr in range(KD // 4):
                over_rms(xr, gr)
                dve.wait_ge(nt_ready, NORM2[1] + gr + 1)
                if gr:
                    low2(gr - 1)
            low2(KD // 4 - 1)

            link(V.memset(conv_in[:, :, 0:2], 0.0))
            n_up = half_count[0]
            half_count[0] += g_up.pairs

            def evacuate_up(par, i):
                dve.wait_ge(lo_half_out, n_up + 2 * i + par + 1)
                hi, lo = psG[:, 2 * par:2 * par + 2, 0:T], halves[:, par, :, :]
                if par == 0:
                    V.tensor_tensor(conv_in[:, :, 2:T + 2], hi, lo, ALU.add).then_inc(pair_out, 1)
                    dve.wait_ge(pair_out, g_up.p0 + 2 * i + 1)

                    def col(at, m):
                        return vec[:, bass.ds(at + 2 * i + m, 1)]

                    for m in range(2):
                        link(V.tensor_scalar(gate[:, m, :], conv_in[:, m, 2:T + 2], col(V_CONV2, m),
                                             col(V_CONVB, m), ALU.mult, ALU.add))
                    for m in range(2):
                        link(V.scalar_tensor_tensor(gate[:, m, :], conv_in[:, m, 1:T + 1],
                                                    col(V_CONV1, m), gate[:, m, :], ALU.mult, ALU.add))
                    link(V.scalar_tensor_tensor(gate[:, 0, :], conv_in[:, 0, 0:T], col(V_CONV0, 0),
                                                gate[:, 0, :], ALU.mult, ALU.add))
                    V.scalar_tensor_tensor(gate[:, 1, :], conv_in[:, 1, 0:T], col(V_CONV0, 1),
                                           gate[:, 1, :], ALU.mult, ALU.add).then_inc(conv_done, 1)
                    dve.wait_ge(conv_done, i + 1)
                else:
                    V.tensor_tensor(branch[:], hi, lo, ALU.add).then_inc(pair_out, 1)
                    dve.wait_ge(pair_out, g_up.p0 + 2 * i + 2)
                    dve.wait_ge(silu_done, i + 1)
                    V.tensor_tensor(gated[:], gate[:], branch[:], ALU.mult).then_inc(gated_ready, 1)
                    dve.wait_ge(ghi_done, i + 1)
                    V.tensor_tensor(GG[:, bass.ds(2 * i, 2), T:2 * T], gated[:],
                                    GG[:, bass.ds(2 * i, 2), 0:T].bitcast(F32), ALU.subtract
                                    ).then_inc(g_ready, 1)

            gemm(g_up, evacuate_up, 5, g_down)

            add_down = add_gated(g_down, 5 * KD, lambda par: halves[:, par, :, :])

            def tail_gains(pair, par):
                dve.wait_ge(tail_sq, 2 * (pair + 1))
                cols = bass.ds(pair * UN, UN)
                V.tensor_tensor(out_n[:, :, cols],
                                psX[:, par, :].rearrange("p (t n) -> p t n", t=TT),
                                g_rows[:, cols].unsqueeze(1).to_broadcast([P, TT, UN]), ALU.mult
                                ).then_inc(tail_out, 1)

            def evacuate_down(par, i):
                add_down(par, i)
                if par:
                    if isinstance(i, int) and i == 0:
                        dve.wait_ge(g_rows_landed, 16)
                    tail_gains(2 * i, 0)
                elif not (isinstance(i, int) and i == 0):
                    tail_gains(2 * i - 1, 1)

            gemm(g_down, evacuate_down, 4)

            dve.wait_ge(tail_sq, 2 * g_down.pairs)
            V.tensor_reduce(tiny[:, 16:18], tiny[:, 0:2 * g_down.pairs].rearrange("p (t n) -> p t n", t=TT),
                            AX_X, ALU.add).then_inc(sumsq_done, 1)
            tail_gains(g_down.pairs - 1, 1)
            dve.wait_ge(root2_done, 1)
            V.reciprocal(tiny[:, 18:20], tiny[:, 18:20]).then_inc(inv_done, 1)
            dve.wait_ge(inv_done, 1)
            dve.wait_ge(tail_out, g_down.pairs)
            for half in range(2):
                cols = slice(half * D // 2, (half + 1) * D // 2)
                V.tensor_scalar(out_n[:, 1, cols], out_n[:, 1, cols], tiny[:, 19:20], None, ALU.mult
                                ).then_inc(final_dve, 1)

        @block.tensor
        def _(pe):
            M = nc.tensor.matmul
            def ada_unit(n, bank):
                s = n % ARING
                pe.wait_ge(ada_landed[s], 16 * (n // ARING) + 16)
                for f in range(AK):
                    k = AK * (n % AU) + f
                    g = k % 4
                    last = M(psX[32 * g:32 * g + 32, bank, :], cond[:, k, :],
                             ada_raw[:, s, f * AN:(f + 1) * AN], start=(k < 4), stop=(k >= KD - 4),
                             tile_position=(0, 32 * g))
                last.then_inc(ada_used, 1)

            pe.wait_ge(pool_chain, 2)
            pe.wait_ge(stage_ready, 3)
            for s in range(4):
                last = nc.tensor.transpose(psX[:, 0, P * s:P * s + P], stage[:, s, :], ident[:])
            last.then_inc(vecT_done, 1)
            pe.wait_ge(cond_ready, 4)
            pe.wait_ge(consts_ready, 1)
            for n in range(ARING):
                ada_unit(n, 0)
            pe.wait_ge(x_landed, 16 * TT)
            for r in range(4):
                wait(pe, hT_ready, r - 1)
                if r == 2:
                    pe.wait_ge(hT_ready, 2)
                if r == 3:
                    pe.wait_ge(hT_ready, 2)
                for j in range(4):
                    for tt in range(TT):
                        last = nc.tensor.transpose(
                            psG[:, 2 * (r % 2) + j // 2, (j % 2) * T + tt * P:(j % 2) * T + tt * P + P],
                            xn[:, tt, (4 * r + j) * P:(4 * r + j + 1) * P], ident[:])
                last.then_inc(xT_done, 1)

            heads_out = [0]

            def ada_columns(b, column, row):
                pe.wait_ge(ada_out, b + 1)
                wait(pe, mod_ready, min(b // 2, BS))
                wait(pe, o_ready, heads_out[0])
                for m in range(BC):
                    last = M(psX[:, 2, M_AT + column + m:M_AT + column + m + 1],
                             ada_rows[:, row, m * P:m * P + P], ones[:, 0:1], start=True, stop=True)
                last.then_inc(ada_cols, 1)

            def sums(tiles, first, last):
                n = len(tiles)
                for j, tile in enumerate(tiles):
                    ins = M(psX[:, 3, 0:T], ones[:, 0:P], tile, start=(first and j == 0),
                            stop=(last and j == n - 1))
                ins.then_inc(ss_used, 1)

            def norm_group(which, gr, groups):
                index, g0 = which
                if gr == 0:
                    wait(pe, root_done, index)
                pe.wait_ge(sq_done, g0 + gr + 1)
                sums([xr[:, j, :] for j in range(4 * gr, 4 * gr + 4)], gr == 0, gr == groups - 1)

            def norm(which, groups):
                for gr in range(groups):
                    norm_group(which, gr, groups)

            def pair(g, par, i, operand, ready, units=None):
                p = g.p0 + 2 * i + par
                for u in units or range(g.units):
                    if u == 0:
                        wait(pe, pair_out, p - 1)
                    n, s, _, _ = g.place(par, i, u)
                    pe.wait_ge(lo_done, n + 1)
                    ready(UK * u + UK - 1)
                    for m in range(2):
                        for f in range(UK):
                            k = UK * u + f
                            at = f * UN + m * P
                            bank = 2 * par + m
                            M(psG[:, bank, :], whi[:, s, at:at + P], operand(k), start=(k == 0),
                              stop=False)
                            last = M(psG[:, bank, 0:T], wlo[:, s, at:at + P], operand(k)[:, 0:T],
                                     start=False, stop=(k == g.units * UK - 1))
                    last.then_inc(mm_used, 1)

            from_aa = lambda k: AA[:, k, :]

            def window_unit(t):
                p, u, s = t // 4, t % 4, t % WSPL
                pe.wait_ge(lo_done, t + 1)
                if p == 0:
                    pe.wait_ge(act_ready, u + 1)
                for m in range(2):
                    if u == 0:
                        wait(pe, tile_out, 2 * (p - 1) + m + 1)
                    for f in range(UK):
                        k, at = UK * u + f, f * UN + m * P
                        M(psG[:, m, :], whi[:, s, at:at + P], AA[:, k, :], start=(k == 0), stop=False)
                        last = M(psG[:, m, 0:T], wlo[:, s, at:at + P], AA[:, k, 0:T], start=False,
                                 stop=(k == KD - 1))
                    if u == 3 and m == 0:
                        last.then_inc(tile_done, 1)
                last.then_inc(mm_used, 1)

            def matrices(r):
                if r == 0:
                    pe.wait_ge(bc_ready, 5)
                wait(pe, bcT_ready, r)
                for q in range(KS):
                    src = (b_wide[:, r, JQ * q:JQ * q + JQ, :, :].rearrange("p j g h -> p (j g h)")
                           if r < 2 else c_twice[:, r - 2, q, :, :].rearrange("p g n -> p (g n)"))
                    last = nc.tensor.transpose(psG[:, 2 + q // 4, (q % 4) * P:(q % 4) * P + P], src,
                                               ident[:])
                last.then_inc(bcT_done, 1)

            for b in range(SHIFT_SCALE1):
                wait(pe, ada_out, b - 1)
                for u in range(AU):
                    if b * AU + u >= ARING:
                        ada_unit(b * AU + u, b % 2)
                    if b == 2 and u % 2:
                        norm_group(NORM1, u // 2, KD // 4)
                if 3 <= b < 7:
                    matrices(b - 3)
                if b:
                    ada_columns(b - 1, (b - 1) % 2 * KD + (b - 1) // 2 * BC, (b - 1) % 2)
            window_unit(0)
            b = SHIFT_SCALE1 - 1
            ada_columns(b, b % 2 * KD + b // 2 * BC, b % 2)
            for t in range(1, EARLY):
                window_unit(t)

            def forget_gates():
                pe.wait_ge(wf_landed, 32)
                for k in range(KD):
                    g = k % 4
                    for a in range(2):
                        last = M(psX[32 * g:32 * g + 32, 1, 0:T], wf[:, k, :],
                                 AA[:, k, a * T:a * T + T].bitcast(F32), start=(k < 4 and a == 0),
                                 stop=(k >= KD - 4 and a == 1), tile_position=(0, 32 * g))
                last.then_inc(f_done, 1)

            def attention_pe(h, part):
                b, scores, output = h % 2, score_bank(h), out_bank(h)
                if part == 0:
                    pe.wait_ge(tile_out, 2 * (3 * (h // 2) + 7))
                    wait(pe, probT_ready, min(h, NH - 2))
                    for tt in range(TT):
                        last = nc.tensor.transpose(psX[:, scores, tt * P:tt * P + P],
                                                   vT[:, h % 2, tt * P:tt * P + P], ident[:])
                    last.then_inc(vN_done, 1)
                elif part == 1:
                    pe.wait_ge(csel_ready, h + 1)
                    pe.wait_ge(vN_ready, h + 1)
                    for tt, at, n in ((0, 0, P), (1, P, 2 * P)):
                        dst = psX[:, scores, at:at + n]
                        t = slice(tt * P, tt * P + P)
                        M(dst, qT[:, h, t], kT[:, h, 0:n], start=True, stop=False)
                        M(dst, csel[:, b, t], ones[0:NH, 0:n], start=False, stop=False)
                        last = M(dst, minus[:], csel[:, b, 0:n], start=False, stop=True)
                    last.then_inc(score_done, 1)
                elif part == 3:
                    pe.wait_ge(prob_ready, h + 1)
                    for n in range(3):
                        last = nc.tensor.transpose(psX[:, scores, n * P:n * P + P],
                                                   prob[:, b, n * P:n * P + P], ident[:])
                    last.then_inc(probT_done, 1)
                elif part == 4:
                    pe.wait_ge(probT_ready, h + 1)
                    if h == NH - 1:
                        pe.wait_ge(y_ready, KS)
                    else:
                        wait(pe, o_ready, h)
                    v = lambda st: vN[:, st, h * HD:h * HD + HD]
                    M(psX[:, output, 0:T], v(0), probT[:, b, 0:T], start=True, stop=False)
                    M(psX[:, output, P:T], v(1), probT[:, b, T:T + P], start=False, stop=True
                      ).then_inc(pv_done, 1)
                    heads_out[0] = h + 1

            def inputs(q, half):
                if q == 0 and half == 0:
                    pe.wait_ge(bcT_ready, 4)
                    pe.wait_ge(tile_out, 2)
                if half == 0:
                    pe.wait_ge(tile_out, q + 1)
                wait(pe, rotated, 2 * q + half)
                for a, mat in enumerate((btr, bti)):
                    for r in (2 * half, 2 * half + 1):
                        rows = slice(32 * r, 32 * r + 32)
                        last = M(psG[:, 2 + r % 2, a * T:a * T + T], mat[rows, q, :], uT[rows, q, :],
                                 start=True, stop=True, tile_position=(32 * r, 0))
                last.then_inc(e_done, 1)

            def outputs(q, part):
                if part == 0:
                    wait(pe, y_ready, q)
                pe.wait_ge(z_prod, 2 * q + part + 1)
                pe.wait_ge(z_prod_pool, 2 * q + part + 1)
                for a, (n, mat) in enumerate((((2, ctr), (3, ctr)), ((0, cti), (1, cti)))[part]):
                    for r in range(JQ):
                        cols = slice(32 * r, 32 * r + 32)
                        last = M(psX[cols, 3, 0:T], mat[:, q, cols],
                                 ssm_w[:, (n + 2 * (q % 2)) % 4, r, :],
                                 start=(part == 0 and a == 0), stop=(part == 1 and a == 1),
                                 tile_position=(0, 32 * r))
                last.then_inc(y_part, 1)

            for t in range(STEPS):
                if t >= EARLY:
                    window_unit(t)
                for n in range(2):
                    a = 2 * t + n
                    b = SHIFT_SCALE1 + a // AU
                    if a % AU == 0:
                        pe.wait_ge(ada_out, b)
                    ada_unit(WINDOW_ADA + a, 0)
                if t % 4 == 1 and t > 4:
                    b = SHIFT_SCALE1 + t // 4 - 1
                    ada_columns(b, b * BC, (t // 4 - 1) % 2)
                if t == 4:
                    forget_gates()
                if t == 5:
                    pe.wait_ge(f_rows, 1)
                    M(psX[0:NH, 1, 0:T], sel[:], rb[:], start=True, stop=True).then_inc(f_sum, 1)
                qn = ssm_piece(t + 2)
                if qn and qn[0] < KS and qn[1] == 0:
                    inputs(qn[0], 0)
                qn = ssm_piece(t)
                if qn and qn[0] < KS and qn[1] == 1:
                    inputs(qn[0], 1)
                if qn and qn[0] < KS and qn[1] == 5:
                    outputs(qn[0], 0)
                if qn and qn[0] >= 1 and qn[1] == 0:
                    outputs(qn[0] - 1, 1)
                for h, part in attention_step(t):
                    attention_pe(h, part)
            b = ADA_BLOCKS - 1
            ada_columns(b, b * BC, (STEPS // 4 - 1) % 2)

            def last_heads(part):
                for h in (NH - 2, NH - 1):
                    attention_pe(h, part)

            def glu_pair(p):
                pair(g_glu, p % 2, p // 2, lambda k: AA[:, KS + k, :],
                     lambda k: pe.wait_ge(glu_act_ready, k // 4 + 1))

            def sums_y(p):
                pe.wait_ge(y_sq_done, p + 1)
                for n in range(2):
                    last = M(psX[:, 0, 0:T], ones[:, 0:P], xr[:, KS + 2 * p + n, :],
                             start=(p == 0 and n == 0), stop=(p == 3 and n == 1))
                last.then_inc(y_ss_used, 1)

            last_heads(0)
            last_heads(1)
            glu_pair(0)
            last_heads(3)
            glu_pair(1)
            last_heads(4)
            sums_y(0)
            glu_pair(2)
            norm(NORMA, 2)
            sums_y(1)
            glu_pair(3)
            sums_y(2)

            ready_out = lambda k: pe.wait_ge(act_ready, NORMA[1] + k // 4 + 1)

            def sums_pair(p, first=False, last=False):
                pe.wait_ge(sq_done, SUMS2 + p + 1)
                if first:
                    pe.wait_ge(root_done, NORM2[0])
                sums([sq[:, 0, :], sq[:, 1, :]], first, last)

            pair(g_out, 0, 0, from_aa, ready_out, range(2))
            sums_y(3)
            for units in (range(2), range(2, 4)):
                if units[0]:
                    pair(g_out, 0, 0, from_aa, ready_out, units)
                pair(g_out, 1, 0, from_aa, ready_out, units)
            sums_pair(0, first=True)
            with nc.tensor.Fori(1, g_out.pairs // 2) as i:
                pair(g_out, 0, i, from_aa, ready_out)
                sums_pair(2 * i - 1)
                pair(g_out, 1, i, from_aa, ready_out)
                sums_pair(2 * i)
            sums_pair(g_out.pairs - 1, last=True)

            ready_up = lambda k: pe.wait_ge(act_ready, NORM2[1] + k // 4 + 1)
            with nc.tensor.Fori(0, g_up.pairs // 2) as i:
                for par in range(2):
                    pair(g_up, par, i, from_aa, ready_up)

            def down_pair(par, i):
                pair(g_down, par, i, lambda k: GG[:, k, :],
                     lambda k: pe.wait_ge(g_ready, (k + 1) // 2))

            def tail(p, par):
                pe.wait_ge(pair_out, g_down.p0 + p + 1)
                wait(pe, tail_out, p - 1)
                for tt in range(TT):
                    for m in range(2):
                        last = nc.tensor.transpose(psX[:, par, tt * T + m * P:tt * T + m * P + P],
                                                   halves[:, par, m, tt * P:tt * P + P], ident[:])
                last.then_inc(tail_T, 1)

            down_pair(0, 0)

            def down_round(i):
                down_pair(1, i)
                tail(2 * i, 0)
                down_pair(0, i + 1)
                tail(2 * i + 1, 1)

            down_round(0)
            with nc.tensor.Fori(1, g_down.pairs // 2 - 1) as i:
                down_round(i)
            down_pair(1, g_down.pairs // 2 - 1)
            tail(g_down.pairs - 2, 0)
            tail(g_down.pairs - 1, 1)


_INS = ["x", "c", "w_ada", "b_ada", "g_mix", "w_in", "b_f", "a_re", "a_im", "log_dt", "ssm_b_re",
        "ssm_b_im", "ssm_c_re", "ssm_c_im", "ssm_d", "w_glu", "b_glu", "g_attn_out", "g_ssm_out",
        "w_out", "g_ffn", "w_up", "conv_w", "conv_b", "w_down", "g_final"]
_MATRICES = ("w_ada", "w_in", "w_glu", "w_out", "w_up", "w_down")


def kernel(**inputs):
    import concourse.bacc as _bacc
    from concourse.bass_utils import run_bass_kernel_spmd as _run

    nc = _bacc.Bacc("TRN2", target_bir_lowering=False, num_devices=1, dynamic_dma_scratch_size=64)
    arrays, args = {}, []
    for name in _INS:
        a = np.ascontiguousarray(inputs[name])
        if name in _MATRICES:
            a = a.reshape(a.shape[1:])
        arrays[f"in_{name}"] = a
        args.append(nc.dram_tensor(f"in_{name}", a.shape, mybir.dt.from_np(a.dtype),
                                   kind="ExternalInput").ap())
    args.append(nc.dram_tensor("out_0", (1, T, D), F32, kind="ExternalOutput").ap())
    build(nc, *args)
    r = _run(nc, [arrays], core_ids=[0])
    return r.results[0]["out_0"]
```
